# Optimizing a Trainium2 kernel written in Bass

```python
import jax, jax.numpy as jnp
from jax import lax
import numpy as np

D_MODEL = 1024
BATCH = 1
SEQ = 512
DEPTH = 1

N_META = 16
ATT_HEADS = 8
ATT_KV_HEADS = 2
ATT_HEAD_DIM = 64
ATT_REP = ATT_HEADS // ATT_KV_HEADS
WINDOW = 128
BLOCK = 128
GLA_HEADS = 4
GLA_DK = 64
GLA_DV = 128
GLA_RANK = 16
GLA_TAU = 16.0
GLA_CHUNK = 64
N_DIR = 2
ATT_WIDTH = ATT_HEADS * ATT_HEAD_DIM
ATT_KV_WIDTH = ATT_KV_HEADS * ATT_HEAD_DIM
GLA_QK_WIDTH = GLA_HEADS * GLA_DK
GLA_WIDTH = GLA_HEADS * GLA_DV
MIX_WIDTH = ATT_WIDTH + GLA_WIDTH
PROJ_WIDTHS = (ATT_WIDTH, ATT_KV_WIDTH, ATT_KV_WIDTH, GLA_QK_WIDTH, GLA_QK_WIDTH, GLA_WIDTH, GLA_WIDTH, N_DIR * GLA_RANK)
IN_WIDTH = sum(PROJ_WIDTHS)
SPLIT_POINTS = tuple(int(v) for v in np.cumsum(PROJ_WIDTHS)[:-1])
D_FF = 2816
LN_EPS = 1e-5
DN_ALPHA = (2.0 * DEPTH) ** 0.25
DN_BETA = (8.0 * DEPTH) ** -0.25

kernel_name = "hymba_swa_gla_macaron_deepnorm_encoder"

def layer_norm(x, g, b):
    xf = x.astype(jnp.float32)
    mu = jnp.mean(xf, axis=-1, keepdims=True)
    xc = xf - mu
    var = jnp.mean(xc * xc, axis=-1, keepdims=True)
    return (xc * lax.rsqrt(var + LN_EPS) * g + b).astype(x.dtype)

def swiglu(h, w_gate, w_up, w_down):
    return (jax.nn.silu(h @ w_gate) * (h @ w_up)) @ w_down

def alibi_slopes():
    return np.array([2.0 ** (-8.0 * (i + 1) / ATT_HEADS) for i in range(ATT_HEADS)], np.float32)

def window_attention(q, k, v, sink):
    b, t = q.shape[:2]
    s = t - N_META
    nb = s // BLOCK
    G, R, Dh = ATT_KV_HEADS, ATT_REP, ATT_HEAD_DIM
    slopes = jnp.asarray(alibi_slopes()).reshape(G, R)
    sink = sink.reshape(G, R).astype(jnp.float32)
    q = q.reshape(b, t, G, R, Dh) * (Dh ** -0.5)
    qm, qr = q[:, :N_META], q[:, N_META:]
    km, kr = k[:, :N_META], k[:, N_META:]
    vm, vr = v[:, :N_META], v[:, N_META:]

    def band(z):
        zp = jnp.pad(z, ((0, 0), (BLOCK, BLOCK), (0, 0), (0, 0))).reshape(b, nb + 2, BLOCK, G, Dh)
        zb = jnp.concatenate([zp[:, :-2], zp[:, 1:-1], zp[:, 2:]], axis=2)
        return jnp.moveaxis(zb, 1, 0)

    qb = jnp.moveaxis(qr.reshape(b, nb, BLOCK, G, R, Dh), 1, 0)
    kb, vb = band(kr), band(vr)
    rel = jnp.arange(3 * BLOCK)[None, :] - BLOCK - jnp.arange(BLOCK)[:, None]
    in_win = jnp.abs(rel) <= WINDOW
    band_bias = -slopes[:, :, None, None] * jnp.abs(rel).astype(jnp.float32)
    key_idx = (jnp.arange(nb)[:, None] - 1) * BLOCK + jnp.arange(3 * BLOCK)[None, :]
    key_ok = (key_idx >= 0) & (key_idx < s)

    def block_fn(args):
        qn, kn, vn, okn = args
        s_band = jnp.einsum('bqgrd,bkgd->bgrqk', qn, kn) + band_bias
        s_band = jnp.where(in_win & okn[None, :], s_band, -jnp.inf)
        s_meta = jnp.einsum('bqgrd,bmgd->bgrqm', qn, km)
        s_sink = jnp.broadcast_to(sink[None, :, :, None, None], s_band.shape[:-1] + (1,))
        p = jax.nn.softmax(jnp.concatenate([s_band, s_meta, s_sink], axis=-1), axis=-1)
        return (jnp.einsum('bgrqk,bkgd->bqgrd', p[..., :3 * BLOCK], vn)
                + jnp.einsum('bgrqm,bmgd->bqgrd', p[..., 3 * BLOCK:3 * BLOCK + N_META], vm))

    o_real = lax.map(block_fn, (qb, kb, vb, key_ok))
    o_real = jnp.moveaxis(o_real, 0, 1).reshape(b, s, ATT_WIDTH)

    k_mq = jnp.concatenate([km, kr[:, :BLOCK]], axis=1)
    v_mq = jnp.concatenate([vm, vr[:, :BLOCK]], axis=1)
    qpos = jnp.arange(N_META)
    kpos = jnp.arange(N_META + BLOCK)
    rel_m = kpos[None, :] - qpos[:, None]
    is_meta_key = (kpos < N_META)[None, :]
    ok_m = is_meta_key | (jnp.abs(rel_m) <= WINDOW)
    bias_m = jnp.where(is_meta_key, 0.0, -slopes[:, :, None, None] * jnp.abs(rel_m).astype(jnp.float32))
    s_m = jnp.where(ok_m, jnp.einsum('bqgrd,bkgd->bgrqk', qm, k_mq) + bias_m, -jnp.inf)
    s_m_sink = jnp.broadcast_to(sink[None, :, :, None, None], s_m.shape[:-1] + (1,))
    p_m = jax.nn.softmax(jnp.concatenate([s_m, s_m_sink], axis=-1), axis=-1)
    o_meta = jnp.einsum('bgrqk,bkgd->bqgrd', p_m[..., :-1], v_mq).reshape(b, N_META, ATT_WIDTH)
    return jnp.concatenate([o_meta, o_real], axis=1)

def gla_direction(q, k, v, lg, inclusive):
    b, l = q.shape[:2]
    nc = l // GLA_CHUNK

    def chunks(z):
        return z.reshape(b, nc, GLA_CHUNK, GLA_HEADS, z.shape[-1]).transpose(1, 0, 3, 2, 4)

    qc, kc, vc, gc = chunks(q), chunks(k), chunks(v), chunks(lg)
    bc = jnp.cumsum(gc, axis=-2)
    ti = jnp.arange(GLA_CHUNK)
    mask = (ti[:, None] >= ti[None, :]) if inclusive else (ti[:, None] > ti[None, :])

    def step(state, xs):
        qn, kn, vn, bn = xs
        o_inter = jnp.einsum('bhtd,bhde->bhte', qn * jnp.exp(bn), state)
        decay = jnp.exp(jnp.where(mask[:, :, None], bn[:, :, :, None, :] - bn[:, :, None, :, :], -jnp.inf))
        a = jnp.einsum('bhtd,bhsd,bhtsd->bhts', qn, kn, decay)
        o = o_inter + jnp.einsum('bhts,bhse->bhte', a, vn)
        b_last = bn[:, :, -1:, :]
        state = (state * jnp.exp(b_last[:, :, 0, :])[..., None]
                 + jnp.einsum('bhsd,bhse->bhde', kn * jnp.exp(b_last - bn), vn))
        return state, o

    state0 = jnp.zeros((b, GLA_HEADS, GLA_DK, GLA_DV), jnp.float32)
    _, o = lax.scan(step, state0, (qc, kc, vc, bc))
    return o.transpose(1, 0, 3, 2, 4).reshape(b, l, GLA_HEADS, GLA_DV)

def gla_mixer(q, k, v, g, z, w2, bias, norm_g):
    b, t = q.shape[:2]
    z = z.reshape(b, t, N_DIR, GLA_RANK)
    lg = jax.nn.log_sigmoid(jnp.einsum('btnr,nrk->btnk', z, w2) + bias) / GLA_TAU
    lead = GLA_CHUNK - N_META
    pad = ((0, 0), (lead, 0), (0, 0), (0, 0))

    def prep(a, d):
        return jnp.pad(a.reshape(b, t, GLA_HEADS, d), pad)

    qh = prep(q * (GLA_DK ** -0.5), GLA_DK)
    kh = prep(k, GLA_DK)
    vh = prep(v, GLA_DV)
    lf = prep(lg[:, :, 0], GLA_DK)
    lb = prep(lg[:, :, 1], GLA_DK)
    o_f = gla_direction(qh, kh, vh, lf, True)
    o_b = jnp.flip(gla_direction(jnp.flip(qh, 1), jnp.flip(kh, 1), jnp.flip(vh, 1), jnp.flip(lb, 1), False), 1)
    o = (o_f + o_b)[:, lead:]
    o = o * lax.rsqrt(jnp.mean(o * o, axis=-1, keepdims=True) + LN_EPS) * norm_g
    return o.reshape(b, t, GLA_WIDTH) * jax.nn.silu(g)

def token_mixer(h, w_in, attn_sink, gla_w2, gla_b, gla_norm_g, w_out):
    b, t = h.shape[:2]
    proj = (h @ w_in).astype(jnp.float32)
    aq, ak, av, gq, gk, gv, gg, gz = jnp.split(proj, SPLIT_POINTS, axis=-1)
    o_att = window_attention(aq.reshape(b, t, ATT_HEADS, ATT_HEAD_DIM),
                             ak.reshape(b, t, ATT_KV_HEADS, ATT_HEAD_DIM),
                             av.reshape(b, t, ATT_KV_HEADS, ATT_HEAD_DIM), attn_sink)
    o_gla = gla_mixer(gq, gk, gv, gg, gz, gla_w2, gla_b, gla_norm_g)
    return jnp.concatenate([o_att, o_gla], axis=-1).astype(h.dtype) @ w_out

def setup_inputs(seed: int = 0) -> dict:
    key = jax.random.key(seed)
    ks = jax.random.split(key, 24)
    nrm = jax.random.normal
    f32 = jnp.float32

    def gain(k, shape):
        return 1.0 + 0.02 * nrm(k, shape, f32)

    def small(k, shape, s=0.02):
        return s * nrm(k, shape, f32)

    return {
        'x': nrm(ks[0], (BATCH, SEQ, D_MODEL), f32),
        'meta_tokens': nrm(ks[1], (N_META, D_MODEL), f32),
        'ln_in_g': gain(ks[2], (D_MODEL,)),
        'ln_in_b': small(ks[3], (D_MODEL,)),
        'ffn1_ln_g': gain(ks[4], (DEPTH, D_MODEL)),
        'ffn1_ln_b': small(ks[5], (DEPTH, D_MODEL)),
        'ffn1_w_gate': nrm(ks[6], (DEPTH, D_MODEL, D_FF), f32) * D_MODEL ** -0.5,
        'ffn1_w_up': nrm(ks[7], (DEPTH, D_MODEL, D_FF), f32) * D_MODEL ** -0.5,
        'ffn1_w_down': nrm(ks[8], (DEPTH, D_FF, D_MODEL), f32) * (D_FF ** -0.5 * DN_BETA),
        'w_in': nrm(ks[9], (DEPTH, D_MODEL, IN_WIDTH), f32) * D_MODEL ** -0.5,
        'attn_sink': small(ks[10], (DEPTH, ATT_HEADS), 0.5),
        'gla_gate_w2': nrm(ks[11], (DEPTH, N_DIR, GLA_RANK, GLA_QK_WIDTH), f32) * GLA_RANK ** -0.5,
        'gla_gate_b': small(ks[12], (DEPTH, N_DIR, GLA_QK_WIDTH), 0.1),
        'gla_norm_g': gain(ks[13], (DEPTH, GLA_DV)),
        'w_out': nrm(ks[14], (DEPTH, MIX_WIDTH, D_MODEL), f32) * (MIX_WIDTH ** -0.5 * DN_BETA),
        'mix_ln_g': gain(ks[15], (DEPTH, D_MODEL)),
        'mix_ln_b': small(ks[16], (DEPTH, D_MODEL)),
        'ffn2_w_gate': nrm(ks[17], (DEPTH, D_MODEL, D_FF), f32) * D_MODEL ** -0.5,
        'ffn2_w_up': nrm(ks[18], (DEPTH, D_MODEL, D_FF), f32) * D_MODEL ** -0.5,
        'ffn2_w_down': nrm(ks[19], (DEPTH, D_FF, D_MODEL), f32) * (D_FF ** -0.5 * DN_BETA),
        'ffn2_ln_g': gain(ks[20], (DEPTH, D_MODEL)),
        'ffn2_ln_b': small(ks[21], (DEPTH, D_MODEL)),
    }

def reference(x, meta_tokens, ln_in_g, ln_in_b, ffn1_ln_g, ffn1_ln_b, ffn1_w_gate, ffn1_w_up, ffn1_w_down,
              w_in, attn_sink, gla_gate_w2, gla_gate_b, gla_norm_g, w_out, mix_ln_g, mix_ln_b,
              ffn2_w_gate, ffn2_w_up, ffn2_w_down, ffn2_ln_g, ffn2_ln_b):
    b = x.shape[0]
    meta = jnp.broadcast_to(meta_tokens[None].astype(x.dtype), (b, N_META, D_MODEL))
    h = layer_norm(jnp.concatenate([meta, x], axis=1), ln_in_g, ln_in_b)
    for i in range(DEPTH):
        h = layer_norm(DN_ALPHA * h + 0.5 * swiglu(h, ffn1_w_gate[i], ffn1_w_up[i], ffn1_w_down[i]),
                       ffn1_ln_g[i], ffn1_ln_b[i])
        h = layer_norm(DN_ALPHA * h + token_mixer(h, w_in[i], attn_sink[i], gla_gate_w2[i], gla_gate_b[i],
                                                  gla_norm_g[i], w_out[i]),
                       mix_ln_g[i], mix_ln_b[i])
        h = layer_norm(DN_ALPHA * h + 0.5 * swiglu(h, ffn2_w_gate[i], ffn2_w_up[i], ffn2_w_down[i]),
                       ffn2_ln_g[i], ffn2_ln_b[i])
    return h[:, N_META:]


_drawn_inputs = setup_inputs


def setup_inputs(seed=0):
    import zlib

    import numpy as np

    out = dict(_drawn_inputs(seed))
    spreads = {}
    factors = {'attn_sink': 25.626,
     'gla_gate_b': 6.229,
     'gla_norm_g': 23.912,
     'mix_ln_g': 2.828,
     'mix_ln_b': 2.817,
     'ffn2_ln_g': 8.71,
     'ffn2_ln_b': 8.111}
    for name, (base, spread) in spreads.items():
        noise = np.random.default_rng([zlib.crc32(name.encode()), seed]).standard_normal(out[name].shape)
        drawn = base * np.exp(spread * noise) if base else spread * noise
        out[name] = __import__('jax').numpy.asarray(drawn.astype(out[name].dtype))
    for name, factor in factors.items():
        out[name] = (out[name] * factor).astype(out[name].dtype)
    return out
```

```python
from contextlib import ExitStack

import numpy as np

import concourse.bass as bass
from concourse import mybir

F32 = mybir.dt.float32
ALU = mybir.AluOpType
ACT = mybir.ActivationFunctionType

P = 128
D_MODEL, SEQ, N_META = 1024, 512, 16
T = SEQ + N_META
HALF = T // 2
KD = D_MODEL // P
D_FF = 2816
KF = D_FF // P
HEADS, GROUPS, DH = 8, 2, 64
REP = HEADS // GROUPS
WINDOW = BLOCK = 128
NB = SEQ // BLOCK
G_HEADS, DK, DV, RANK, TAU = 4, 64, 128, 16, 16.0
N_DIR = 2
PAIRS = G_HEADS * DK // P
CH = 88
NCH = T // CH
MID = CH // 2
EPS = 1e-5
ALPHA = 2.0 ** 0.25
NEG = -1e30
EXP_LIMIT = 40.0 * TAU

SINK_COL = N_META
KEYS = T + 1
S_MID = N_META + 1 + 3 * BLOCK
S_END = N_META + 1 + 2 * BLOCK
S_META = N_META + 1 + BLOCK
MROW = 32

C_G = [0, 16, 32, 48]
C_B = [8, 24, 40, 56]
C_NORM = 64
C_GATE = 65
C_SINK = 69
C_SINKM = C_SINK + HEADS
N_PAR = C_SINKM + GROUPS

FF_CHUNK = 256
N_GU = D_FF // FF_CHUNK
N_DN = D_MODEL // FF_CHUNK
IN_COLS = [544, 512, 512, 512, 256]
N_IN, N_OUT = len(IN_COLS), 2
GU = [0, N_GU + N_DN + N_IN + N_OUT]
DN = [GU[0] + N_GU, GU[1] + N_GU]
IN0 = DN[0] + N_DN
OUT0 = IN0 + N_IN
SLOT = KF * FF_CHUNK
N_CONST = 7

def slopes():
    return [2.0 ** (-8.0 * (i + 1) / HEADS) for i in range(HEADS)]


def build(nc, xT, params, rel_mid, rel_first, bias_meta, ident_in, masks_in, reset_in, w2_in,
          gate, up, down, w_in, w_out, out):
    with ExitStack() as ctx:
        def sb(name, shape, dt=F32):
            return ctx.enter_context(nc.sbuf_tensor(name, shape, dt))

        def sem(name):
            return ctx.enter_context(nc.semaphore(name))

        PS = ctx.enter_context(nc.psum_tensor("PS", [P, 8, 512], F32))
        H = sb("H", [P, KD, T])
        X = sb("X", [P, KD, T])
        wbuf = sb("wbuf", [P, 2, SLOT])
        big = sb("big", [P, KF * T])
        hid = big[:, :].rearrange("p (m t) -> p m t", m=KF)
        tmp_a = sb("tmp_a", [P, 2, T])
        tmp_b = sb("tmp_b", [P, 2, T])
        std = sb("std", [P, T])
        rstd = sb("rstd", [P, T])
        tmp_g = sb("tmp_g", [P, 2, T])
        ones = sb("ones", [P, P])
        ones_dv = sb("ones_dv", [P, P])
        eps = sb("eps", [P, 2])
        par = sb("par", [P, N_PAR])
        ident = sb("ident", [P, P])
        masks = sb("masks", [CH, N_DIR, CH])
        reset = sb("reset", [P, T])
        w2 = sb("w2", [N_DIR * RANK, N_DIR, PAIRS * P])
        rel = sb("rel", [P, S_MID + S_END])
        bias_m = sb("bias_m", [P, GROUPS, S_META])
        credit = sb("credit", [1, 6])

        arena = sb("arena", [P, 13840])
        pools = {"big": [big, 0, KF * T], "arena": [arena, 0, 13840]}

        def part(pool, shape):
            buf, start, size = pools[pool]
            n = int(np.prod(shape[1:]))
            pools[pool][1] += n
            assert start + n <= size, (pool, start, n, size)
            ap = buf[0:shape[0], start:start + n]
            if len(shape) == 2:
                return ap
            names = "abcd"[:len(shape) - 1]
            return ap.rearrange(f"p ({' '.join(names)}) -> p {' '.join(names)}",
                                **{n: s for n, s in zip(names, shape[1:])})

        mix = part("big", [P, KD, T])
        gv = part("big", [CH, NCH, G_HEADS * DV])
        sg = part("big", [P, G_HEADS, T])
        zT = part("big", [N_DIR * RANK, T])
        kT = sb("kT", [P, KEYS])
        qT = part("arena", [P, REP, T])
        av = part("arena", [P, NB + 1, P])
        mark = pools["arena"][1]
        gqT = part("arena", [P, PAIRS, T])
        gkT = part("arena", [P, PAIRS, T])
        V = part("arena", [P, PAIRS, N_DIR, T])
        B_end = part("arena", [P, PAIRS * N_DIR, NCH])
        E_end = part("arena", [P, PAIRS * N_DIR, NCH])
        q_in = part("arena", [P, N_DIR, T])
        k_in = part("arena", [P, N_DIR, T])
        q_ex = part("arena", [P, N_DIR, T])
        k_ex = part("arena", [P, N_DIR, T])
        kxT = part("big", [CH, NCH, N_DIR * P])
        state = part("arena", [P, N_DIR, NCH, DV])
        a_dir = part("arena", [CH, 2, N_DIR * 2 * CH])
        a_sum = part("arena", [CH, 2, 2 * CH])
        pools["arena"][1] = mark
        bias_mid = part("arena", [P, HEADS, S_MID])
        bias_first = part("arena", [P, HEADS, S_END])
        PT = part("arena", [P, GROUPS, 3, REP * BLOCK])
        PTm = part("arena", [N_META, GROUPS, REP * BLOCK])
        gO = mix[:, REP:KD, :]
        scores = tmp_a[:, :, :].rearrange("p a t -> p (a t)")[:, 0:2 * 402]
        scores2 = tmp_b[:, :, :].rearrange("p a t -> p (a t)")[:, 0:2 * 402]
        N_UNIT = 1 + NB * REP
        smin = sb("smin", [P, 2 * N_UNIT])
        ssum = sb("ssum", [P, 2 * N_UNIT])
        srec = sb("srec", [P, 2 * N_UNIT])

        def score_buf(n):
            return (scores, scores2)[n // 2 % 2].rearrange("p (a t) -> p a t", a=2)[:, n % 2, :]

        x_loaded = sem("x_loaded")
        par_loaded = sem("par_loaded")
        const_loaded = sem("const_loaded")
        w_loaded = [sem(f"w_loaded{i}") for i in range(2)]
        ready0 = sem("ready0")
        mean_ready = sem("mean_ready")
        centred = sem("centred")
        squared = sem("squared")
        sq_summed = sem("sq_summed")
        std_ready = sem("std_ready")
        rstd_ready = sem("rstd_ready")
        normed = sem("normed")
        h_ready = sem("h_ready")
        gu_ready = sem("gu_ready")
        silu_ready = sem("silu_ready")
        hid_done = sem("hid_done")
        res_ready = sem("res_ready")
        res_done = sem("res_done")
        proj_ready = sem("proj_ready")
        proj_done = sem("proj_done")
        gate_ready = sem("gate_ready")
        gate_abs = sem("gate_abs")
        gate_exp = sem("gate_exp")
        gate_ln = sem("gate_ln")
        gate_min = sem("gate_min")
        log_gate = sem("log_gate")
        scanned = sem("scanned")
        ends_done = sem("ends_done")
        decay_done = sem("decay_done")
        end_exp = sem("end_exp")
        rel_a = sem("rel_a")
        clamp_lo = sem("clamp_lo")
        clamped = sem("clamped")
        rel_b = sem("rel_b")
        dec_exp = sem("dec_exp")
        dec_dve = sem("dec_dve")
        dec_pool = sem("dec_pool")
        kx_ready = sem("kx_ready")
        kx_done = sem("kx_done")
        st_ready = sem("st_ready")
        st_done = sem("st_done")
        a_ready = sem("a_ready")
        a_masked = sem("a_masked")
        a_done = sem("a_done")
        o_ready = sem("o_ready")
        o_done = sem("o_done")
        o_sq = sem("o_sq")
        o_ssum = sem("o_ssum")
        o_std = sem("o_std")
        o_rstd = sem("o_rstd")
        o_gated = sem("o_gated")
        o_final = sem("o_final")
        rel_done = sem("rel_done")
        bias_done = sem("bias_done")
        s_ready = sem("s_ready")
        s_max = sem("s_max")
        p_exp = sem("p_exp")
        p_rec = sem("p_rec")
        p_norm = sem("p_norm")
        pt_ready = sem("pt_ready")
        pt_act = sem("pt_act")
        pt_dve = sem("pt_dve")
        ptm_ready = sem("ptm_ready")
        ptm_done = sem("ptm_done")
        att_ready = sem("att_ready")
        att_done = sem("att_done")
        out_done = sem("out_done")

        def halves(ap):
            return ap.rearrange("p (h c) -> p h c", h=2)

        def pair(bank, rows=P):
            return PS[0:rows, bank:bank + 2, 0:HALF]

        def w_view(slot, kt, cols):
            return wbuf[:, slot, 0:kt * cols].rearrange("p (k n) -> p k n", k=kt)

        def gu_view(slot):
            return wbuf[:, slot, 0:2 * KD * FF_CHUNK].rearrange("p (g k n) -> p g k n", g=2, k=KD)

        TILES = ([("z", 0, 0, 0)] + [("g", i, 0, 32 + P * i) for i in range(G_HEADS)]
                 + [("gq", i, 1, P * i) for i in range(PAIRS)] + [("gk", i, 1, 256 + P * i) for i in range(PAIRS)]
                 + [("gv", i, 2, 0) for i in range(NCH)]
                 + [("aq", i, 3, P * i) for i in range(REP)] + [("ak", 0, 4, 0), ("av", 0, 4, P)])
        LAST_OF = [max(n for n, t in enumerate(TILES) if t[2] == c) for c in range(N_IN)]
        GATES = [(j, d) for j in range(PAIRS) for d in range(N_DIR)]
        GATES_AFTER = {TILES.index(("g", 3, 0, 32 + 3 * P)): [0, 1], TILES.index(("gq", 1, 1, P)): [2, 3]}
        UNITS = [(-1, 0)] + [(n, j) for n in range(NB) for j in range(REP)]

        def unit_keys(n):
            blocks = [0] if n < 0 else [b for b in (n - 1, n, n + 1) if 0 <= b < NB]
            lo, hi = SINK_COL + 1 + BLOCK * blocks[0], SINK_COL + 1 + BLOCK * (blocks[-1] + 1)
            runs = [(0, hi)] if blocks[0] == 0 else [(0, SINK_COL + 1), (lo, hi)]
            return runs, blocks

        def chunk(ap, c):
            return ap[..., CH * c:CH * (c + 1)]

        def unit_cols(u):
            return sum(hi - lo for lo, hi in unit_keys(UNITS[u][0])[0])

        def gate_col(q):
            j, d = GATES[q]
            return PAIRS * d + j

        def normalise(pool, u):
            for g in range(GROUPS):
                i = 2 * u + g
                p = score_buf(i)[:, 0:unit_cols(u)]
                pool.wait_ge(p_rec, i + 1)
                nc.gpsimd.tensor_scalar(p, p, srec[:, i:i + 1], None, ALU.mult).then_inc(p_norm, 1)

        block = ctx.enter_context(nc.Block())

        @block.sync
        def _(sp):
            def load_gu(f, k, slot):
                dst = gu_view(slot)
                sp.dma_start(dst[:, 0], gate[f][k].rearrange("p (k n) -> p k n", k=KD)).then_inc(w_loaded[slot], 16)
                sp.dma_start(dst[:, 1], up[f][k].rearrange("p (k n) -> p k n", k=KD)).then_inc(w_loaded[slot], 16)

            def load_halves(src, slot, cols):
                h = cols // 2
                sp.dma_start(wbuf[:, slot, 0:h], src[:, 0:h]).then_inc(w_loaded[slot], 16)
                sp.dma_start(wbuf[:, slot, h:cols], src[:, h:cols]).then_inc(w_loaded[slot], 16)

            for h in range(2):
                sp.dma_start(X[:, 4 * h:4 * h + 4, :],
                             xT[:, 4 * h * T:(4 * h + 4) * T].rearrange("p (k t) -> p k t", k=4)).then_inc(x_loaded, 16)
            for f in range(2):
                if f:
                    sp.wait_ge(res_ready, KD + 4)
                load_gu(f, 0, 0)
                if f:
                    sp.wait_ge(res_ready, 2 * KD)
                load_gu(f, 1, 1)
                sp.wait_ge(gu_ready, KF * f + 2)
                load_gu(f, 2, 0)
                with sp.Fori(0, (N_GU - 3) // 2) as i:
                    sp.wait_ge(gu_ready, KF * f + 4 + 4 * i)
                    load_gu(f, 2 * i + 3, 1)
                    sp.wait_ge(gu_ready, KF * f + 6 + 4 * i)
                    load_gu(f, 2 * i + 4, 0)
                for q in range(N_DN):
                    if q < 2:
                        sp.wait_ge(gu_ready, KF * f + KF - 2 + 2 * q)
                    else:
                        sp.wait_ge(res_ready, 2 * KD * f + 2 * (q - 1))
                    load_halves(down[f][q], (DN[f] + q) % 2, SLOT)
                if f == 0:
                    for n in range(N_IN):
                        if n < 2:
                            sp.wait_ge(res_ready, KD - 2 + 2 * n)
                        else:
                            sp.wait_ge(proj_ready, LAST_OF[n - 2] + 1)
                        load_halves(w_in[n], (IN0 + n) % 2, KD * IN_COLS[n])
                    for n in range(N_OUT):
                        sp.wait_ge(proj_ready, LAST_OF[N_IN - 2 + n] + 1)
                        load_halves(w_out[n], (OUT0 + n) % 2, KD * 512)
            for k in range(KD):
                sp.wait_ge(h_ready, 3 * KD + k + 1)
                sp.dma_start(out[k], H[:, k, N_META:T]).then_inc(out_done, 16)
            sp.wait_ge(out_done, 16 * KD)

        @block.tensor
        def _(pe):
            def loaded(c, slot, half_c):
                pe.wait_ge(w_loaded[slot], 32 * half_c + 32)

            def layer_norm(L):
                if L == 0:
                    pe.wait_ge(ready0, 5)
                    pe.wait_ge(x_loaded, 32)
                for k in range(KD):
                    if L:
                        pe.wait_ge(res_done, 2 + KD * (L - 1) + k + 1)
                    for h in range(2):
                        mm = nc.tensor.matmul(PS[:, 4 + h, 0:HALF], ones[:, :], X[:, k, h * HALF:(h + 1) * HALF],
                                              start=k == 0, stop=k == KD - 1)
                mm.then_inc(mean_ready, 1)
                for k in range(KD):
                    pe.wait_ge(squared, KD * L + k + 1)
                    for h in range(2):
                        mm = nc.tensor.matmul(PS[:, 6 + h, 0:HALF], ones[:, :], tmp_b[:, k % 2, h * HALF:(h + 1) * HALF],
                                              start=k == 0, stop=k == KD - 1)
                    mm.then_inc(sq_summed, 1)

            def gu_tiles(c, slot, half_c, m0, f):
                loaded(c, slot, half_c)
                w = gu_view(slot)
                for s in range(2):
                    pe.wait_ge(hid_done, KF * f + m0 + s + 1)
                    for g in range(2):
                        for k in range(KD):
                            for h in range(2):
                                mm = nc.tensor.matmul(PS[:, 4 * s + 2 * g + h, 0:HALF], w[:, g, k, s * P:(s + 1) * P],
                                                      H[:, k, h * HALF:(h + 1) * HALF], start=k == 0, stop=k == KD - 1)
                    mm.then_inc(gu_ready, 1)

            def res_tiles(c, slot, half_c, r0, src, kt, cols):
                loaded(c, slot, half_c)
                w = w_view(slot, kt, cols)
                for s in range(cols // P):
                    pe.wait_ge(res_done, r0 + s + 1)
                    for k in range(kt):
                        for h in range(2):
                            mm = nc.tensor.matmul(PS[:, 2 * (s % 2) + h, 0:HALF], w[:, k, s * P:(s + 1) * P],
                                                  src[:, k, h * HALF:(h + 1) * HALF], start=k == 0, stop=k == kt - 1)
                    mm.then_inc(res_ready, 1)

            def ffn(f):
                gu_tiles(GU[f], 0, GU[f] // 2, 0, f)
                with pe.Fori(0, (N_GU - 1) // 2) as i:
                    gu_tiles(None, 1, GU[f] // 2 + i, 4 * i + 2, f)
                    gu_tiles(None, 0, GU[f] // 2 + 1 + i, 4 * i + 4, f)
                pe.wait_ge(hid_done, 2 + KF * (f + 1))
                with pe.Fori(0, N_DN // 2) as i:
                    res_tiles(None, 1, DN[f] // 2 + i, 2 * KD * f + 4 * i, hid, KF, FF_CHUNK)
                    res_tiles(None, 0, DN[f] // 2 + 1 + i, 2 * KD * f + 4 * i + 2, hid, KF, FF_CHUNK)

            def proj_tile(n):
                kind, i, c, col = TILES[n]
                ci = IN0 + c
                if n == 0 or TILES[n - 1][2] != c:
                    loaded(ci, ci % 2, ci // 2)
                w = w_view(ci % 2, KD, IN_COLS[c])
                bank = 2 * (n % 2)
                pe.wait_ge(proj_done, n + 1)
                if kind == "gv":
                    for k in range(KD):
                        mm = nc.tensor.matmul(PS[0:CH, bank, :], chunk(H[:, k, :], i), w[:, k, :],
                                              start=k == 0, stop=k == KD - 1)
                elif kind == "av":
                    for t in range(NB + 1):
                        rows = N_META if t == 0 else BLOCK
                        lo = 0 if t == 0 else N_META + BLOCK * (t - 1)
                        dst = PS[0:rows, bank + 1, 0:P] if t == 0 else PS[:, bank, P * (t - 1):P * t]
                        for k in range(KD):
                            mm = nc.tensor.matmul(dst, H[:, k, lo:lo + rows], w[:, k, col:col + P],
                                                  start=k == 0, stop=k == KD - 1)
                else:
                    m = N_DIR * RANK if kind == "z" else P
                    for k in range(KD):
                        for h in range(2):
                            mm = nc.tensor.matmul(PS[0:m, bank + h, 0:HALF], w[:, k, col:col + m],
                                                  H[:, k, h * HALF:(h + 1) * HALF], start=k == 0, stop=k == KD - 1)
                mm.then_inc(proj_ready, 1)

            def gates(q):
                j, d = GATES[q]
                if q == 0:
                    pe.wait_ge(const_loaded, 16 * N_CONST)
                    pe.wait_ge(proj_done, 2 + 1)
                if q >= 2:
                    pe.wait_ge(gate_abs, q - 1)
                    pe.wait_ge(gate_min, q - 1)
                for h in range(2):
                    mm = nc.tensor.matmul(PS[:, 4 + 2 * (q % 2) + h, 0:HALF], w2[:, d, j * P:(j + 1) * P],
                                          zT[:, h * HALF:(h + 1) * HALF], start=True, stop=True)
                mm.then_inc(gate_ready, 1)

            def gla(j):
                pe.wait_ge(dec_pool, 2 * N_DIR * (j + 1))
                if j:
                    pe.wait_ge(o_done, NCH * j)
                for cc in range(NCH // 2):
                    n = j * (NCH // 2) + cc
                    if n >= 2:
                        pe.wait_ge(kx_done, n - 1)
                    if n == 0:
                        pe.wait_ge(gate_abs, len(GATES))
                        pe.wait_ge(gate_min, len(GATES))
                    for s in range(2):
                        for d in range(N_DIR):
                            mm = nc.tensor.transpose(PS[0:CH, 4 + n % 2, (2 * s + d) * P:(2 * s + d + 1) * P],
                                                     chunk(k_ex[:, d, :], 2 * cc + s), ident[:, :])
                    mm.then_inc(kx_ready, 1)
                pe.wait_ge(kx_done, (NCH // 2) * (j + 1))
                for s in range(NCH - 1):
                    n = j * (NCH - 1) + s
                    if n >= 2:
                        pe.wait_ge(st_done, 2 * (n - 1))
                    for d in range(N_DIR):
                        c = s if d == 0 else NCH - 1 - s
                        for a in range(2):
                            mm = nc.tensor.matmul(PS[DK * a:DK * (a + 1), 6 + n % 2, d * P:(d + 1) * P],
                                                  kxT[:, c, d * P + DK * a:d * P + DK * (a + 1)],
                                                  gv[:, c, (2 * j + a) * DV:(2 * j + a + 1) * DV], start=True, stop=True)
                    mm.then_inc(st_ready, 1)

                def a_scores(c):
                    n = j * NCH + c
                    if n >= 2:
                        pe.wait_ge(a_masked, n - 1)
                    elif n == 0:
                        pe.wait_ge(dec_dve, 2 * N_DIR)
                        pe.wait_ge(proj_done, 2 + len(TILES))
                    if c == 0:
                        pe.wait_ge(dec_dve, 2 * N_DIR * (j + 1))
                    for d in range(N_DIR):
                        for a in range(2):
                            rows = slice(DK * a, DK * (a + 1))
                            mm = nc.tensor.matmul(PS[0:CH, 2 * (n % 2) + a, d * CH:(d + 1) * CH],
                                                  chunk(k_in[rows, d, :], c), chunk(q_in[rows, d, :], c),
                                                  start=True, stop=True)
                    mm.then_inc(a_ready, 1)

                a_scores(0)
                for c in range(NCH):
                    if c + 1 < NCH:
                        a_scores(c + 1)
                    n = j * NCH + c
                    pe.wait_ge(a_done, n + 1)
                    if n >= 2:
                        pe.wait_ge(o_done, n - 1)
                    if c == 0:
                        pe.wait_ge(st_done, 2 * (NCH - 1) * (j + 1))
                    for a in range(2):
                        rows = slice(DK * a, DK * (a + 1))
                        dst = PS[:, 4 + 2 * (n % 2) + a, 0:CH]
                        dirs = [d for d in range(N_DIR) if (c > 0 if d == 0 else c < NCH - 1)]
                        nc.tensor.matmul(dst, gv[:, c, (2 * j + a) * DV:(2 * j + a + 1) * DV],
                                         a_sum[:, n % 2, a * CH:(a + 1) * CH], start=True, stop=False)
                        for d in dirs:
                            step = c if d == 0 else NCH - 1 - c
                            mm = nc.tensor.matmul(dst, state[rows, d, step, :], chunk(q_ex[rows, d, :], c),
                                                  start=False, stop=d == dirs[-1])
                    mm.then_inc(o_ready, 1)

            def gla_norm():
                for h in range(G_HEADS):
                    pe.wait_ge(o_sq, h + 1)
                    if h == 0:
                        pe.wait_ge(kx_done, PAIRS * NCH // 2)
                        pe.wait_ge(st_done, 2 * PAIRS * (NCH - 1))
                    if h >= 2:
                        pe.wait_ge(o_std, h - 1)
                    for x in range(2):
                        mm = nc.tensor.matmul(PS[:, 4 + 2 * (h % 2) + x, 0:HALF], ones_dv[:, :],
                                              tmp_a[:, h % 2, x * HALF:(x + 1) * HALF], start=True, stop=True)
                    mm.then_inc(o_ssum, 1)

            def att_scores(u):
                n, j = UNITS[u]
                runs, _ = unit_keys(n)
                if u == 0:
                    pe.wait_ge(a_masked, PAIRS * NCH)
                else:
                    pe.wait_ge(s_max, 2 * u)
                for g in range(GROUPS):
                    rows = slice(DH * g, DH * (g + 1))
                    if n < 0:
                        for r in range(REP):
                            mm = nc.tensor.matmul(PS[MROW * r:MROW * (r + 1), g, 0:S_META], qT[rows, r, 0:MROW],
                                                  kT[rows, 0:S_META], start=True, stop=True, tile_position=(DH * g, MROW * r))
                    else:
                        q = qT[rows, j, N_META + BLOCK * n:N_META + BLOCK * (n + 1)]
                        col = 0
                        for lo, hi in runs:
                            mm = nc.tensor.matmul(PS[:, g, col:col + hi - lo], q, kT[rows, lo:hi], start=True, stop=True)
                            col += hi - lo
                mm.then_inc(s_ready, 1)

            def att_transposes(u):
                n, j = UNITS[u]
                _, blocks = unit_keys(n)
                if u == 0:
                    pe.wait_ge(o_std, G_HEADS)
                if u >= 1:
                    pe.wait_ge(pt_act, u)
                    pe.wait_ge(pt_dve, u)
                    if j == 0:
                        pe.wait_ge(ptm_done, 2 * (n + 1))
                for g in range(GROUPS):
                    pe.wait_ge(p_norm, 2 * u + g + 1)
                    p = score_buf(2 * u + g)
                    nc.tensor.transpose(PS[0:N_META, 6 + g, j * P:(j + 1) * P], p[:, 0:N_META], ident[:, :])
                    for i in range(len(blocks)):
                        lo = SINK_COL + 1 + BLOCK * i
                        mm = nc.tensor.transpose(PS[:, 4 + g, i * P:(i + 1) * P], p[:, lo:lo + BLOCK], ident[:, :])
                    mm.then_inc(pt_ready, 1)

            def att_values(n):
                _, blocks = unit_keys(n)
                u = 0 if n < 0 else REP * (n + 1)
                pe.wait_ge(pt_act, u + 1)
                pe.wait_ge(pt_dve, u + 1)
                pe.wait_ge(ptm_done, 2 * (n + 2))
                cols = P if n < 0 else REP * BLOCK
                if n >= 1:
                    pe.wait_ge(att_done, n)
                if n < 0:
                    pe.wait_ge(o_done, PAIRS * NCH)
                for g in range(GROUPS):
                    dst = PS[DH * g:DH * (g + 1), 2 + (n + 1) % 2, 0:cols]
                    c = slice(DH * g, DH * (g + 1))
                    nc.tensor.matmul(dst, av[0:N_META, 0, c], PTm[:, g, 0:cols], start=True, stop=False)
                    for i, b in enumerate(blocks):
                        mm = nc.tensor.matmul(dst, av[:, 1 + b, c], PT[:, g, i, 0:cols],
                                              start=False, stop=i == len(blocks) - 1)
                mm.then_inc(att_ready, 1)

            for s in (hid_done, res_done, proj_done):
                pe.wait_ge(s, 2)
            layer_norm(0)
            pe.wait_ge(h_ready, KD)
            ffn(0)
            layer_norm(1)
            pe.wait_ge(h_ready, 2 * KD)
            for n in range(len(TILES)):
                proj_tile(n)
                for q in GATES_AFTER.get(n, []):
                    gates(q)
            for j in range(PAIRS):
                gla(j)
            gla_norm()
            att_scores(0)
            for u in range(len(UNITS)):
                if u + 1 < len(UNITS):
                    att_scores(u + 1)
                att_transposes(u)
                if u == 0 or UNITS[u][1] == REP - 1:
                    att_values(UNITS[u][0])
            pe.wait_ge(o_final, G_HEADS)
            pe.wait_ge(att_done, NB + 1)
            for n in range(N_OUT):
                c = OUT0 + n
                res_tiles(c, c % 2, c // 2, KD + 4 * n, mix, KD, 512)
            layer_norm(2)
            pe.wait_ge(h_ready, 3 * KD)
            ffn(1)
            layer_norm(3)

        @block.scalar
        def _(act):
            act.dma_start(par[:, :], params).then_inc(par_loaded, 16)
            act.dma_start(ident[:, :], ident_in).then_inc(const_loaded, 16)
            act.dma_start(masks[:, :, :], masks_in).then_inc(const_loaded, 16)
            act.dma_start(reset[:, :], reset_in).then_inc(const_loaded, 16)
            act.dma_start(w2[:, :, :], w2_in).then_inc(const_loaded, 16)
            act.dma_start(rel[:, 0:S_MID], rel_mid).then_inc(const_loaded, 16)
            act.dma_start(rel[:, S_MID:S_MID + S_END], rel_first).then_inc(const_loaded, 16)
            act.dma_start(bias_m[:, :, :], bias_meta).then_inc(const_loaded, 16)

            def layer_norm(L):
                if L == 0:
                    act.wait_ge(par_loaded, 16)
                    act.wait_ge(ready0, 5)
                for k in range(KD):
                    act.wait_ge(centred, KD * L + k + 1)
                    if KD * L + k >= 2:
                        act.wait_ge(sq_summed, KD * L + k - 1)
                    nc.scalar.activation(tmp_b[:, k % 2, :], X[:, k, :], ACT.Square).then_inc(squared, 1)
                act.wait_ge(sq_summed, KD * (L + 1))
                e = min(L, 1)
                nc.scalar.activation(halves(std[:, :]), pair(6), ACT.Sqrt, bias=eps[:, e:e + 1]).then_inc(std_ready, 1)
                for k in range(KD):
                    act.wait_ge(normed, KD * L + k + 1)
                    nc.scalar.activation(H[:, k, :], X[:, k, :], ACT.Identity, scale=par[:, C_G[L] + k:C_G[L] + k + 1],
                                         bias=par[:, C_B[L] + k:C_B[L] + k + 1]).then_inc(h_ready, 1)

            def silu_tile(m, s, f):
                act.wait_ge(gu_ready, KF * f + m + 1)
                nc.scalar.activation(halves(tmp_a[:, s, :]), pair(4 * s), ACT.Silu).then_inc(silu_ready, 1)

            def ffn(f):
                for s in range(2):
                    silu_tile(s, s, f)
                with act.Fori(0, (N_GU - 1) // 2) as i:
                    for s in range(4):
                        silu_tile(4 * i + 2 + s, s % 2, f)

            def proj_out(n):
                kind, i, _, _ = TILES[n]
                bank = 2 * (n % 2)
                act.wait_ge(proj_ready, n + 1)
                if kind == "z":
                    last = nc.scalar.activation(halves(zT), pair(bank, N_DIR * RANK), ACT.Copy)
                elif kind == "g":
                    last = nc.scalar.activation(halves(sg[:, i, :]), pair(bank), ACT.Silu)
                elif kind == "gq":
                    last = nc.scalar.activation(halves(gqT[:, i, :]), pair(bank), ACT.Copy, scale=DK ** -0.5)
                elif kind == "gk":
                    last = nc.scalar.activation(halves(gkT[:, i, :]), pair(bank), ACT.Copy)
                elif kind == "gv":
                    last = nc.scalar.activation(gv[:, i, :], PS[0:CH, bank, :], ACT.Copy)
                elif kind == "aq":
                    last = nc.scalar.activation(halves(qT[:, i, :]), pair(bank), ACT.Copy, scale=DH ** -0.5)
                elif kind == "ak":
                    nc.scalar.activation(kT[:, 0:N_META], PS[:, bank, 0:N_META], ACT.Copy)
                    nc.scalar.activation(kT[:, N_META + 1:HALF + 1], PS[:, bank, N_META:HALF], ACT.Copy)
                    last = nc.scalar.activation(kT[:, HALF + 1:KEYS], PS[:, bank + 1, 0:HALF], ACT.Copy)
                else:
                    nc.scalar.activation(av[:, 1:NB + 1, :], PS[:, bank, :].rearrange("p (t n) -> p t n", n=P), ACT.Copy)
                    last = nc.scalar.activation(av[0:N_META, 0, :], PS[0:N_META, bank + 1, 0:P], ACT.Copy)
                last.then_inc(proj_done, 1)

            def gates(q):
                act.wait_ge(gate_ready, q + 1)
                if q >= 2:
                    act.wait_ge(log_gate, q - 1)
                ln = tmp_a[:, q % 2, :]
                nc.scalar.activation(halves(ln), pair(4 + 2 * (q % 2)), ACT.Abs,
                                     bias=par[:, C_GATE + gate_col(q):C_GATE + gate_col(q) + 1]).then_inc(gate_abs, 1)
                act.wait_ge(gate_abs, q + 1)
                nc.scalar.activation(ln, ln, ACT.Exp, scale=-1.0).then_inc(gate_exp, 1)
                act.wait_ge(gate_exp, q + 1)
                nc.scalar.activation(ln, ln, ACT.Ln, bias=1.0).then_inc(gate_ln, 1)

            def decays(j):
                if j:
                    act.wait_ge(o_ready, NCH * j)
                for d in range(N_DIR):
                    q = N_DIR * j + d
                    sign = 1.0 if d == 0 else -1.0
                    act.wait_ge(ends_done, q + 1)
                    nc.scalar.activation(E_end[:, q, :], B_end[:, q, :], ACT.Exp, scale=1.0 / TAU).then_inc(end_exp, 1)
                    act.wait_ge(clamped, q + 1)
                    nc.scalar.activation(q_in[:, d, :], tmp_a[:, d, :], ACT.Exp, scale=sign / TAU).then_inc(dec_exp, 1)
                    nc.scalar.activation(k_in[:, d, :], tmp_a[:, d, :], ACT.Exp, scale=-sign / TAU).then_inc(dec_exp, 1)
                    act.wait_ge(rel_b, q + 1)
                    from_start, to_end = V[:, j, d, :], tmp_b[:, d, :]
                    ex_q, ex_k = (from_start, to_end) if d == 0 else (to_end, from_start)
                    nc.scalar.activation(q_ex[:, d, :], ex_q, ACT.Exp, scale=1.0 / TAU).then_inc(dec_exp, 1)
                    nc.scalar.activation(k_ex[:, d, :], ex_k, ACT.Exp, scale=1.0 / TAU).then_inc(dec_exp, 1)

            def gla(j):
                for cc in range(NCH // 2):
                    n = j * (NCH // 2) + cc
                    act.wait_ge(kx_ready, n + 1)
                    nc.scalar.activation(kxT[:, 2 * cc:2 * cc + 2, :],
                                         PS[0:CH, 4 + n % 2, :].rearrange("p (s n) -> p s n", s=2), ACT.Copy).then_inc(kx_done, 1)
                for c in range(NCH):
                    n = j * NCH + c
                    act.wait_ge(o_ready, n + 1)
                    nc.scalar.activation(chunk(gO[:, 2 * j:2 * j + 2, :], c),
                                         PS[:, 4 + 2 * (n % 2):6 + 2 * (n % 2), 0:CH],
                                         ACT.Copy).then_inc(o_done, 1)

            def gla_norm():
                act.wait_ge(o_done, PAIRS * NCH)
                for h in range(G_HEADS):
                    if h >= 2:
                        act.wait_ge(o_ssum, h - 1)
                        act.wait_ge(o_rstd, h - 1)
                    nc.scalar.activation(tmp_a[:, h % 2, :], gO[:, h, :], ACT.Square).then_inc(o_sq, 1)
                    act.wait_ge(o_ssum, h + 1)
                    nc.scalar.activation(halves(tmp_b[:, h % 2, :]), pair(4 + 2 * (h % 2)), ACT.Sqrt,
                                         bias=eps[:, 0:1]).then_inc(o_std, 1)

            def att_exp(u):
                cols = unit_cols(u)
                for g in range(GROUPS):
                    i = 2 * u + g
                    act.wait_ge(s_max, i + 1)
                    p = score_buf(i)[:, 0:cols]
                    nc.scalar.activation(p, p, ACT.Exp, scale=-1.0, bias=smin[:, i:i + 1],
                                         accum_out=ssum[:, i:i + 1]).then_inc(p_exp, 1)

            def att_copy(u):
                n, j = UNITS[u]
                k = len(unit_keys(n)[1])
                act.wait_ge(pt_ready, 2 * u + 1)
                if n >= 0:
                    act.wait_ge(att_ready, n + 1)
                nc.scalar.activation(PT[:, 0, 0:k, j * P:(j + 1) * P],
                                     PS[:, 4, 0:k * P].rearrange("p (k n) -> p k n", n=P), ACT.Copy).then_inc(pt_act, 1)
                if u == 0 or j == REP - 1:
                    c = (j + 1) * P
                    nc.scalar.activation(PTm[:, 0, 0:c], PS[0:N_META, 6, 0:c], ACT.Copy).then_inc(ptm_done, 1)

            layer_norm(0)
            ffn(0)
            layer_norm(1)
            for n in range(len(TILES)):
                proj_out(n)
                for q in GATES_AFTER.get(n, []):
                    gates(q)
            for j in range(PAIRS):
                decays(j)
                gla(j)
            gla_norm()
            att_exp(0)
            for u in range(len(UNITS)):
                if u + 1 < len(UNITS):
                    att_exp(u + 1)
                att_copy(u)
            layer_norm(2)
            ffn(1)
            layer_norm(3)

        @block.vector
        def _(dve):
            def layer_norm(L):
                dve.wait_ge(mean_ready, L + 1)
                for k in range(KD):
                    x = halves(X[:, k, :])
                    nc.vector.tensor_tensor(x, x, pair(4), ALU.subtract).then_inc(centred, 1)
                dve.wait_ge(std_ready, L + 1)
                nc.vector.reciprocal(rstd[:, :], std[:, :]).then_inc(rstd_ready, 1)
                dve.wait_ge(rstd_ready, L + 1)
                for k in range(KD):
                    nc.vector.tensor_tensor(X[:, k, :], X[:, k, :], rstd[:, :], ALU.mult).then_inc(normed, 1)

            def hidden_tile(m, s, f):
                dve.wait_ge(silu_ready, KF * f + m + 1)
                nc.vector.tensor_tensor(halves(hid[:, m, :]), halves(tmp_a[:, s, :]), pair(4 * s + 2),
                                        ALU.mult).then_inc(hid_done, 1)

            def residual_tile(n, s, r, share):
                dve.wait_ge(res_ready, r + 1)
                nc.vector.scalar_tensor_tensor(halves(X[:, n, :]), pair(2 * s), share, halves(H[:, n, :]),
                                               ALU.mult, ALU.add).then_inc(res_done, 1)

            def ffn(f):
                for s in range(2):
                    hidden_tile(s, s, f)
                with dve.Fori(0, (N_GU - 1) // 2) as i:
                    for s in range(4):
                        hidden_tile(4 * i + 2 + s, s % 2, f)
                with dve.Fori(0, KD // 2) as i:
                    for s in range(2):
                        residual_tile(2 * i + s, s, 2 * KD * f + 2 * i + s, 0.5 / ALPHA)

            def gates(q):
                j, d = GATES[q]
                v = V[:, j, d, :]
                lg = tmp_b[:, q % 2, :]
                dve.wait_ge(gate_abs, q + 1)
                nc.vector.tensor_scalar(halves(lg), pair(4 + 2 * (q % 2)), par[:, C_GATE + gate_col(q):C_GATE + gate_col(q) + 1],
                                        0.0, ALU.add, ALU.min).then_inc(gate_min, 1)
                dve.wait_ge(gate_min, q + 1)
                dve.wait_ge(gate_ln, q + 1)
                nc.vector.tensor_tensor(lg, lg, tmp_a[:, q % 2, :], ALU.subtract).then_inc(log_gate, 1)
                dve.wait_ge(log_gate, q + 1)
                nc.vector.tensor_tensor_scan(v, reset[:, :], lg, 0.0, ALU.mult, ALU.add).then_inc(scanned, 1)
                dve.wait_ge(scanned, q + 1)
                nc.vector.tensor_copy(B_end[:, q, :], v.rearrange("p (c t) -> p c t", c=NCH)[:, :, CH - 1]).then_inc(ends_done, 1)
                if d == 1:
                    dve.wait_ge(ends_done, q + 1)
                    nc.vector.tensor_tensor(v, v, lg, ALU.subtract).then_inc(decay_done, 1)

            def decays(j):
                dve.wait_ge(decay_done, j + 1)
                if j:
                    dve.wait_ge(dec_exp, 4 * N_DIR * j)
                for d in range(N_DIR):
                    q = N_DIR * j + d
                    v = V[:, j, d, :].rearrange("p (c t) -> p c t", c=NCH)
                    a = tmp_a[:, d, :].rearrange("p (c t) -> p c t", c=NCH)
                    b = tmp_b[:, d, :].rearrange("p (c t) -> p c t", c=NCH)
                    nc.vector.tensor_tensor(a, v, v[:, :, MID:MID + 1].to_broadcast([P, NCH, CH]),
                                            ALU.subtract).then_inc(rel_a, 1)
                    nc.vector.tensor_tensor(b, B_end[:, q, :].unsqueeze(2).to_broadcast([P, NCH, CH]), v,
                                            ALU.subtract).then_inc(rel_b, 1)
                    dve.wait_ge(rel_a, q + 1)
                    nc.vector.tensor_scalar(tmp_a[:, d, :], tmp_a[:, d, :], -EXP_LIMIT, EXP_LIMIT,
                                            ALU.max, ALU.min).then_inc(clamped, 1)
                for d in range(N_DIR):
                    q = N_DIR * j + d
                    dve.wait_ge(dec_exp, 4 * q + 1)
                    nc.vector.tensor_tensor(q_in[:, d, :], q_in[:, d, :], gqT[:, j, :], ALU.mult).then_inc(dec_dve, 1)
                    dve.wait_ge(dec_exp, 4 * q + 2)
                    nc.vector.tensor_tensor(k_in[:, d, :], k_in[:, d, :], gkT[:, j, :], ALU.mult).then_inc(dec_dve, 1)

            def gla(j):
                for s in range(NCH - 1):
                    n = j * (NCH - 1) + s
                    dve.wait_ge(st_ready, n + 1)
                    if s:
                        dve.wait_ge(st_done, 2 * n)
                    elif j:
                        dve.wait_ge(o_ready, NCH * j)
                    for d in range(N_DIR):
                        q = N_DIR * j + d
                        c = s if d == 0 else NCH - 1 - s
                        new = PS[:, 6 + n % 2, d * P:(d + 1) * P]
                        if s == 0:
                            nc.vector.tensor_copy(state[:, d, 1, :], new).then_inc(st_done, 1)
                        else:
                            dve.wait_ge(end_exp, q + 1)
                            nc.vector.scalar_tensor_tensor(state[:, d, s + 1, :], state[:, d, s, :], E_end[:, q, c:c + 1],
                                                           new, ALU.mult, ALU.add).then_inc(st_done, 1)
                for c in range(NCH):
                    n = j * NCH + c
                    dve.wait_ge(a_ready, n + 1)
                    both = a_dir[:, n % 2, :]
                    nc.vector.tensor_tensor(both.rearrange("p (a d t) -> p a d t", d=2, a=2),
                                            PS[0:CH, 2 * (n % 2):2 * (n % 2) + 2, 0:2 * CH].rearrange("p a (d t) -> p a d t", d=2),
                                            masks[:, :, :].unsqueeze(1).to_broadcast([CH, 2, N_DIR, CH]),
                                            ALU.mult).then_inc(a_masked, 1)
                    dve.wait_ge(a_masked, n + 1)
                    if n >= 2:
                        dve.wait_ge(o_ready, n - 1)
                    both = both.rearrange("p (a d t) -> p a d t", d=2, a=2)
                    nc.vector.tensor_tensor(a_sum[:, n % 2, :].rearrange("p (a t) -> p a t", a=2), both[:, :, 0, :], both[:, :, 1, :],
                                            ALU.add).then_inc(a_done, 1)

            def gla_norm():
                dve.wait_ge(o_done, PAIRS * NCH)
                for h in range(G_HEADS):
                    r = (std, rstd)[h % 2]
                    nc.vector.scalar_tensor_tensor(tmp_g[:, h % 2, :], gO[:, h, :], par[:, C_NORM:C_NORM + 1], sg[:, h, :],
                                                   ALU.mult, ALU.mult).then_inc(o_gated, 1)
                    dve.wait_ge(o_std, h + 1)
                    nc.vector.reciprocal(r[:, :], tmp_b[:, h % 2, :]).then_inc(o_rstd, 1)
                    dve.wait_ge(o_rstd, h + 1)
                    dve.wait_ge(o_gated, h + 1)
                    nc.vector.tensor_tensor(gO[:, h, :], tmp_g[:, h % 2, :], r[:, :], ALU.mult).then_inc(o_final, 1)

            def att_max(u):
                n, j = UNITS[u]
                cols = unit_cols(u)
                dve.wait_ge(s_ready, u + 1)
                dve.wait_ge(bias_done, 1 if n < 0 else 2 if n == 0 else 3)
                if u >= 2:
                    dve.wait_ge(pt_ready, 2 * (u - 1))
                for g in range(GROUPS):
                    i = 2 * u + g
                    h = REP * g + j
                    if n < 0:
                        bias = bias_m[:, g, :]
                    elif n == 0:
                        bias = bias_first[:, h, :]
                    else:
                        bias = bias_mid[:, h, 0:cols]
                    nc.vector.tensor_tensor_reduce(out=score_buf(i)[:, 0:cols], in0=PS[:, g, 0:cols], in1=bias, scale=-1.0,
                                                   scalar=-NEG, op0=ALU.add, op1=ALU.min,
                                                   accum_out=smin[:, i:i + 1]).then_inc(s_max, 1)

            def att_recip(u):
                for g in range(GROUPS):
                    i = 2 * u + g
                    dve.wait_ge(p_exp, i + 1)
                    nc.vector.reciprocal(srec[:, i:i + 1], ssum[:, i:i + 1]).then_inc(p_rec, 1)

            def att_copy(u):
                n, j = UNITS[u]
                k = len(unit_keys(n)[1])
                dve.wait_ge(pt_ready, 2 * u + 2)
                if n >= 0:
                    dve.wait_ge(att_ready, n + 1)
                nc.vector.tensor_copy(PT[:, 1, 0:k, j * P:(j + 1) * P],
                                      PS[:, 5, 0:k * P].rearrange("p (k n) -> p k n", n=P)).then_inc(pt_dve, 1)
                if u == 0 or j == REP - 1:
                    c = (j + 1) * P
                    nc.vector.tensor_copy(PTm[:, 1, 0:c], PS[0:N_META, 7, 0:c]).then_inc(ptm_done, 1)
                    dve.wait_ge(att_ready, n + 2)
                    o = PS[:, 2 + (n + 1) % 2, :]
                    if n < 0:
                        nc.vector.tensor_copy(mix[:, 0:REP, 0:N_META],
                                              o[:, 0:P].rearrange("p (r m) -> p r m", r=REP)[:, :, 0:N_META]).then_inc(att_done, 1)
                    else:
                        nc.vector.tensor_copy(mix[:, 0:REP, N_META + n * BLOCK:N_META + (n + 1) * BLOCK],
                                              o.rearrange("p (r m) -> p r m", r=REP)).then_inc(att_done, 1)

            layer_norm(0)
            ffn(0)
            layer_norm(1)
            for q in range(len(GATES)):
                gates(q)
            for j in range(PAIRS):
                decays(j)
                gla(j)
            gla_norm()
            att_max(0)
            for u in range(len(UNITS)):
                if u + 1 < len(UNITS):
                    att_max(u + 1)
                att_recip(u)
                att_copy(u)
            for n in range(KD):
                residual_tile(n, n % 2, KD + n, 1.0 / ALPHA)
            layer_norm(2)
            ffn(1)
            layer_norm(3)

        @block.gpsimd
        def _(pool):
            nc.gpsimd.memset(ones[:, :], 1.0 / D_MODEL).then_inc(ready0, 1)
            nc.gpsimd.memset(ones_dv[:, :], 1.0 / DV).then_inc(ready0, 1)
            nc.gpsimd.memset(eps[:, 0:1], EPS).then_inc(ready0, 1)
            nc.gpsimd.memset(eps[:, 1:2], EPS / ALPHA ** 2).then_inc(ready0, 1)
            nc.gpsimd.memset(kT[:, SINK_COL:SINK_COL + 1], 0.0).then_inc(ready0, 1)
            for n, s in enumerate((hid_done, hid_done, res_done, res_done, proj_done, proj_done)):
                nc.gpsimd.memset(credit[:, n:n + 1], 0.0).then_inc(s, 1)
            pool.wait_ge(const_loaded, 16 * N_CONST)
            pool.wait_ge(par_loaded, 16)
            nc.gpsimd.tensor_copy(bias_m[:, :, SINK_COL:SINK_COL + 1], par[:, C_SINKM:C_SINKM + GROUPS].unsqueeze(2)).then_inc(bias_done, 1)
            for j in range(PAIRS):
                for d in range(N_DIR):
                    q = N_DIR * j + d
                    pool.wait_ge(dec_exp, 4 * q + 3)
                    nc.gpsimd.tensor_tensor(q_ex[:, d, :], q_ex[:, d, :], gqT[:, j, :], ALU.mult).then_inc(dec_pool, 1)
                    pool.wait_ge(dec_exp, 4 * q + 4)
                    nc.gpsimd.tensor_tensor(k_ex[:, d, :], k_ex[:, d, :], gkT[:, j, :], ALU.mult).then_inc(dec_pool, 1)
            pool.wait_ge(o_done, PAIRS * NCH)
            for src, dst in ((rel[:, S_MID:S_MID + S_END], bias_first), (rel[:, 0:S_MID], bias_mid)):
                for h, slope in enumerate(slopes()):
                    nc.gpsimd.tensor_scalar(dst[:, h, :], src, slope, None, ALU.mult).then_inc(rel_done, 1)
                pool.wait_ge(rel_done, HEADS if dst is bias_first else 2 * HEADS)
                nc.gpsimd.tensor_copy(dst[:, :, SINK_COL:SINK_COL + 1], par[:, C_SINK:C_SINK + HEADS].unsqueeze(2)).then_inc(bias_done, 1)
            for u in range(len(UNITS)):
                normalise(pool, u)


def shape_constants():
    i, m = np.arange(BLOCK)[:, None], np.arange(3 * BLOCK)[None, :]
    dist = np.abs(m - BLOCK - i).astype(np.float32)
    band = np.where(dist <= WINDOW, -dist, NEG).astype(np.float32)
    head = np.zeros((BLOCK, N_META + 1), np.float32)
    rel_mid = np.concatenate([head, band], 1)
    rel_first = np.concatenate([head, band[:, BLOCK:]], 1)
    row = np.arange(P)
    q = (row % MROW)[:, None]
    kpos = (N_META + np.arange(BLOCK))[None, :]
    dist = np.abs(kpos - q).astype(np.float32)
    bias_meta = np.zeros((P, GROUPS, S_META), np.float32)
    for g in range(GROUPS):
        slope = np.array([slopes()[REP * g + r // MROW] for r in row], np.float32)[:, None]
        bias_meta[:, g, N_META + 1:] = np.where(dist <= WINDOW, -slope * dist, NEG)
    s, t = np.arange(CH)[:, None], np.arange(CH)[None, :]
    masks = np.stack([s <= t, s > t], 1).astype(np.float32)
    reset = np.ones((P, T), np.float32)
    reset[:, ::CH] = 0.0
    return {"rel_mid": rel_mid, "rel_first": rel_first, "bias_meta": bias_meta,
            "ident": np.eye(P, dtype=np.float32), "masks": masks, "reset": reset}


def lay_out(x, meta_tokens, ln_in_g, ln_in_b, ffn1_ln_g, ffn1_ln_b, ffn1_w_gate, ffn1_w_up, ffn1_w_down,
            w_in, attn_sink, gla_gate_w2, gla_gate_b, gla_norm_g, w_out, mix_ln_g, mix_ln_b,
            ffn2_w_gate, ffn2_w_up, ffn2_w_down, ffn2_ln_g, ffn2_ln_b):
    def kcols(w):
        return w.reshape(-1, P, w.shape[1]).transpose(1, 0, 2)

    def chunks(w, cols):
        k = kcols(w)
        n = w.shape[1] // cols
        return k.reshape(P, -1, n, cols).transpose(2, 0, 1, 3).reshape(n, P, -1)

    tokens = np.concatenate([meta_tokens, x[0]], 0)
    arrays = {"xT": kcols(tokens.T).reshape(P, -1)}
    cols = [v.reshape(KD, P).T for v in (ln_in_g, ln_in_b, ffn1_ln_g, ffn1_ln_b, mix_ln_g, mix_ln_b, ffn2_ln_g, ffn2_ln_b)]
    cols.append(gla_norm_g.reshape(DV, 1))
    cols.append(gla_gate_b.reshape(N_DIR * PAIRS, P).T)
    cols.append(np.broadcast_to(attn_sink.reshape(1, HEADS), (P, HEADS)))
    cols.append(np.repeat(attn_sink.reshape(GROUPS, REP), MROW, 1).T)
    arrays["params"] = np.concatenate(cols, 1)
    w2 = np.zeros((N_DIR * RANK, N_DIR, PAIRS * P), gla_gate_w2.dtype)
    for d in range(N_DIR):
        w2[d * RANK:(d + 1) * RANK, d] = gla_gate_w2[0, d]
    arrays["w2"] = w2
    for f, (g, u, dn) in enumerate([(ffn1_w_gate, ffn1_w_up, ffn1_w_down), (ffn2_w_gate, ffn2_w_up, ffn2_w_down)]):
        arrays[f"gate{f}"] = chunks(g[0], FF_CHUNK)
        arrays[f"up{f}"] = chunks(u[0], FF_CHUNK)
        arrays[f"down{f}"] = chunks(dn[0], FF_CHUNK)
    at = np.cumsum([0, HEADS * DH, GROUPS * DH, GROUPS * DH, G_HEADS * DK, G_HEADS * DK, G_HEADS * DV, G_HEADS * DV,
                    N_DIR * RANK])
    aq, ak, av, gq, gk, gv, gg, gz = [w_in[0][:, a:b] for a, b in zip(at[:-1], at[1:])]
    aq = aq.reshape(D_MODEL, GROUPS, REP, DH).transpose(0, 2, 1, 3).reshape(D_MODEL, -1)
    groups = [[gz, gg], [gq, gk], [gv], [aq], [ak, av]]
    for n, ws in enumerate(groups):
        arrays[f"w_in{n}"] = kcols(np.concatenate(ws, 1)).reshape(P, -1)
    wo = w_out[0]
    att = wo[:HEADS * DH].reshape(GROUPS, REP, DH, D_MODEL).transpose(1, 0, 2, 3).reshape(-1, D_MODEL)
    arrays["w_out"] = chunks(np.concatenate([att, wo[HEADS * DH:]], 0), 512)
    return arrays


def kernel(**inputs):
    import concourse.bacc as bacc
    from concourse.bass_utils import run_bass_kernel_spmd

    arrays = lay_out(**{k: np.asarray(v) for k, v in inputs.items()})
    arrays.update(shape_constants())
    arrays = {k: np.ascontiguousarray(v) for k, v in arrays.items()}
    nc = bacc.Bacc("TRN2", target_bir_lowering=False, num_devices=1)
    ap = {k: nc.dram_tensor(f"in_{k}", v.shape, F32, kind="ExternalInput").ap() for k, v in arrays.items()}
    out = nc.dram_tensor("out_T", (KD, P, SEQ), F32, kind="ExternalOutput").ap()
    build(nc, ap["xT"], ap["params"], ap["rel_mid"], ap["rel_first"], ap["bias_meta"], ap["ident"], ap["masks"],
          ap["reset"], ap["w2"], [ap["gate0"], ap["gate1"]], [ap["up0"], ap["up1"]], [ap["down0"], ap["down1"]],
          [ap[f"w_in{n}"] for n in range(N_IN)], ap["w_out"], out)
    r = run_bass_kernel_spmd(nc, [{f"in_{k}": v for k, v in arrays.items()}], core_ids=[0])
    y = r.results[0]["out_T"]
    return np.ascontiguousarray(y.reshape(D_MODEL, SEQ).T.reshape(1, SEQ, D_MODEL))
```

```python
from contextlib import ExitStack

import numpy as np

import concourse.bass as bass
from concourse import mybir

F32 = mybir.dt.float32
F16 = mybir.dt.float16
I32 = mybir.dt.int32
ALU = mybir.AluOpType
ACT = mybir.ActivationFunctionType
AX = mybir.AxisListType
LARGEST = bass.bass_isa.ReduceOp.max

P = 128
D_MODEL, SEQ, N_META = 1024, 512, 16
T = SEQ + N_META
HALF = T // 2
KD = D_MODEL // P
D_FF = 2816
KF = D_FF // P
HEADS, GROUPS, DH = 8, 2, 64
REP = HEADS // GROUPS
WINDOW = BLOCK = 128
NB = SEQ // BLOCK
G_HEADS, DK, DV, RANK, TAU = 4, 64, 128, 16, 16.0
N_DIR = 2
PAIRS = G_HEADS * DK // P
CH = 88
NCH = T // CH
MID = CH // 2
EPS = 1e-5
ALPHA = 2.0 ** 0.25
NEG = -1e30
EXP_LIMIT = 40.0 * TAU

SINK_COL = N_META
KEYS = T + 1
S_MID = N_META + 1 + 3 * BLOCK
S_END = N_META + 1 + 2 * BLOCK
S_META = N_META + 1 + BLOCK
MROW = 32

C_G = [0, 16, 32, 48]
C_B = [8, 24, 40, 56]
C_NORM = 64
C_GATE = 65
C_SINK = 69
C_SINKM = C_SINK + HEADS
N_PAR = C_SINKM + GROUPS

N_GU, N_DN = KF, KD
IN_COLS = [N_DIR * RANK + 2 * P] + [2 * P] * 8
N_IN, N_OUT = len(IN_COLS), KD // 2
GU = [0, N_GU + N_DN + N_IN + N_OUT]
DN = [GU[0] + N_GU, GU[1] + N_GU]
IN0 = DN[0] + N_DN
OUT0 = IN0 + N_IN
GU_COLS = 2 * KD * P
DN_COLS = KF * P
OUT_COLS = KD * 2 * P
SLOT = DN_COLS
N_CONST = 7
PRODUCTS = ((0, 0), (0, 1), (1, 0))
EXP_MASK = 0x7F800000
EXP_ONE = float(1 << 23)
EXP_TOP = 14
XF_GU, XF_IN, XF_INQ, XF_HID, XF_MIX = [0, 2], 1, 3, [4, 6], 5
N_XF = 7
HID, MIX = [0, 2], 1
B_STEPS = 9


def slopes():
    return [2.0 ** (-8.0 * (i + 1) / HEADS) for i in range(HEADS)]


def build(nc, xT, params, rel_mid, rel_first, bias_meta, ident_in, masks_in, reset_in, w2_in,
          gate, up, down, w_in, w_out, out):
    with ExitStack() as ctx:
        def sb(name, shape, dt=F32):
            return ctx.enter_context(nc.sbuf_tensor(name, shape, dt))

        def sem(name):
            return ctx.enter_context(nc.semaphore(name))

        PS = ctx.enter_context(nc.psum_tensor("PS", [P, 8, 512], F32))
        H = sb("H", [P, KD, T])
        X = sb("X", [P, KD, T])
        xs = sb("xs", [P, 2, KD, T], F16)
        stage = sb("stage", [P, 2, SLOT])
        wsp = sb("wsp", [P, 2, 2, SLOT], F16)
        big = sb("big", [P, (KF + 2) * T])
        hid = big[:, :].rearrange("p (m t) -> p m t", m=KF + 2)
        hid_s = big[:, :].bitcast(F16).rearrange("p (m s t) -> p m s t", m=KF + 2, s=2)
        tmp_a = sb("tmp_a", [P, 2, T])
        tmp_b = sb("tmp_b", [P, 2, T])
        std = sb("std", [P, T])
        rstd = sb("rstd", [P, T])
        cmax = sb("cmax", [P, 2])
        call = sb("call", [P, 2])
        cexp = sb("cexp", [P, 2], I32)
        cneg = sb("cneg", [P, 2], I32)
        wscale = sb("wscale", [P, 2])
        winv = sb("winv", [P, 2])
        oscale = sb("oscale", [P, 2])
        bmax = sb("bmax", [P, 6])
        ball = sb("ball", [P, 6])
        bound = sb("bound", [P, 3])
        bexp = sb("bexp", [P, 3], I32)
        bneg = sb("bneg", [P, 3], I32)
        xscale = sb("xscale", [P, 3])
        xinv = sb("xinv", [P, N_XF])
        par_s = sb("par_s", [P, 48])
        hmax = sb("hmax", [P, KF])
        hm = sb("hm", [P, 3])
        hall = sb("hall", [P, 3])
        hexp = sb("hexp", [P, 3], I32)
        hneg = sb("hneg", [P, 3], I32)
        hscale = sb("hscale", [P, 3])
        hinv = sb("hinv", [P, 3])
        mmax = sb("mmax", [P, 2])
        ones = sb("ones", [P, P])
        ones_dv = sb("ones_dv", [P, P])
        eps = sb("eps", [P, 2])
        par = sb("par", [P, N_PAR])
        ident = sb("ident", [P, P])
        masks = sb("masks", [CH, N_DIR, CH])
        reset = sb("reset", [P, T])
        w2 = sb("w2", [N_DIR * RANK, N_DIR, PAIRS * P])
        rel = sb("rel", [P, S_MID + S_END])
        bias_m = sb("bias_m", [P, GROUPS, S_META])
        credit = sb("credit", [1, 6])

        arena = sb("arena", [P, 9616])
        pools = {"big": [big, 0, (KF + 2) * T], "arena": [arena, 0, 9616],
                 "X": [X[:, :, :].rearrange("p k t -> p (k t)"), 0, KD * T]}

        def part(pool, shape):
            buf, start, size = pools[pool]
            n = int(np.prod(shape[1:]))
            pools[pool][1] += n
            assert start + n <= size, (pool, start, n, size)
            ap = buf[0:shape[0], start:start + n]
            if len(shape) == 2:
                return ap
            names = "abcd"[:len(shape) - 1]
            return ap.rearrange(f"p ({' '.join(names)}) -> p {' '.join(names)}",
                                **{n: s for n, s in zip(names, shape[1:])})

        mix = part("big", [P, KD, T])
        gv = part("big", [CH, NCH, G_HEADS * DV])
        sg = part("big", [P, G_HEADS, T])
        zT = part("big", [N_DIR * RANK, T])
        kT = sb("kT", [P, KEYS])
        qT = part("arena", [P, REP, T])
        av = part("arena", [P, NB + 1, P])
        mark = pools["arena"][1]
        gqT = part("X", [P, PAIRS, T])
        gkT = part("X", [P, PAIRS, T])
        V = part("X", [P, PAIRS, N_DIR, T])
        B_end = part("arena", [P, PAIRS * N_DIR, NCH])
        E_end = part("arena", [P, PAIRS * N_DIR, NCH])
        q_in = part("arena", [P, N_DIR, T])
        k_in = part("arena", [P, N_DIR, T])
        q_ex = part("arena", [P, N_DIR, T])
        k_ex = part("arena", [P, N_DIR, T])
        kxT = part("big", [CH, NCH, N_DIR * P])
        state = part("arena", [P, N_DIR, NCH, DV])
        a_dir = part("arena", [CH, 2, N_DIR * 2 * CH])
        a_sum = part("arena", [CH, 2, 2 * CH])
        pools["arena"][1] = mark
        pools["X"][1] = 0
        tmp_g = part("X", [P, 2, T])
        pools["X"][1] = 0
        bias_mid = part("arena", [P, HEADS, S_MID])
        bias_first = part("arena", [P, HEADS, S_END])
        PT = part("X", [P, GROUPS, 3, REP * BLOCK])
        PTm = part("X", [N_META, GROUPS, REP * BLOCK])
        gO = mix[:, REP:KD, :]
        scores = tmp_a[:, :, :].rearrange("p a t -> p (a t)")[:, 0:2 * 402]
        scores2 = tmp_b[:, :, :].rearrange("p a t -> p (a t)")[:, 0:2 * 402]
        N_UNIT = 1 + NB * REP
        smin = sb("smin", [P, 2 * N_UNIT])
        ssum = sb("ssum", [P, 2 * N_UNIT])
        srec = sb("srec", [P, 2 * N_UNIT])

        def score_buf(n):
            return (scores, scores2)[n // 2 % 2].rearrange("p (a t) -> p a t", a=2)[:, n % 2, :]

        x_loaded = sem("x_loaded")
        par_loaded = sem("par_loaded")
        const_loaded = sem("const_loaded")
        w_loaded = [sem(f"w_loaded{i}") for i in range(2)]
        ready0 = sem("ready0")
        mean_ready = sem("mean_ready")
        centred = sem("centred")
        squared = sem("squared")
        sq_summed = sem("sq_summed")
        std_ready = sem("std_ready")
        rstd_ready = sem("rstd_ready")
        normed = sem("normed")
        h_ready = sem("h_ready")
        gu_ready = sem("gu_ready")
        silu_ready = sem("silu_ready")
        w_max = sem("w_max")
        w_all = sem("w_all")
        w_scale = sem("w_scale")
        w_hi = sem("w_hi")
        w_ready = sem("w_ready")
        out_scale = sem("out_scale")
        b_max = sem("b_max")
        b_all = sem("b_all")
        b_step = sem("b_step")
        h_max = sem("h_max")
        h_all = sem("h_all")
        h_step = sem("h_step")
        xf_done = sem("xf_done")
        hs_hi = sem("hs_hi")
        hs_ready = sem("hs_ready")
        x_hi = sem("x_hi")
        x_ready = sem("x_ready")
        m_max = sem("m_max")
        m_hi = sem("m_hi")
        m_ready = sem("m_ready")
        hid_done = sem("hid_done")
        res_ready = sem("res_ready")
        res_done = sem("res_done")
        proj_ready = sem("proj_ready")
        proj_done = sem("proj_done")
        gate_ready = sem("gate_ready")
        gate_abs = sem("gate_abs")
        gate_exp = sem("gate_exp")
        gate_ln = sem("gate_ln")
        gate_min = sem("gate_min")
        log_gate = sem("log_gate")
        scanned = sem("scanned")
        ends_done = sem("ends_done")
        decay_done = sem("decay_done")
        end_exp = sem("end_exp")
        rel_a = sem("rel_a")
        clamp_lo = sem("clamp_lo")
        clamped = sem("clamped")
        rel_b = sem("rel_b")
        dec_exp = sem("dec_exp")
        dec_dve = sem("dec_dve")
        dec_pool = sem("dec_pool")
        kx_ready = sem("kx_ready")
        kx_done = sem("kx_done")
        st_ready = sem("st_ready")
        st_done = sem("st_done")
        a_ready = sem("a_ready")
        a_masked = sem("a_masked")
        a_done = sem("a_done")
        o_ready = sem("o_ready")
        o_done = sem("o_done")
        o_sq = sem("o_sq")
        o_ssum = sem("o_ssum")
        o_std = sem("o_std")
        o_rstd = sem("o_rstd")
        o_gated = sem("o_gated")
        o_final = sem("o_final")
        rel_done = sem("rel_done")
        bias_done = sem("bias_done")
        s_ready = sem("s_ready")
        s_max = sem("s_max")
        p_exp = sem("p_exp")
        p_rec = sem("p_rec")
        p_norm = sem("p_norm")
        pt_ready = sem("pt_ready")
        pt_act = sem("pt_act")
        pt_dve = sem("pt_dve")
        ptm_ready = sem("ptm_ready")
        ptm_done = sem("ptm_done")
        att_ready = sem("att_ready")
        att_done = sem("att_done")
        out_done = sem("out_done")

        def halves(ap):
            return ap.rearrange("p (h c) -> p h c", h=2)

        def pair(bank, rows=P):
            return PS[0:rows, bank:bank + 2, 0:HALF]

        def w_view(slot, part, kt, cols):
            return wsp[:, slot, part, 0:kt * cols].rearrange("p (k n) -> p k n", k=kt)

        Z = N_DIR * RANK
        TILES = ([("z", 0, 0, 0)] + [("g", i, i // 2, (Z if i < 2 else 0) + P * (i % 2)) for i in range(G_HEADS)]
                 + [("gq", i, 2, P * i) for i in range(PAIRS)] + [("gk", i, 3, P * i) for i in range(PAIRS)]
                 + [("gv", i, 4 + i // NCH, 0) for i in range(2 * NCH)]
                 + [("aq", i, 6 + i // 2, P * (i % 2)) for i in range(REP)] + [("ak", 0, 8, 0), ("av", 0, 8, P)])
        LAST_OF = [max(n for n, t in enumerate(TILES) if t[2] == c) for c in range(N_IN)]
        GATES = [(j, d) for j in range(PAIRS) for d in range(N_DIR)]
        GATES_AFTER = {1: [0, 1], 3: [2, 3]}
        UNITS = [(-1, 0)] + [(n, j) for n in range(NB) for j in range(REP)]

        def unit_keys(n):
            blocks = [0] if n < 0 else [b for b in (n - 1, n, n + 1) if 0 <= b < NB]
            lo, hi = SINK_COL + 1 + BLOCK * blocks[0], SINK_COL + 1 + BLOCK * (blocks[-1] + 1)
            runs = [(0, hi)] if blocks[0] == 0 else [(0, SINK_COL + 1), (lo, hi)]
            return runs, blocks

        def chunk(ap, c):
            return ap[..., CH * c:CH * (c + 1)]

        def unit_cols(u):
            return sum(hi - lo for lo, hi in unit_keys(UNITS[u][0])[0])

        def gate_col(q):
            j, d = GATES[q]
            return PAIRS * d + j

        def normalise(pool, u):
            for g in range(GROUPS):
                i = 2 * u + g
                p = score_buf(i)[:, 0:unit_cols(u)]
                pool.wait_ge(p_rec, i + 1)
                nc.gpsimd.tensor_scalar(p, p, srec[:, i:i + 1], None, ALU.mult).then_inc(p_norm, 1)

        block = ctx.enter_context(nc.Block())

        @block.sync
        def _(sp):
            def load_gu(f, m, slot):
                sp.dma_start(stage[:, slot, 0:KD * P], gate[f][m]).then_inc(w_loaded[slot], 16)
                sp.dma_start(stage[:, slot, KD * P:GU_COLS], up[f][m]).then_inc(w_loaded[slot], 16)

            def load_halves(src, slot, cols):
                h = cols // 2
                sp.dma_start(stage[:, slot, 0:h], src[:, 0:h]).then_inc(w_loaded[slot], 16)
                sp.dma_start(stage[:, slot, h:cols], src[:, h:cols]).then_inc(w_loaded[slot], 16)

            for h in range(2):
                sp.dma_start(X[:, 4 * h:4 * h + 4, :],
                             xT[:, 4 * h * T:(4 * h + 4) * T].rearrange("p (k t) -> p k t", k=4)).then_inc(x_loaded, 16)
            for f in range(2):
                for m in range(2):
                    if f:
                        sp.wait_ge(w_ready, GU[f] + m - 1)
                    load_gu(f, m, (GU[f] + m) % 2)
                with sp.Fori(0, (N_GU - 2) // 2) as i:
                    for t in range(2):
                        sp.wait_ge(w_ready, GU[f] + 1 + t + 2 * i)
                        load_gu(f, 2 * i + 2 + t, (GU[f] + t) % 2)
                with sp.Fori(0, N_DN // 2) as i:
                    for t in range(2):
                        sp.wait_ge(w_ready, DN[f] - 1 + t + 2 * i)
                        load_halves(down[f][2 * i + t], (DN[f] + t) % 2, DN_COLS)
                if f == 0:
                    for n in range(N_IN):
                        sp.wait_ge(w_ready, IN0 + n - 1)
                        load_halves(w_in[n], (IN0 + n) % 2, KD * IN_COLS[n])
                    for n in range(N_OUT):
                        sp.wait_ge(w_ready, OUT0 + n - 1)
                        load_halves(w_out[n], (OUT0 + n) % 2, OUT_COLS)
            for k in range(KD):
                sp.wait_ge(h_ready, 3 * KD + k + 1)
                sp.dma_start(out[k], H[:, k, N_META:T]).then_inc(out_done, 16)
            sp.wait_ge(out_done, 16 * KD)

        @block.tensor
        def _(pe):
            def layer_norm(L):
                if L == 0:
                    pe.wait_ge(ready0, 5)
                    pe.wait_ge(x_loaded, 32)
                for k in range(KD):
                    if L:
                        pe.wait_ge(res_done, 2 + KD * (L - 1) + k + 1)
                    for h in range(2):
                        mm = nc.tensor.matmul(PS[:, 4 + h, 0:HALF], ones[:, :], X[:, k, h * HALF:(h + 1) * HALF],
                                              start=k == 0, stop=k == KD - 1)
                mm.then_inc(mean_ready, 1)
                for k in range(KD):
                    pe.wait_ge(squared, KD * L + k + 1)
                    for h in range(2):
                        mm = nc.tensor.matmul(PS[:, 6 + h, 0:HALF], ones[:, :], tmp_b[:, k % 2, h * HALF:(h + 1) * HALF],
                                              start=k == 0, stop=k == KD - 1)
                    mm.then_inc(sq_summed, 1)

            def gu_tile(c, slot, m, s, f, first=False):
                pe.wait_ge(w_ready, c + 1)
                pe.wait_ge(hid_done, KF * f + m + 1)
                for g in range(2):
                    for k in range(KD):
                        if first and g == 0:
                            pe.wait_ge(x_ready, 2 * KD * f + k + 1)
                        for wp, xp in PRODUCTS:
                            w = wsp[:, slot, wp, (g * KD + k) * P:(g * KD + k + 1) * P]
                            for h in range(2):
                                mm = nc.tensor.matmul(PS[:, 4 * s + 2 * g + h, 0:HALF], w, xs[:, xp, k, h * HALF:(h + 1) * HALF],
                                                      start=k == 0 and wp + xp == 0, stop=k == KD - 1 and wp == 1)
                mm.then_inc(gu_ready, 1)

            def res_tile(r, s, w, src, kt, k_sem=None, k0=0):
                pe.wait_ge(res_done, r + 1)
                for k in range(kt):
                    if k_sem is not None:
                        pe.wait_ge(k_sem, k0 + k + 1)
                    for wp, xp in PRODUCTS:
                        for h in range(2):
                            mm = nc.tensor.matmul(PS[:, 2 * s + h, 0:HALF], w(wp, k), src(xp, k)[:, h * HALF:(h + 1) * HALF],
                                                  start=k == 0 and wp + xp == 0, stop=k == kt - 1 and wp == 1)
                mm.then_inc(res_ready, 1)

            def ffn(f):
                for m in range(2):
                    gu_tile(GU[f] + m, (GU[f] + m) % 2, m, m, f, first=m == 0)
                with pe.Fori(0, (N_GU - 2) // 2) as i:
                    for t in range(2):
                        gu_tile(GU[f] + 2 + t + 2 * i, (GU[f] + t) % 2, 2 * i + 2 + t, t, f)

                def down_tile(c, slot, r, s, first=False):
                    pe.wait_ge(w_ready, c + 1)
                    res_tile(r, s, lambda p, k: wsp[:, slot, p, k * P:(k + 1) * P], lambda p, k: hid_s[:, k, p, :], KF,
                             hs_ready if first else None, KF * f)

                pe.wait_ge(hid_done, 2 + KF * (f + 1))
                for q in range(2):
                    down_tile(DN[f] + q, (DN[f] + q) % 2, 2 * KD * f + q, q, first=q == 0)
                with pe.Fori(0, (N_DN - 2) // 2) as i:
                    for t in range(2):
                        down_tile(DN[f] + 2 + t + 2 * i, (DN[f] + t) % 2, 2 * KD * f + 2 + t + 2 * i, t)

            def proj_tile(n):
                kind, i, c, col = TILES[n]
                ci = IN0 + c
                pe.wait_ge(w_ready, ci + 1)
                bank = 2 * (n % 2)
                pe.wait_ge(proj_done, n + 1)

                def products(dst, cols, lhs_is_x, h=None):
                    for k in range(KD):
                        if n == 0:
                            pe.wait_ge(x_ready, KD + k + 1)
                        for wp, xp in PRODUCTS:
                            w = w_view(ci % 2, wp, KD, IN_COLS[c])[:, k, col:col + cols[0]]
                            x = xs[:, xp, k, cols[1]:cols[2]]
                            mm = nc.tensor.matmul(dst, x if lhs_is_x else w, w if lhs_is_x else x,
                                                  start=k == 0 and wp + xp == 0, stop=k == KD - 1 and wp == 1)
                    return mm

                if kind == "gv":
                    mm = products(PS[0:CH, bank, 0:2 * P], (2 * P, CH * (i % NCH), CH * (i % NCH + 1)), True)
                elif kind == "av":
                    for t in range(NB + 1):
                        rows = N_META if t == 0 else BLOCK
                        lo = 0 if t == 0 else N_META + BLOCK * (t - 1)
                        dst = PS[0:rows, bank + 1, 0:P] if t == 0 else PS[:, bank, P * (t - 1):P * t]
                        mm = products(dst, (P, lo, lo + rows), True)
                else:
                    m = Z if kind == "z" else P
                    for h in range(2):
                        mm = products(PS[0:m, bank + h, 0:HALF], (m, h * HALF, (h + 1) * HALF), False)
                mm.then_inc(proj_ready, 1)

            def gates(q):
                j, d = GATES[q]
                if q == 0:
                    pe.wait_ge(const_loaded, 16 * N_CONST)
                    pe.wait_ge(proj_done, 2 + 1)
                if q >= 2:
                    pe.wait_ge(gate_abs, q - 1)
                    pe.wait_ge(gate_min, q - 1)
                for h in range(2):
                    mm = nc.tensor.matmul(PS[:, 4 + 2 * (q % 2) + h, 0:HALF], w2[:, d, j * P:(j + 1) * P],
                                          zT[:, h * HALF:(h + 1) * HALF], start=True, stop=True)
                mm.then_inc(gate_ready, 1)

            def gla(j):
                pe.wait_ge(dec_pool, 2 * N_DIR * (j + 1))
                if j:
                    pe.wait_ge(o_done, NCH * j)
                for cc in range(NCH // 2):
                    n = j * (NCH // 2) + cc
                    if n >= 2:
                        pe.wait_ge(kx_done, n - 1)
                    if n == 0:
                        pe.wait_ge(gate_abs, len(GATES))
                        pe.wait_ge(gate_min, len(GATES))
                    for s in range(2):
                        for d in range(N_DIR):
                            mm = nc.tensor.transpose(PS[0:CH, 4 + n % 2, (2 * s + d) * P:(2 * s + d + 1) * P],
                                                     chunk(k_ex[:, d, :], 2 * cc + s), ident[:, :])
                    mm.then_inc(kx_ready, 1)
                pe.wait_ge(kx_done, (NCH // 2) * (j + 1))
                for s in range(NCH - 1):
                    n = j * (NCH - 1) + s
                    if n >= 2:
                        pe.wait_ge(st_done, 2 * (n - 1))
                    for d in range(N_DIR):
                        c = s if d == 0 else NCH - 1 - s
                        for a in range(2):
                            mm = nc.tensor.matmul(PS[DK * a:DK * (a + 1), 6 + n % 2, d * P:(d + 1) * P],
                                                  kxT[:, c, d * P + DK * a:d * P + DK * (a + 1)],
                                                  gv[:, c, (2 * j + a) * DV:(2 * j + a + 1) * DV], start=True, stop=True)
                    mm.then_inc(st_ready, 1)

                def a_scores(c):
                    n = j * NCH + c
                    if n >= 2:
                        pe.wait_ge(a_masked, n - 1)
                    elif n == 0:
                        pe.wait_ge(dec_dve, 2 * N_DIR)
                        pe.wait_ge(proj_done, 2 + len(TILES))
                    if c == 0:
                        pe.wait_ge(dec_dve, 2 * N_DIR * (j + 1))
                    for d in range(N_DIR):
                        for a in range(2):
                            rows = slice(DK * a, DK * (a + 1))
                            mm = nc.tensor.matmul(PS[0:CH, 2 * (n % 2) + a, d * CH:(d + 1) * CH],
                                                  chunk(k_in[rows, d, :], c), chunk(q_in[rows, d, :], c),
                                                  start=True, stop=True)
                    mm.then_inc(a_ready, 1)

                a_scores(0)
                for c in range(NCH):
                    if c + 1 < NCH:
                        a_scores(c + 1)
                    n = j * NCH + c
                    pe.wait_ge(a_done, n + 1)
                    if n >= 2:
                        pe.wait_ge(o_done, n - 1)
                    if c == 0:
                        pe.wait_ge(st_done, 2 * (NCH - 1) * (j + 1))
                    for a in range(2):
                        rows = slice(DK * a, DK * (a + 1))
                        dst = PS[:, 4 + 2 * (n % 2) + a, 0:CH]
                        dirs = [d for d in range(N_DIR) if (c > 0 if d == 0 else c < NCH - 1)]
                        nc.tensor.matmul(dst, gv[:, c, (2 * j + a) * DV:(2 * j + a + 1) * DV],
                                         a_sum[:, n % 2, a * CH:(a + 1) * CH], start=True, stop=False)
                        for d in dirs:
                            step = c if d == 0 else NCH - 1 - c
                            mm = nc.tensor.matmul(dst, state[rows, d, step, :], chunk(q_ex[rows, d, :], c),
                                                  start=False, stop=d == dirs[-1])
                    mm.then_inc(o_ready, 1)

            def gla_norm():
                for h in range(G_HEADS):
                    pe.wait_ge(o_sq, h + 1)
                    if h == 0:
                        pe.wait_ge(kx_done, PAIRS * NCH // 2)
                        pe.wait_ge(st_done, 2 * PAIRS * (NCH - 1))
                    if h >= 2:
                        pe.wait_ge(o_std, h - 1)
                    for x in range(2):
                        mm = nc.tensor.matmul(PS[:, 4 + 2 * (h % 2) + x, 0:HALF], ones_dv[:, :],
                                              tmp_a[:, h % 2, x * HALF:(x + 1) * HALF], start=True, stop=True)
                    mm.then_inc(o_ssum, 1)

            def att_scores(u):
                n, j = UNITS[u]
                runs, _ = unit_keys(n)
                if u == 0:
                    pe.wait_ge(a_masked, PAIRS * NCH)
                else:
                    pe.wait_ge(s_max, 2 * u)
                for g in range(GROUPS):
                    rows = slice(DH * g, DH * (g + 1))
                    if n < 0:
                        for r in range(REP):
                            mm = nc.tensor.matmul(PS[MROW * r:MROW * (r + 1), g, 0:S_META], qT[rows, r, 0:MROW],
                                                  kT[rows, 0:S_META], start=True, stop=True, tile_position=(DH * g, MROW * r))
                    else:
                        q = qT[rows, j, N_META + BLOCK * n:N_META + BLOCK * (n + 1)]
                        col = 0
                        for lo, hi in runs:
                            mm = nc.tensor.matmul(PS[:, g, col:col + hi - lo], q, kT[rows, lo:hi], start=True, stop=True)
                            col += hi - lo
                mm.then_inc(s_ready, 1)

            def att_transposes(u):
                n, j = UNITS[u]
                _, blocks = unit_keys(n)
                if u == 0:
                    pe.wait_ge(o_std, G_HEADS)
                if u >= 1:
                    pe.wait_ge(pt_act, u)
                    pe.wait_ge(pt_dve, u)
                    if j == 0:
                        pe.wait_ge(ptm_done, 2 * (n + 1))
                for g in range(GROUPS):
                    pe.wait_ge(p_norm, 2 * u + g + 1)
                    p = score_buf(2 * u + g)
                    nc.tensor.transpose(PS[0:N_META, 6 + g, j * P:(j + 1) * P], p[:, 0:N_META], ident[:, :])
                    for i in range(len(blocks)):
                        lo = SINK_COL + 1 + BLOCK * i
                        mm = nc.tensor.transpose(PS[:, 4 + g, i * P:(i + 1) * P], p[:, lo:lo + BLOCK], ident[:, :])
                    mm.then_inc(pt_ready, 1)

            def att_values(n):
                _, blocks = unit_keys(n)
                u = 0 if n < 0 else REP * (n + 1)
                pe.wait_ge(pt_act, u + 1)
                pe.wait_ge(pt_dve, u + 1)
                pe.wait_ge(ptm_done, 2 * (n + 2))
                cols = P if n < 0 else REP * BLOCK
                if n >= 1:
                    pe.wait_ge(att_done, n)
                if n < 0:
                    pe.wait_ge(o_done, PAIRS * NCH)
                for g in range(GROUPS):
                    dst = PS[DH * g:DH * (g + 1), 2 + (n + 1) % 2, 0:cols]
                    c = slice(DH * g, DH * (g + 1))
                    nc.tensor.matmul(dst, av[0:N_META, 0, c], PTm[:, g, 0:cols], start=True, stop=False)
                    for i, b in enumerate(blocks):
                        mm = nc.tensor.matmul(dst, av[:, 1 + b, c], PT[:, g, i, 0:cols],
                                              start=False, stop=i == len(blocks) - 1)
                mm.then_inc(att_ready, 1)

            for s in (hid_done, res_done, proj_done):
                pe.wait_ge(s, 2)
            layer_norm(0)
            ffn(0)
            layer_norm(1)
            for n in range(len(TILES)):
                proj_tile(n)
                if n in LAST_OF:
                    for q in GATES_AFTER.get(LAST_OF.index(n), []):
                        gates(q)
            for j in range(PAIRS):
                gla(j)
            gla_norm()
            att_scores(0)
            for u in range(len(UNITS)):
                if u + 1 < len(UNITS):
                    att_scores(u + 1)
                att_transposes(u)
                if u == 0 or UNITS[u][1] == REP - 1:
                    att_values(UNITS[u][0])
            for n in range(KD):
                c = OUT0 + n // 2
                pe.wait_ge(w_ready, c + 1)
                res_tile(KD + n, n % 2, lambda p, k: w_view(c % 2, p, KD, 2 * P)[:, k, P * (n % 2):P * (n % 2 + 1)],
                         lambda p, k: xs[:, p, k, :], KD, m_ready if n == 0 else None)
            layer_norm(2)
            ffn(1)
            layer_norm(3)

        @block.scalar
        def _(act):
            act.dma_start(par[:, :], params).then_inc(par_loaded, 16)
            act.dma_start(ident[:, :], ident_in).then_inc(const_loaded, 16)
            act.dma_start(masks[:, :, :], masks_in).then_inc(const_loaded, 16)
            act.dma_start(reset[:, :], reset_in).then_inc(const_loaded, 16)
            act.dma_start(w2[:, :, :], w2_in).then_inc(const_loaded, 16)
            act.dma_start(rel[:, 0:S_MID], rel_mid).then_inc(const_loaded, 16)
            act.dma_start(rel[:, S_MID:S_MID + S_END], rel_first).then_inc(const_loaded, 16)
            act.dma_start(bias_m[:, :, :], bias_meta).then_inc(const_loaded, 16)

            def layer_norm(L):
                if L == 0:
                    act.wait_ge(par_loaded, 16)
                    act.wait_ge(ready0, 5)
                for k in range(KD):
                    act.wait_ge(centred, KD * L + k + 1)
                    if KD * L + k >= 2:
                        act.wait_ge(sq_summed, KD * L + k - 1)
                    nc.scalar.activation(tmp_b[:, k % 2, :], X[:, k, :], ACT.Square).then_inc(squared, 1)
                act.wait_ge(sq_summed, KD * (L + 1))
                e = min(L, 1)
                nc.scalar.activation(halves(std[:, :]), pair(6), ACT.Sqrt, bias=eps[:, e:e + 1]).then_inc(std_ready, 1)
                for k in range(KD):
                    act.wait_ge(normed, KD * L + k + 1)
                    nc.scalar.activation(H[:, k, :], X[:, k, :], ACT.Identity, scale=par[:, C_G[L] + k:C_G[L] + k + 1],
                                         bias=par[:, C_B[L] + k:C_B[L] + k + 1]).then_inc(h_ready, 1)
                    if L < 3:
                        if L == 0 and k == 0:
                            act.wait_ge(b_step, B_STEPS)
                        nc.scalar.activation(xs[:, 0, k, :], X[:, k, :], ACT.Identity, scale=par_s[:, C_G[L] + k:C_G[L] + k + 1],
                                             bias=par_s[:, C_B[L] + k:C_B[L] + k + 1]).then_inc(x_hi, 1)

            def split_hi(c, slot, cols):
                act.wait_ge(w_scale, 4 * c + 3)
                nc.scalar.activation(wsp[:, slot, 0, 0:cols], stage[:, slot, 0:cols], ACT.Copy,
                                     scale=wscale[:, slot:slot + 1]).then_inc(w_hi, 1)

            def silu_tile(c, slot, m, s, f):
                act.wait_ge(gu_ready, KF * f + m + 1)
                act.wait_ge(out_scale, c + 1)
                nc.scalar.activation(halves(tmp_a[:, s, :]), pair(4 * s), ACT.Silu,
                                     scale=oscale[:, slot:slot + 1]).then_inc(silu_ready, 1)

            def ffn(f):
                with act.Fori(0, (N_GU - 2) // 2) as i:
                    for t in range(2):
                        c, slot = GU[f] + t + 2 * i, (GU[f] + t) % 2
                        split_hi(c + 1, 1 - slot, GU_COLS)
                        silu_tile(c, slot, 2 * i + t, t, f)
                for m in (KF - 2, KF - 1):
                    c = GU[f] + m
                    split_hi(c + 1, (c + 1) % 2, GU_COLS if m < KF - 1 else DN_COLS)
                    silu_tile(c, c % 2, m, m % 2, f)
                for m in range(KF):
                    if m == 0:
                        act.wait_ge(h_step, 4 * HID[f] + 3)
                        act.wait_ge(hid_done, 2 + KF * (f + 1))
                    if m >= 2:
                        act.wait_ge(hs_ready, KF * f + m - 1)
                    nc.scalar.activation(hid_s[:, m, 0, :], hid[:, m + 2, :], ACT.Copy,
                                         scale=hscale[:, HID[f]:HID[f] + 1]).then_inc(hs_hi, 1)
                for q in range(N_DN):
                    c = DN[f] + q + 1
                    if q < N_DN - 1 or f == 0:
                        if q:
                            act.wait_ge(res_ready, 2 * KD * f + q)
                        split_hi(c, c % 2, DN_COLS if q < N_DN - 1 else KD * IN_COLS[0])

            def proj_out(n):
                kind, i, c, _ = TILES[n]
                bank = 2 * (n % 2)
                slot = (IN0 + c) % 2
                back = oscale[:, slot:slot + 1]

                def out(dst, src, func=ACT.Copy):
                    return nc.scalar.activation(dst, src, func, scale=back[0:src.shape[0]])

                act.wait_ge(proj_ready, n + 1)
                act.wait_ge(out_scale, IN0 + c + 1)
                if kind == "z":
                    last = out(halves(zT), pair(bank, Z))
                elif kind == "g":
                    last = out(halves(sg[:, i, :]), pair(bank), ACT.Silu)
                elif kind == "gv":
                    last = out(gv[:, i % NCH, 2 * P * (i // NCH):2 * P * (i // NCH + 1)], PS[0:CH, bank, 0:2 * P])
                elif kind == "ak":
                    out(kT[:, 0:N_META], PS[:, bank, 0:N_META])
                    out(kT[:, N_META + 1:HALF + 1], PS[:, bank, N_META:HALF])
                    last = out(kT[:, HALF + 1:KEYS], PS[:, bank + 1, 0:HALF])
                elif kind == "av":
                    out(av[:, 1:NB + 1, :], PS[:, bank, :].rearrange("p (t n) -> p t n", n=P))
                    last = out(av[0:N_META, 0, :], PS[0:N_META, bank + 1, 0:P])
                else:
                    last = out(halves({"gq": gqT, "gk": gkT, "aq": qT}[kind][:, i, :]), pair(bank))
                last.then_inc(proj_done, 1)

            def gates(q):
                act.wait_ge(gate_ready, q + 1)
                if q >= 2:
                    act.wait_ge(log_gate, q - 1)
                ln = tmp_a[:, q % 2, :]
                nc.scalar.activation(halves(ln), pair(4 + 2 * (q % 2)), ACT.Abs,
                                     bias=par[:, C_GATE + gate_col(q):C_GATE + gate_col(q) + 1]).then_inc(gate_abs, 1)
                act.wait_ge(gate_abs, q + 1)
                nc.scalar.activation(ln, ln, ACT.Exp, scale=-1.0).then_inc(gate_exp, 1)
                act.wait_ge(gate_exp, q + 1)
                nc.scalar.activation(ln, ln, ACT.Ln, bias=1.0).then_inc(gate_ln, 1)

            def decays(j):
                if j:
                    act.wait_ge(o_ready, NCH * j)
                for d in range(N_DIR):
                    q = N_DIR * j + d
                    sign = 1.0 if d == 0 else -1.0
                    act.wait_ge(ends_done, q + 1)
                    nc.scalar.activation(E_end[:, q, :], B_end[:, q, :], ACT.Exp, scale=1.0 / TAU).then_inc(end_exp, 1)
                    act.wait_ge(clamped, q + 1)
                    nc.scalar.activation(q_in[:, d, :], tmp_a[:, d, :], ACT.Exp, scale=sign / TAU).then_inc(dec_exp, 1)
                    nc.scalar.activation(k_in[:, d, :], tmp_a[:, d, :], ACT.Exp, scale=-sign / TAU).then_inc(dec_exp, 1)
                    act.wait_ge(rel_b, q + 1)
                    from_start, to_end = V[:, j, d, :], tmp_b[:, d, :]
                    ex_q, ex_k = (from_start, to_end) if d == 0 else (to_end, from_start)
                    nc.scalar.activation(q_ex[:, d, :], ex_q, ACT.Exp, scale=1.0 / TAU).then_inc(dec_exp, 1)
                    nc.scalar.activation(k_ex[:, d, :], ex_k, ACT.Exp, scale=1.0 / TAU).then_inc(dec_exp, 1)

            def gla(j):
                for cc in range(NCH // 2):
                    n = j * (NCH // 2) + cc
                    act.wait_ge(kx_ready, n + 1)
                    nc.scalar.activation(kxT[:, 2 * cc:2 * cc + 2, :],
                                         PS[0:CH, 4 + n % 2, :].rearrange("p (s n) -> p s n", s=2), ACT.Copy).then_inc(kx_done, 1)
                for c in range(NCH):
                    n = j * NCH + c
                    act.wait_ge(o_ready, n + 1)
                    nc.scalar.activation(chunk(gO[:, 2 * j:2 * j + 2, :], c),
                                         PS[:, 4 + 2 * (n % 2):6 + 2 * (n % 2), 0:CH],
                                         ACT.Copy).then_inc(o_done, 1)

            def gla_norm():
                act.wait_ge(o_done, PAIRS * NCH)
                for h in range(G_HEADS):
                    if h >= 2:
                        act.wait_ge(o_ssum, h - 1)
                        act.wait_ge(o_rstd, h - 1)
                    nc.scalar.activation(tmp_a[:, h % 2, :], gO[:, h, :], ACT.Square).then_inc(o_sq, 1)
                    act.wait_ge(o_ssum, h + 1)
                    nc.scalar.activation(halves(tmp_b[:, h % 2, :]), pair(4 + 2 * (h % 2)), ACT.Sqrt,
                                         bias=eps[:, 0:1]).then_inc(o_std, 1)

            def att_exp(u):
                cols = unit_cols(u)
                for g in range(GROUPS):
                    i = 2 * u + g
                    act.wait_ge(s_max, i + 1)
                    p = score_buf(i)[:, 0:cols]
                    nc.scalar.activation(p, p, ACT.Exp, scale=-1.0, bias=smin[:, i:i + 1],
                                         accum_out=ssum[:, i:i + 1]).then_inc(p_exp, 1)

            def att_copy(u):
                n, j = UNITS[u]
                k = len(unit_keys(n)[1])
                act.wait_ge(pt_ready, 2 * u + 1)
                if n < 0:
                    act.wait_ge(o_final, G_HEADS)
                if n >= 0:
                    act.wait_ge(att_ready, n + 1)
                nc.scalar.activation(PT[:, 0, 0:k, j * P:(j + 1) * P],
                                     PS[:, 4, 0:k * P].rearrange("p (k n) -> p k n", n=P), ACT.Copy).then_inc(pt_act, 1)
                if u == 0 or j == REP - 1:
                    c = (j + 1) * P
                    nc.scalar.activation(PTm[:, 0, 0:c], PS[0:N_META, 6, 0:c], ACT.Copy).then_inc(ptm_done, 1)

            split_hi(0, 0, GU_COLS)
            layer_norm(0)
            ffn(0)
            layer_norm(1)
            for n in range(len(TILES)):
                if n == 0 or n - 1 in LAST_OF:
                    c = IN0 + TILES[n][2] + 1
                    split_hi(c, c % 2, KD * 2 * P)
                proj_out(n)
                if n in LAST_OF:
                    for q in GATES_AFTER.get(LAST_OF.index(n), []):
                        gates(q)
            for j in range(PAIRS):
                decays(j)
                gla(j)
            gla_norm()
            att_exp(0)
            for u in range(len(UNITS)):
                if u + 1 < len(UNITS):
                    att_exp(u + 1)
                att_copy(u)
            for k in range(KD):
                act.wait_ge(h_step, 4 * MIX + 3)
                nc.scalar.activation(xs[:, 0, k, :], mix[:, k, :], ACT.Copy, scale=hscale[:, MIX:MIX + 1]).then_inc(m_hi, 1)
            for n in range(N_OUT):
                c = OUT0 + n + 1
                if n:
                    act.wait_ge(res_ready, KD + 2 * n)
                split_hi(c, c % 2, OUT_COLS if n < N_OUT - 1 else GU_COLS)
            layer_norm(2)
            ffn(1)
            layer_norm(3)

        @block.vector
        def _(dve):
            def layer_norm(L):
                dve.wait_ge(mean_ready, L + 1)
                for k in range(KD):
                    x = halves(X[:, k, :])
                    nc.vector.tensor_tensor(x, x, pair(4), ALU.subtract).then_inc(centred, 1)
                dve.wait_ge(std_ready, L + 1)
                nc.vector.reciprocal(rstd[:, :], std[:, :]).then_inc(rstd_ready, 1)
                dve.wait_ge(rstd_ready, L + 1)

                def split_lo(k):
                    dve.wait_ge(x_hi, KD * L + k + 1)
                    nc.vector.scalar_tensor_tensor(xs[:, 1, k, :], H[:, k, :], xscale[:, L:L + 1], xs[:, 0, k, :],
                                                   ALU.mult, ALU.subtract).then_inc(x_ready, 1)

                for k in range(KD):
                    nc.vector.tensor_tensor(X[:, k, :], X[:, k, :], rstd[:, :], ALU.mult).then_inc(normed, 1)
                    if k >= 2 and L < 3:
                        split_lo(k - 2)
                if L < 3:
                    split_lo(KD - 2)
                    split_lo(KD - 1)

            def scale_of(largest, e, neg, scale, inv, signal, at):
                nc.vector.tensor_scalar(e, largest.bitcast(I32), EXP_MASK, None, ALU.bitwise_and).then_inc(signal, 1)
                dve.wait_ge(signal, at + 1)
                nc.vector.tensor_scalar(neg, e, (EXP_TOP + 1) * EXP_ONE, -1.0, ALU.max, ALU.mult).then_inc(signal, 1)
                dve.wait_ge(signal, at + 2)
                nc.vector.tensor_scalar(scale.bitcast(I32), neg, (2 * 127 + EXP_TOP) * EXP_ONE, None, ALU.add).then_inc(signal, 1)
                nc.vector.tensor_scalar(inv.bitcast(I32), neg, -1.0, -EXP_TOP * EXP_ONE, ALU.mult, ALU.add).then_inc(signal, 1)

            def hidden_max(m):
                nc.vector.tensor_reduce(hmax[:, :].unsqueeze(2)[:, m, :], hid[:, m + 2, :], AX.X, ALU.max,
                                        apply_absolute_value=True).then_inc(h_max, 1)

            def split(c, slot, half_c, cols, xf=None, tile=None, tile_at=0):
                one = slice(slot, slot + 1)
                if tile is not None:
                    dve.wait_ge(hid_done, 2 + tile_at + tile + 1)
                dve.wait_ge(w_loaded[slot], 32 * half_c + 32)
                nc.vector.tensor_reduce(cmax[:, one], stage[:, slot, 0:cols], AX.X, ALU.max,
                                        apply_absolute_value=True).then_inc(w_max, 1)
                if tile is not None:
                    hidden_max(tile)
                dve.wait_ge(w_all, c + 1)
                scale_of(call[:, one], cexp[:, one], cneg[:, one], wscale[:, one], winv[:, one], w_scale, 4 * c)
                if xf is not None:
                    out_scale_of(c, slot, xf)
                dve.wait_ge(w_hi, c + 1)
                nc.vector.scalar_tensor_tensor(wsp[:, slot, 1, 0:cols], stage[:, slot, 0:cols], wscale[:, one],
                                               wsp[:, slot, 0, 0:cols], ALU.mult, ALU.subtract).then_inc(w_ready, 1)

            def out_scale_of(c, slot, xf):
                dve.wait_ge(w_scale, 4 * c + 4)
                nc.vector.tensor_tensor(oscale[:, slot:slot + 1], winv[:, slot:slot + 1], xinv[:, xf:xf + 1],
                                        ALU.mult).then_inc(out_scale, 1)

            def hidden_tile(m, slot, s, f):
                dve.wait_ge(silu_ready, KF * f + m + 1)
                nc.vector.scalar_tensor_tensor(halves(hid[:, m + 2, :]), pair(4 * s + 2), oscale[:, slot:slot + 1],
                                               halves(tmp_a[:, s, :]), ALU.mult, ALU.mult).then_inc(hid_done, 1)

            def residual_tile(n, s, r, slot):
                dve.wait_ge(res_ready, r + 1)
                nc.vector.scalar_tensor_tensor(halves(X[:, n, :]), pair(2 * s), oscale[:, slot:slot + 1], halves(H[:, n, :]),
                                               ALU.mult, ALU.add).then_inc(res_done, 1)

            def back_scale(i, xf, share):
                one = slice(i, i + 1)
                dve.wait_ge(h_all, i + 1)
                scale_of(hall[:, one], hexp[:, one], hneg[:, one], hscale[:, one], hinv[:, one], h_step, 4 * i)
                dve.wait_ge(h_step, 4 * i + 4)
                nc.vector.tensor_scalar(xinv[:, xf:xf + 1], hinv[:, one], share, None, ALU.mult).then_inc(xf_done, 1)

            def ffn(f):
                def step(m):
                    c = GU[f] + m
                    last = m == KF - 1
                    split(c + 1, (c + 1) % 2, (c + 1) // 2, DN_COLS if last else GU_COLS, None if last else XF_GU[f],
                          m - 1 if m else None, KF * f)
                    hidden_tile(m, c % 2, m % 2, f)

                step(0)
                step(1)
                with dve.Fori(0, (N_GU - 4) // 2) as i:
                    for t in range(2):
                        m, c, slot = 2 + t + 2 * i, GU[f] + 2 + t + 2 * i, (GU[f] + t) % 2
                        split(c + 1, 1 - slot, (GU[f] + t + 3) // 2 + i, GU_COLS, XF_GU[f], m - 1, KF * f)
                        hidden_tile(m, slot, t, f)
                step(KF - 2)
                step(KF - 1)
                dve.wait_ge(hid_done, 2 + KF * (f + 1))
                hidden_max(KF - 1)
                dve.wait_ge(h_max, (KF + 1) * f + KF)
                nc.vector.tensor_reduce(hm[:, HID[f]:HID[f] + 1], hmax[:, :], AX.X, ALU.max).then_inc(h_max, 1)
                back_scale(HID[f], XF_HID[f], 0.5 / ALPHA)
                for m in range(KF):
                    dve.wait_ge(hs_hi, KF * f + m + 1)
                    nc.vector.scalar_tensor_tensor(hid_s[:, m, 1, :], hid[:, m + 2, :], hscale[:, HID[f]:HID[f] + 1], hid_s[:, m, 0, :],
                                                   ALU.mult, ALU.subtract).then_inc(hs_ready, 1)
                dve.wait_ge(xf_done, HID[f] + 1)
                for q in range(N_DN):
                    c = DN[f] + q
                    out_scale_of(c, c % 2, XF_HID[f])
                    if q < N_DN - 1:
                        split(c + 1, (c + 1) % 2, (c + 1) // 2, DN_COLS)
                    elif f == 0:
                        split(c + 1, (c + 1) % 2, (c + 1) // 2, KD * IN_COLS[0], XF_IN)
                    dve.wait_ge(out_scale, c + 1)
                    residual_tile(q, q % 2, 2 * KD * f + q, c % 2)

            def gates(q):
                j, d = GATES[q]
                v = V[:, j, d, :]
                lg = tmp_b[:, q % 2, :]
                dve.wait_ge(gate_abs, q + 1)
                nc.vector.tensor_scalar(halves(lg), pair(4 + 2 * (q % 2)), par[:, C_GATE + gate_col(q):C_GATE + gate_col(q) + 1],
                                        0.0, ALU.add, ALU.min).then_inc(gate_min, 1)
                dve.wait_ge(gate_min, q + 1)
                dve.wait_ge(gate_ln, q + 1)
                nc.vector.tensor_tensor(lg, lg, tmp_a[:, q % 2, :], ALU.subtract).then_inc(log_gate, 1)
                dve.wait_ge(log_gate, q + 1)
                nc.vector.tensor_tensor_scan(v, reset[:, :], lg, 0.0, ALU.mult, ALU.add).then_inc(scanned, 1)
                dve.wait_ge(scanned, q + 1)
                nc.vector.tensor_copy(B_end[:, q, :], v.rearrange("p (c t) -> p c t", c=NCH)[:, :, CH - 1]).then_inc(ends_done, 1)
                if d == 1:
                    dve.wait_ge(ends_done, q + 1)
                    nc.vector.tensor_tensor(v, v, lg, ALU.subtract).then_inc(decay_done, 1)

            def decays(j):
                dve.wait_ge(decay_done, j + 1)
                if j:
                    dve.wait_ge(dec_exp, 4 * N_DIR * j)
                for d in range(N_DIR):
                    q = N_DIR * j + d
                    v = V[:, j, d, :].rearrange("p (c t) -> p c t", c=NCH)
                    a = tmp_a[:, d, :].rearrange("p (c t) -> p c t", c=NCH)
                    b = tmp_b[:, d, :].rearrange("p (c t) -> p c t", c=NCH)
                    nc.vector.tensor_tensor(a, v, v[:, :, MID:MID + 1].to_broadcast([P, NCH, CH]),
                                            ALU.subtract).then_inc(rel_a, 1)
                    nc.vector.tensor_tensor(b, B_end[:, q, :].unsqueeze(2).to_broadcast([P, NCH, CH]), v,
                                            ALU.subtract).then_inc(rel_b, 1)
                    dve.wait_ge(rel_a, q + 1)
                    nc.vector.tensor_scalar(tmp_a[:, d, :], tmp_a[:, d, :], -EXP_LIMIT, EXP_LIMIT,
                                            ALU.max, ALU.min).then_inc(clamped, 1)
                for d in range(N_DIR):
                    q = N_DIR * j + d
                    dve.wait_ge(dec_exp, 4 * q + 1)
                    nc.vector.tensor_tensor(q_in[:, d, :], q_in[:, d, :], gqT[:, j, :], ALU.mult).then_inc(dec_dve, 1)
                    dve.wait_ge(dec_exp, 4 * q + 2)
                    nc.vector.tensor_tensor(k_in[:, d, :], k_in[:, d, :], gkT[:, j, :], ALU.mult).then_inc(dec_dve, 1)

            def gla(j):
                for s in range(NCH - 1):
                    n = j * (NCH - 1) + s
                    dve.wait_ge(st_ready, n + 1)
                    if s:
                        dve.wait_ge(st_done, 2 * n)
                    elif j:
                        dve.wait_ge(o_ready, NCH * j)
                    for d in range(N_DIR):
                        q = N_DIR * j + d
                        c = s if d == 0 else NCH - 1 - s
                        new = PS[:, 6 + n % 2, d * P:(d + 1) * P]
                        if s == 0:
                            nc.vector.tensor_copy(state[:, d, 1, :], new).then_inc(st_done, 1)
                        else:
                            dve.wait_ge(end_exp, q + 1)
                            nc.vector.scalar_tensor_tensor(state[:, d, s + 1, :], state[:, d, s, :], E_end[:, q, c:c + 1],
                                                           new, ALU.mult, ALU.add).then_inc(st_done, 1)
                for c in range(NCH):
                    n = j * NCH + c
                    dve.wait_ge(a_ready, n + 1)
                    both = a_dir[:, n % 2, :]
                    nc.vector.tensor_tensor(both.rearrange("p (a d t) -> p a d t", d=2, a=2),
                                            PS[0:CH, 2 * (n % 2):2 * (n % 2) + 2, 0:2 * CH].rearrange("p a (d t) -> p a d t", d=2),
                                            masks[:, :, :].unsqueeze(1).to_broadcast([CH, 2, N_DIR, CH]),
                                            ALU.mult).then_inc(a_masked, 1)
                    dve.wait_ge(a_masked, n + 1)
                    if n >= 2:
                        dve.wait_ge(o_ready, n - 1)
                    both = both.rearrange("p (a d t) -> p a d t", d=2, a=2)
                    nc.vector.tensor_tensor(a_sum[:, n % 2, :].rearrange("p (a t) -> p a t", a=2), both[:, :, 0, :], both[:, :, 1, :],
                                            ALU.add).then_inc(a_done, 1)

            def gla_norm():
                dve.wait_ge(o_done, PAIRS * NCH)
                for h in range(G_HEADS):
                    r = (std, rstd)[h % 2]
                    nc.vector.scalar_tensor_tensor(tmp_g[:, h % 2, :], gO[:, h, :], par[:, C_NORM:C_NORM + 1], sg[:, h, :],
                                                   ALU.mult, ALU.mult).then_inc(o_gated, 1)
                    dve.wait_ge(o_std, h + 1)
                    nc.vector.reciprocal(r[:, :], tmp_b[:, h % 2, :]).then_inc(o_rstd, 1)
                    dve.wait_ge(o_rstd, h + 1)
                    dve.wait_ge(o_gated, h + 1)
                    nc.vector.tensor_tensor(gO[:, h, :], tmp_g[:, h % 2, :], r[:, :], ALU.mult).then_inc(o_final, 1)

            def att_max(u):
                n, j = UNITS[u]
                cols = unit_cols(u)
                dve.wait_ge(s_ready, u + 1)
                dve.wait_ge(bias_done, 1 if n < 0 else 2 if n == 0 else 3)
                if u >= 2:
                    dve.wait_ge(pt_ready, 2 * (u - 1))
                for g in range(GROUPS):
                    i = 2 * u + g
                    h = REP * g + j
                    if n < 0:
                        bias = bias_m[:, g, :]
                    elif n == 0:
                        bias = bias_first[:, h, :]
                    else:
                        bias = bias_mid[:, h, 0:cols]
                    nc.vector.tensor_tensor_reduce(out=score_buf(i)[:, 0:cols], in0=PS[:, g, 0:cols], in1=bias, scale=-1.0,
                                                   scalar=-NEG, op0=ALU.add, op1=ALU.min,
                                                   accum_out=smin[:, i:i + 1]).then_inc(s_max, 1)

            def att_recip(u):
                for g in range(GROUPS):
                    i = 2 * u + g
                    dve.wait_ge(p_exp, i + 1)
                    nc.vector.reciprocal(srec[:, i:i + 1], ssum[:, i:i + 1]).then_inc(p_rec, 1)

            def att_copy(u):
                n, j = UNITS[u]
                k = len(unit_keys(n)[1])
                dve.wait_ge(pt_ready, 2 * u + 2)
                if n >= 0:
                    dve.wait_ge(att_ready, n + 1)
                nc.vector.tensor_copy(PT[:, 1, 0:k, j * P:(j + 1) * P],
                                      PS[:, 5, 0:k * P].rearrange("p (k n) -> p k n", n=P)).then_inc(pt_dve, 1)
                if u == 0 or j == REP - 1:
                    c = (j + 1) * P
                    nc.vector.tensor_copy(PTm[:, 1, 0:c], PS[0:N_META, 7, 0:c]).then_inc(ptm_done, 1)
                    dve.wait_ge(att_ready, n + 2)
                    o = PS[:, 2 + (n + 1) % 2, :]
                    if n < 0:
                        nc.vector.tensor_copy(mix[:, 0:REP, 0:N_META],
                                              o[:, 0:P].rearrange("p (r m) -> p r m", r=REP)[:, :, 0:N_META]).then_inc(att_done, 1)
                    else:
                        nc.vector.tensor_copy(mix[:, 0:REP, N_META + n * BLOCK:N_META + (n + 1) * BLOCK],
                                              o.rearrange("p (r m) -> p r m", r=REP)).then_inc(att_done, 1)

            def layer_norm_scales():
                dve.wait_ge(par_loaded, 16)
                nc.vector.tensor_reduce(bmax[:, :], par[:, 0:48].rearrange("p (v k) -> p v k", k=KD), AX.X, ALU.max,
                                        apply_absolute_value=True).then_inc(b_max, 1)
                dve.wait_ge(b_all, 1)
                gain_bias = ball[:, :].rearrange("p (l v) -> p l v", v=2)
                nc.vector.scalar_tensor_tensor(bound[:, :], gain_bias[:, :, 0], D_MODEL ** 0.5, gain_bias[:, :, 1],
                                               ALU.mult, ALU.add).then_inc(b_step, 1)
                dve.wait_ge(b_step, 1)
                scale_of(bound[:, :], bexp[:, :], bneg[:, :], xscale[:, :], xinv[:, 0:3], b_step, 1)
                dve.wait_ge(b_step, 5)
                nc.vector.tensor_scalar(xinv[:, XF_INQ:XF_INQ + 1], xinv[:, XF_IN:XF_IN + 1], DH ** -0.5, None,
                                        ALU.mult).then_inc(b_step, 1)
                for L in range(3):
                    nc.vector.tensor_scalar(par_s[:, 16 * L:16 * L + 16], par[:, 16 * L:16 * L + 16], xscale[:, L:L + 1], None,
                                            ALU.mult).then_inc(b_step, 1)
                dve.wait_ge(b_step, B_STEPS)

            layer_norm_scales()
            split(0, 0, 0, GU_COLS, XF_GU[0])
            layer_norm(0)
            ffn(0)
            layer_norm(1)
            for i in range(N_IN):
                c = IN0 + i + 1
                if i:
                    dve.wait_ge(proj_done, 2 + LAST_OF[i - 1] + 1)
                xf = None if i == N_IN - 1 else XF_INQ if i + 1 in (2, 6, 7) else XF_IN
                split(c, c % 2, c // 2, KD * 2 * P, xf)
                for q in GATES_AFTER.get(i, []):
                    gates(q)
            for j in range(PAIRS):
                decays(j)
                gla(j)
            gla_norm()
            dve.wait_ge(o_final, G_HEADS)
            nc.vector.tensor_reduce(mmax[:, 0:1], gO.rearrange("p k t -> p (k t)"), AX.X, ALU.max,
                                    apply_absolute_value=True).then_inc(m_max, 1)
            att_max(0)
            for u in range(len(UNITS)):
                if u + 1 < len(UNITS):
                    att_max(u + 1)
                att_recip(u)
                att_copy(u)
            dve.wait_ge(att_done, NB + 1)
            nc.vector.tensor_reduce(mmax[:, 1:2], mix[:, 0:REP, :].rearrange("p k t -> p (k t)"), AX.X, ALU.max,
                                    apply_absolute_value=True).then_inc(m_max, 1)
            dve.wait_ge(m_max, 2)
            nc.vector.tensor_reduce(hm[:, MIX:MIX + 1], mmax[:, :], AX.X, ALU.max).then_inc(m_max, 1)
            back_scale(MIX, XF_MIX, 1.0 / ALPHA)
            for k in range(KD):
                dve.wait_ge(m_hi, k + 1)
                nc.vector.scalar_tensor_tensor(xs[:, 1, k, :], mix[:, k, :], hscale[:, MIX:MIX + 1], xs[:, 0, k, :],
                                               ALU.mult, ALU.subtract).then_inc(m_ready, 1)
            dve.wait_ge(xf_done, MIX + 1)
            for n in range(N_OUT):
                c = OUT0 + n
                out_scale_of(c, c % 2, XF_MIX)
                last = n == N_OUT - 1
                split(c + 1, (c + 1) % 2, (c + 1) // 2, GU_COLS if last else OUT_COLS, XF_GU[1] if last else None)
                dve.wait_ge(out_scale, c + 1)
                for t in range(2):
                    residual_tile(2 * n + t, t, KD + 2 * n + t, c % 2)
            layer_norm(2)
            ffn(1)
            layer_norm(3)

        @block.gpsimd
        def _(pool):
            nc.gpsimd.memset(ones[:, :], 1.0 / D_MODEL).then_inc(ready0, 1)
            nc.gpsimd.memset(ones_dv[:, :], 1.0 / DV).then_inc(ready0, 1)
            nc.gpsimd.memset(eps[:, 0:1], EPS).then_inc(ready0, 1)
            nc.gpsimd.memset(eps[:, 1:2], EPS / ALPHA ** 2).then_inc(ready0, 1)
            nc.gpsimd.memset(kT[:, SINK_COL:SINK_COL + 1], 0.0).then_inc(ready0, 1)
            for n, s in enumerate((hid_done, hid_done, res_done, res_done, proj_done, proj_done)):
                nc.gpsimd.memset(credit[:, n:n + 1], 0.0).then_inc(s, 1)

            def over_all(c, slot):
                pool.wait_ge(w_max, c + 1)
                nc.gpsimd.partition_all_reduce(call[:, slot:slot + 1], cmax[:, slot:slot + 1], P, LARGEST).then_inc(w_all, 1)

            def over_all_range(a, b):
                for c in range(a, b):
                    over_all(c, c % 2)

            def over_all_h(i):
                nc.gpsimd.partition_all_reduce(hall[:, i:i + 1], hm[:, i:i + 1], P, LARGEST).then_inc(h_all, 1)

            pool.wait_ge(b_max, 1)
            nc.gpsimd.partition_all_reduce(ball[:, :], bmax[:, :], P, LARGEST).then_inc(b_all, 1)
            pool.wait_ge(const_loaded, 16 * N_CONST)
            nc.gpsimd.tensor_copy(bias_m[:, :, SINK_COL:SINK_COL + 1], par[:, C_SINKM:C_SINKM + GROUPS].unsqueeze(2)).then_inc(bias_done, 1)
            over_all_range(0, DN[0] + 1)
            pool.wait_ge(h_max, KF + 1)
            over_all_h(HID[0])
            over_all_range(DN[0] + 1, OUT0 + 1)
            for j in range(PAIRS):
                for d in range(N_DIR):
                    q = N_DIR * j + d
                    pool.wait_ge(dec_exp, 4 * q + 3)
                    nc.gpsimd.tensor_tensor(q_ex[:, d, :], q_ex[:, d, :], gqT[:, j, :], ALU.mult).then_inc(dec_pool, 1)
                    pool.wait_ge(dec_exp, 4 * q + 4)
                    nc.gpsimd.tensor_tensor(k_ex[:, d, :], k_ex[:, d, :], gkT[:, j, :], ALU.mult).then_inc(dec_pool, 1)
            pool.wait_ge(o_done, PAIRS * NCH)
            for src, dst in ((rel[:, S_MID:S_MID + S_END], bias_first), (rel[:, 0:S_MID], bias_mid)):
                for h, slope in enumerate(slopes()):
                    nc.gpsimd.tensor_scalar(dst[:, h, :], src, slope, None, ALU.mult).then_inc(rel_done, 1)
                pool.wait_ge(rel_done, HEADS if dst is bias_first else 2 * HEADS)
                nc.gpsimd.tensor_copy(dst[:, :, SINK_COL:SINK_COL + 1], par[:, C_SINK:C_SINK + HEADS].unsqueeze(2)).then_inc(bias_done, 1)
            for u in range(len(UNITS)):
                normalise(pool, u)
            pool.wait_ge(m_max, 3)
            over_all_h(MIX)
            over_all_range(OUT0 + 1, DN[1] + 1)
            pool.wait_ge(h_max, 2 * (KF + 1))
            over_all_h(HID[1])
            over_all_range(DN[1] + 1, DN[1] + N_DN)


def shape_constants():
    i, m = np.arange(BLOCK)[:, None], np.arange(3 * BLOCK)[None, :]
    dist = np.abs(m - BLOCK - i).astype(np.float32)
    band = np.where(dist <= WINDOW, -dist, NEG).astype(np.float32)
    head = np.zeros((BLOCK, N_META + 1), np.float32)
    rel_mid = np.concatenate([head, band], 1)
    rel_first = np.concatenate([head, band[:, BLOCK:]], 1)
    row = np.arange(P)
    q = (row % MROW)[:, None]
    kpos = (N_META + np.arange(BLOCK))[None, :]
    dist = np.abs(kpos - q).astype(np.float32)
    bias_meta = np.zeros((P, GROUPS, S_META), np.float32)
    for g in range(GROUPS):
        slope = np.array([slopes()[REP * g + r // MROW] for r in row], np.float32)[:, None]
        bias_meta[:, g, N_META + 1:] = np.where(dist <= WINDOW, -slope * dist, NEG)
    s, t = np.arange(CH)[:, None], np.arange(CH)[None, :]
    masks = np.stack([s <= t, s > t], 1).astype(np.float32)
    reset = np.ones((P, T), np.float32)
    reset[:, ::CH] = 0.0
    return {"rel_mid": rel_mid, "rel_first": rel_first, "bias_meta": bias_meta,
            "ident": np.eye(P, dtype=np.float32), "masks": masks, "reset": reset}


def lay_out(x, meta_tokens, ln_in_g, ln_in_b, ffn1_ln_g, ffn1_ln_b, ffn1_w_gate, ffn1_w_up, ffn1_w_down,
            w_in, attn_sink, gla_gate_w2, gla_gate_b, gla_norm_g, w_out, mix_ln_g, mix_ln_b,
            ffn2_w_gate, ffn2_w_up, ffn2_w_down, ffn2_ln_g, ffn2_ln_b):
    def kcols(w):
        return w.reshape(-1, P, w.shape[1]).transpose(1, 0, 2)

    def chunks(w, cols):
        k = kcols(w)
        n = w.shape[1] // cols
        return k.reshape(P, -1, n, cols).transpose(2, 0, 1, 3).reshape(n, P, -1)

    tokens = np.concatenate([meta_tokens, x[0]], 0)
    arrays = {"xT": kcols(tokens.T).reshape(P, -1)}
    cols = [v.reshape(KD, P).T for v in (ln_in_g, ln_in_b, ffn1_ln_g, ffn1_ln_b, mix_ln_g, mix_ln_b, ffn2_ln_g, ffn2_ln_b)]
    cols.append(gla_norm_g.reshape(DV, 1))
    cols.append(gla_gate_b.reshape(N_DIR * PAIRS, P).T)
    cols.append(np.broadcast_to(attn_sink.reshape(1, HEADS), (P, HEADS)))
    cols.append(np.repeat(attn_sink.reshape(GROUPS, REP), MROW, 1).T)
    arrays["params"] = np.concatenate(cols, 1)
    w2 = np.zeros((N_DIR * RANK, N_DIR, PAIRS * P), gla_gate_w2.dtype)
    for d in range(N_DIR):
        w2[d * RANK:(d + 1) * RANK, d] = gla_gate_w2[0, d]
    arrays["w2"] = w2
    for f, (g, u, dn) in enumerate([(ffn1_w_gate, ffn1_w_up, ffn1_w_down), (ffn2_w_gate, ffn2_w_up, ffn2_w_down)]):
        arrays[f"gate{f}"] = chunks(g[0], P)
        arrays[f"up{f}"] = chunks(u[0], P)
        arrays[f"down{f}"] = chunks(dn[0], P)
    at = np.cumsum([0, HEADS * DH, GROUPS * DH, GROUPS * DH, G_HEADS * DK, G_HEADS * DK, G_HEADS * DV, G_HEADS * DV,
                    N_DIR * RANK])
    aq, ak, av, gq, gk, gv, gg, gz = [w_in[0][:, a:b] for a, b in zip(at[:-1], at[1:])]
    aq = aq.reshape(D_MODEL, GROUPS, REP, DH).transpose(0, 2, 1, 3).reshape(D_MODEL, -1)
    groups = [[gz, gg[:, :256]], [gg[:, 256:]], [gq], [gk], [gv[:, :256]], [gv[:, 256:]], [aq[:, :256]], [aq[:, 256:]],
              [ak, av]]
    for n, ws in enumerate(groups):
        arrays[f"w_in{n}"] = kcols(np.concatenate(ws, 1)).reshape(P, -1)
    wo = w_out[0]
    att = wo[:HEADS * DH].reshape(GROUPS, REP, DH, D_MODEL).transpose(1, 0, 2, 3).reshape(-1, D_MODEL)
    arrays["w_out"] = chunks(np.concatenate([att, wo[HEADS * DH:]], 0), 2 * P)
    return arrays


def kernel(**inputs):
    import concourse.bacc as bacc
    from concourse.bass_utils import run_bass_kernel_spmd

    arrays = lay_out(**{k: np.asarray(v) for k, v in inputs.items()})
    arrays.update(shape_constants())
    arrays = {k: np.ascontiguousarray(v) for k, v in arrays.items()}
    nc = bacc.Bacc("TRN2", target_bir_lowering=False, num_devices=1)
    ap = {k: nc.dram_tensor(f"in_{k}", v.shape, F32, kind="ExternalInput").ap() for k, v in arrays.items()}
    out = nc.dram_tensor("out_T", (KD, P, SEQ), F32, kind="ExternalOutput").ap()
    build(nc, ap["xT"], ap["params"], ap["rel_mid"], ap["rel_first"], ap["bias_meta"], ap["ident"], ap["masks"],
          ap["reset"], ap["w2"], [ap["gate0"], ap["gate1"]], [ap["up0"], ap["up1"]], [ap["down0"], ap["down1"]],
          [ap[f"w_in{n}"] for n in range(N_IN)], ap["w_out"], out)
    r = run_bass_kernel_spmd(nc, [{f"in_{k}": v for k, v in arrays.items()}], core_ids=[0])
    y = r.results[0]["out_T"]
    return np.ascontiguousarray(y.reshape(D_MODEL, SEQ).T.reshape(1, SEQ, D_MODEL))
```

```python
from contextlib import ExitStack

import numpy as np

import concourse.bass as bass
from concourse import mybir

F32 = mybir.dt.float32
F16 = mybir.dt.float16
I32 = mybir.dt.int32
ALU = mybir.AluOpType
ACT = mybir.ActivationFunctionType
AX = mybir.AxisListType
LARGEST = bass.bass_isa.ReduceOp.max

P = 128
D_MODEL, SEQ, N_META = 1024, 512, 16
T = SEQ + N_META
HALF = T // 2
KD = D_MODEL // P
D_FF = 2816
KF = D_FF // P
HEADS, GROUPS, DH = 8, 2, 64
REP = HEADS // GROUPS
WINDOW = BLOCK = 128
NB = SEQ // BLOCK
G_HEADS, DK, DV, RANK, TAU = 4, 64, 128, 16, 16.0
N_DIR = 2
PAIRS = G_HEADS * DK // P
CH = 88
NCH = T // CH
MID = CH // 2
EPS = 1e-5
ALPHA = 2.0 ** 0.25
NEG = -1e30
EXP_LIMIT = 40.0 * TAU

SINK_COL = N_META
KEYS = T + 1
S_MID = N_META + 1 + 3 * BLOCK
S_END = N_META + 1 + 2 * BLOCK
S_META = N_META + 1 + BLOCK
MROW = 32

C_G = [0, 16, 32, 48]
C_B = [8, 24, 40, 56]
C_NORM = 64
C_GATE = 65
C_SINK = 69
C_SINKM = C_SINK + HEADS
N_PAR = C_SINKM + GROUPS

N_GU, N_DN = KF, KD
IN_COLS = [N_DIR * RANK + 2 * P] + [2 * P] * 8
N_IN, N_OUT = len(IN_COLS), KD // 2
GU = [0, N_GU + N_DN + N_IN + N_OUT]
DN = [GU[0] + N_GU, GU[1] + N_GU]
IN0 = DN[0] + N_DN
OUT0 = IN0 + N_IN
GU_COLS = 2 * KD * P
DN_COLS = KF * P
OUT_COLS = KD * 2 * P
SLOT = DN_COLS
N_CONST = 7
PRODUCTS = ((0, 0), (1, 0), (0, 1))
EXP_MASK = 0x7F800000
EXP_ONE = float(1 << 23)
EXP_TOP = 14
XF_GU, XF_IN, XF_INQ, XF_FOUND = [0, 2], 1, 3, 4
KF_A = KF - 3
HID, HID_B, MIX = [0, 3], [1, 4], 2
N_FOUND = 5
N_XF = XF_FOUND + N_FOUND
SHIFT_TILES = [4, 6, 4, 6]
SHIFT_SUMS = [sum(n - 1 for n in SHIFT_TILES[:L]) for L in range(5)]
HI_STEPS = [5, 7, 11, 15]
LO_STEPS = [3, 5, 5, 9, 9, 15]
NORM_SUMS = [0, 2]
NORM_STEPS = 5
B_STEPS = 9


def slopes():
    return [2.0 ** (-8.0 * (i + 1) / HEADS) for i in range(HEADS)]


def build(nc, xT, params, rel_in, head_in, bias_meta, ident_in, masks_in, reset_in, w2_in,
          gate, up, down, w_in, w_out, out):
    with ExitStack() as ctx:
        def sb(name, shape, dt=F32):
            return ctx.enter_context(nc.sbuf_tensor(name, shape, dt))

        def sem(name):
            return ctx.enter_context(nc.semaphore(name))

        PS = ctx.enter_context(nc.psum_tensor("PS", [P, 8, 512], F32))
        H = sb("H", [P, KD, T])
        X = sb("X", [P, KD, T])
        xs = sb("xs", [P, 2, KD, T], F16)
        stage = sb("stage", [P, 2, SLOT])
        wsp = sb("wsp", [P, 2, 2, SLOT], F16)
        big = sb("big", [P, (KF + 2) * T])
        hid = big[:, :].rearrange("p (m t) -> p m t", m=KF + 2)
        hid_s = big[:, :].bitcast(F16).rearrange("p (m s t) -> p m s t", m=KF + 2, s=2)
        tmp_a = sb("tmp_a", [P, 2, T])
        tmp_b = sb("tmp_b", [P, 2, T])
        std = sb("std", [P, T])
        rstd = sb("rstd", [P, T])
        cmax = sb("cmax", [P, 2])
        call = sb("call", [P, 2])
        cexp = sb("cexp", [P, 2], I32)
        cneg = sb("cneg", [P, 2], I32)
        wscale = sb("wscale", [P, 2])
        winv = sb("winv", [P, 2])
        oscale = sb("oscale", [P, 2])
        oscale_b = sb("oscale_b", [P, 2])
        bmax = sb("bmax", [P, 6])
        ball = sb("ball", [P, 6])
        bound = sb("bound", [P, 3])
        bexp = sb("bexp", [P, 3], I32)
        bneg = sb("bneg", [P, 3], I32)
        xscale = sb("xscale", [P, 3])
        xinv = sb("xinv", [P, N_XF])
        par_s = sb("par_s", [P, 48])
        hmax = sb("hmax", [P, KF])
        hm = sb("hm", [P, N_FOUND])
        hall = sb("hall", [P, N_FOUND])
        hexp = sb("hexp", [P, N_FOUND], I32)
        hneg = sb("hneg", [P, N_FOUND], I32)
        hscale = sb("hscale", [P, N_FOUND])
        hinv = sb("hinv", [P, N_FOUND])
        mmax = sb("mmax", [P, 1 + (NB + 1) * REP])
        ones = sb("ones", [P, P])
        ones_dv = sb("ones_dv", [P, P])
        eps = sb("eps", [P, 2])
        par = sb("par", [P, N_PAR])
        ident = sb("ident", [P, P])
        masks = sb("masks", [CH, N_DIR, CH])
        reset = sb("reset", [P, T])
        w2 = sb("w2", [N_DIR * RANK, N_DIR, PAIRS * P])
        rel = sb("rel", [P, S_MID + S_END])
        head = sb("head", [P, REP + HEADS])
        sinks = sb("sinks", [P, HEADS])
        qscale = sb("qscale", [P, REP])
        bias_m = sb("bias_m", [P, GROUPS, S_META])
        credit = sb("credit", [1, 6])

        arena = sb("arena", [P, 9616])
        pools = {"big": [big, 0, (KF + 2) * T], "arena": [arena, 0, 9616],
                 "X": [X[:, :, :].rearrange("p k t -> p (k t)"), 0, KD * T]}

        def part(pool, shape):
            buf, start, size = pools[pool]
            n = int(np.prod(shape[1:]))
            pools[pool][1] += n
            assert start + n <= size, (pool, start, n, size)
            ap = buf[0:shape[0], start:start + n]
            if len(shape) == 2:
                return ap
            names = "abcd"[:len(shape) - 1]
            return ap.rearrange(f"p ({' '.join(names)}) -> p {' '.join(names)}",
                                **{n: s for n, s in zip(names, shape[1:])})

        mix = part("big", [P, KD, T])
        gv = part("big", [CH, NCH, G_HEADS * DV])
        sg = part("big", [P, G_HEADS, T])
        kT = sb("kT", [P, KEYS])
        qT = part("arena", [P, REP, T])
        av = part("arena", [P, NB + 1, P])
        mark = pools["arena"][1]
        gqT = part("X", [P, PAIRS, T])
        gkT = part("X", [P, PAIRS, T])
        V = part("X", [P, PAIRS, N_DIR, T])
        B_end = part("arena", [P, PAIRS * N_DIR, NCH])
        E_end = part("arena", [P, PAIRS * N_DIR, NCH])
        decayed_0 = [part("arena", [P, N_DIR, T]) for _ in range(4)]
        decayed_1 = xs[:, :, :, :].rearrange("p a k t -> p (a k t)").bitcast(F32).rearrange("p (b d t) -> p b d t", b=4, d=N_DIR)
        q_in, k_in, q_ex, k_ex = [[decayed_0[b], decayed_1[:, b, :, :]] for b in range(4)]
        kxT = part("big", [CH, NCH, N_DIR * P])
        mark_big = pools["big"][1]
        zT = part("big", [N_DIR * RANK, T])
        pools["big"][1] = mark_big
        state = [part(pool, [P, N_DIR, NCH, DV]) for pool in ("arena", "big")]
        a_dir = part("arena", [CH, 2, N_DIR * 2 * CH])
        a_sum = part("arena", [CH, 2, 2 * CH])
        pools["arena"][1] = mark
        pools["X"][1] = 0
        PT = part("X", [P, GROUPS, 4, REP * BLOCK])
        rel_1 = part("arena", [P, S_MID + S_END])
        rels = (rel, rel_1)
        diag = part("arena", [P, 2, GROUPS, P])
        gO = mix[:, REP:KD, :]
        pools["X"][1] = 0
        o_squares, o_rms = [[part(pool, [P, 2, T]) for pool in ("X", "arena")] for _ in range(2)]
        scores = tmp_a[:, :, :].rearrange("p a t -> p (a t)")[:, 0:2 * 402]
        scores2 = tmp_b[:, :, :].rearrange("p a t -> p (a t)")[:, 0:2 * 402]
        N_UNIT = 1 + NB * REP
        smin = sb("smin", [P, 2 * N_UNIT])
        ssum = sb("ssum", [P, 2 * N_UNIT])
        srec = sb("srec", [P, 2 * N_UNIT])

        def score_buf(n):
            return (scores, scores2)[n // 2 % 2].rearrange("p (a t) -> p a t", a=2)[:, n % 2, :]

        x_loaded = [sem(f"x_loaded{i}") for i in range(2)]
        par_loaded = sem("par_loaded")
        const_loaded = sem("const_loaded")
        w_loaded = [sem(f"w_loaded{i}") for i in range(2)]
        ready0 = sem("ready0")
        x_summed = sem("x_summed")
        mean_ready = sem("mean_ready")
        centred = sem("centred")
        squared = sem("squared")
        sq_summed = sem("sq_summed")
        sq_total = sem("sq_total")
        delta_ready = sem("delta_ready")
        delta_out = sem("delta_out")
        var_ready = sem("var_ready")
        shifted0 = sem("shifted0")
        shifted = sem("shifted")
        std_ready = sem("std_ready")
        rstd_ready = sem("rstd_ready")
        normed = sem("normed")
        h_ready = sem("h_ready")
        gu_ready = sem("gu_ready")
        silu_ready = sem("silu_ready")
        w_max = sem("w_max")
        w_all = sem("w_all")
        w_scale = sem("w_scale")
        w_hi = sem("w_hi")
        w_ready = sem("w_ready")
        out_scale = sem("out_scale")
        out_scale_b = sem("out_scale_b")
        b_max = sem("b_max")
        b_all = sem("b_all")
        b_step = sem("b_step")
        h_max = sem("h_max")
        h_all = sem("h_all")
        h_step = sem("h_step")
        xf_done = sem("xf_done")
        hs_hi = sem("hs_hi")
        hs_ready = sem("hs_ready")
        x_hi = sem("x_hi")
        x_ready = sem("x_ready")
        m_max = sem("m_max")
        m_hi = sem("m_hi")
        m_ready = sem("m_ready")
        hid_done = sem("hid_done")
        res_ready = sem("res_ready")
        res_ready_b = sem("res_ready_b")
        res_a = sem("res_a")
        res_done = sem("res_done")
        proj_ready = sem("proj_ready")
        proj_done = sem("proj_done")
        gate_ready = sem("gate_ready")
        gate_abs = sem("gate_abs")
        gate_exp = sem("gate_exp")
        gate_ln = sem("gate_ln")
        gate_min = sem("gate_min")
        log_gate = sem("log_gate")
        scanned = sem("scanned")
        ends_done = sem("ends_done")
        decay_done = sem("decay_done")
        end_exp = sem("end_exp")
        rel_a = sem("rel_a")
        clamp_lo = sem("clamp_lo")
        clamped = sem("clamped")
        rel_b = sem("rel_b")
        dec_exp = sem("dec_exp")
        dec_dve = sem("dec_dve")
        dec_pool = sem("dec_pool")
        kx_ready = sem("kx_ready")
        kx_done = sem("kx_done")
        st_ready = sem("st_ready")
        st_done = sem("st_done")
        a_ready = sem("a_ready")
        a_masked = sem("a_masked")
        a_done = sem("a_done")
        o_ready = sem("o_ready")
        o_done = sem("o_done")
        o_sq = sem("o_sq")
        o_ssum = sem("o_ssum")
        o_std = sem("o_std")
        o_rstd = sem("o_rstd")
        o_gated = sem("o_gated")
        o_final = sem("o_final")
        sinks_done = sem("sinks_done")
        rel_copied = sem("rel_copied")
        sink_set = sem("sink_set")
        q_scale = sem("q_scale")
        bias_done = sem("bias_done")
        s_ready = sem("s_ready")
        s_max = sem("s_max")
        p_exp = sem("p_exp")
        p_rec = sem("p_rec")
        diag_done = sem("diag_done")
        pt_ready = sem("pt_ready")
        pt_out = sem("pt_out")
        att_ready = sem("att_ready")
        att_done = sem("att_done")
        out_done = sem("out_done")

        def halves(ap):
            return ap.rearrange("p (h c) -> p h c", h=2)

        def pair(bank, rows=P):
            return PS[0:rows, bank:bank + 2, 0:HALF]

        def w_view(slot, part, kt, cols):
            return wsp[:, slot, part, 0:kt * cols].rearrange("p (k n) -> p k n", k=kt)

        Z = N_DIR * RANK
        TILES = ([("z", 0, 0, 0)] + [("g", i, i // 2, (Z if i < 2 else 0) + P * (i % 2)) for i in range(G_HEADS)]
                 + [("gq", i, 2, P * i) for i in range(PAIRS)] + [("gk", i, 3, P * i) for i in range(PAIRS)]
                 + [("gv", i, 4 + i // NCH, 0) for i in range(2 * NCH)]
                 + [("aq", i, 6 + i // 2, P * (i % 2)) for i in range(REP)] + [("ak", 0, 8, 0), ("av", 0, 8, P)])
        LAST_QUERY = max(n for n, t in enumerate(TILES) if t[0] == "aq")
        LAST_OF = [max(n for n, t in enumerate(TILES) if t[2] == c) for c in range(N_IN)]
        GATES = [(j, d) for j in range(PAIRS) for d in range(N_DIR)]
        GATES_AFTER = {0: [0], 1: [1], 2: [2], 3: [3]}
        DECAYS_AT = {6: 0, 7: 1}
        UNITS = [(-1, 0)] + [(n, j) for n in range(NB) for j in range(REP)]

        def unit_keys(n):
            blocks = [0] if n < 0 else [b for b in (n - 1, n, n + 1) if 0 <= b < NB]
            lo, hi = SINK_COL + 1 + BLOCK * blocks[0], SINK_COL + 1 + BLOCK * (blocks[-1] + 1)
            runs = [(0, hi)] if blocks[0] == 0 else [(0, SINK_COL + 1), (lo, hi)]
            return runs, blocks

        def rel_start(n):
            return S_MID if n == 0 else 0

        def chunk(ap, c):
            return ap[..., CH * c:CH * (c + 1)]

        def unit_cols(u):
            return sum(hi - lo for lo, hi in unit_keys(UNITS[u][0])[0])

        def gate_col(q):
            j, d = GATES[q]
            return PAIRS * d + j

        x_sum, sq_sum = std, rstd
        delta, delta_sq = tmp_a[:, 0, :], tmp_a[:, 1, :]

        def centre_order(L):
            first = SHIFT_TILES[L] if L else 0
            return list(range(first, KD)) + list(range(first))

        def centre_count(L, k):
            return KD * L + centre_order(L).index(k) + 1

        def add_tile(vector, engine, L, n):
            if n > 1:
                engine.wait_ge(x_summed, SHIFT_SUMS[L] + n - 1)
            vector.tensor_tensor(x_sum[:, :], X[:, 0, :] if n == 1 else x_sum[:, :], X[:, n, :], ALU.add).then_inc(x_summed, 1)

        block = ctx.enter_context(nc.Block())

        @block.sync
        def _(sp):
            def load_gu(f, m, slot):
                sp.dma_start(stage[:, slot, 0:KD * P], gate[f][m]).then_inc(w_loaded[slot], 16)
                sp.dma_start(stage[:, slot, KD * P:GU_COLS], up[f][m]).then_inc(w_loaded[slot], 16)

            def load_halves(src, slot, cols):
                h = cols // 2
                sp.dma_start(stage[:, slot, 0:h], src[:, 0:h]).then_inc(w_loaded[slot], 16)
                sp.dma_start(stage[:, slot, h:cols], src[:, h:cols]).then_inc(w_loaded[slot], 16)

            for h in range(2):
                sp.dma_start(X[:, 4 * h:4 * h + 4, :],
                             xT[:, 4 * h * T:(4 * h + 4) * T].rearrange("p (k t) -> p k t", k=4)).then_inc(x_loaded[h], 16)
            for f in range(2):
                for m in range(2):
                    if f:
                        sp.wait_ge(w_ready, GU[f] + m - 1)
                    load_gu(f, m, (GU[f] + m) % 2)
                with sp.Fori(0, (N_GU - 2) // 2) as i:
                    for t in range(2):
                        sp.wait_ge(w_ready, GU[f] + 1 + t + 2 * i)
                        load_gu(f, 2 * i + 2 + t, (GU[f] + t) % 2)
                with sp.Fori(0, N_DN // 2) as i:
                    for t in range(2):
                        sp.wait_ge(w_ready, DN[f] - 1 + t + 2 * i)
                        load_halves(down[f][2 * i + t], (DN[f] + t) % 2, DN_COLS)
                if f == 0:
                    for n in range(N_IN):
                        sp.wait_ge(w_ready, IN0 + n - 1)
                        load_halves(w_in[n], (IN0 + n) % 2, KD * IN_COLS[n])
                    for n in range(N_OUT):
                        sp.wait_ge(w_ready, OUT0 + n - 1)
                        load_halves(w_out[n], (OUT0 + n) % 2, OUT_COLS)
            for k in range(KD):
                sp.wait_ge(h_ready, 3 * KD + k + 1)
                sp.dma_start(out[k], H[:, k, N_META:T]).then_inc(out_done, 16)
            sp.wait_ge(out_done, 16 * KD)

        @block.tensor
        def _(pe):
            def shift_mean(L):
                pe.wait_ge(x_summed, SHIFT_SUMS[L + 1])
                for h in range(2):
                    mm = nc.tensor.matmul(PS[:, 6 + h, 0:HALF], ones[:, :], x_sum[:, h * HALF:(h + 1) * HALF], start=True, stop=True)
                mm.then_inc(mean_ready, 1)

            def layer_norm(L):
                if L:
                    pe.wait_ge(res_done, 2 + KD * L - 1)
                for k in range(SHIFT_TILES[L], KD):
                    if k == KD - 1 and L:
                        squares(L, sq_sum[:, :], True)
                    if L:
                        pe.wait_ge(res_done, 2 + KD * (L - 1) + k + 1)
                    else:
                        pe.wait_ge(centred, k + 1)
                    for h in range(2):
                        mm = nc.tensor.matmul(PS[:, h, 0:HALF], ones[:, :], X[:, k, h * HALF:(h + 1) * HALF],
                                              start=k == SHIFT_TILES[L], stop=k == KD - 1)
                mm.then_inc(delta_ready, 1)
                if L == 0:
                    squares(L, sq_sum[:, :], True)
                pe.wait_ge(squared, KD * (L + 1))
                squares(L, tmp_b[:, 1, :], False).then_inc(sq_total, 1)

            def squares(L, src, first):
                if first:
                    pe.wait_ge(sq_summed, (KD - 2) * (L + 1))
                for h in range(2):
                    mm = nc.tensor.matmul(PS[:, 4 + h, 0:HALF], ones[:, :], src[:, h * HALF:(h + 1) * HALF],
                                          start=first, stop=not first)
                return mm

            def gu_tile(c, slot, m, s, f, first=False):
                pe.wait_ge(w_ready, c + 1)
                pe.wait_ge(hid_done, KF * f + m + 1)
                for g, k in [(g, k) for k in range(KD) for g in range(2)] if first else [(g, k) for g in range(2) for k in range(KD)]:
                    for wp, xp in PRODUCTS:
                        if first and g == 0 and wp == 0:
                            pe.wait_ge((x_hi, x_ready)[xp], 2 * KD * f + k + 1)
                        w = wsp[:, slot, wp, (g * KD + k) * P:(g * KD + k + 1) * P]
                        for h in range(2):
                            mm = nc.tensor.matmul(PS[:, 4 * s + 2 * g + h, 0:HALF], w, xs[:, xp, k, h * HALF:(h + 1) * HALF],
                                                  start=k == 0 and wp + xp == 0, stop=k == KD - 1 and xp == 1)
                mm.then_inc(gu_ready, 1)

            def res_tile(r, s, w, src, kt, k_sem=None, k0=0, norm=None, split_at=None, before_b=None):
                pe.wait_ge(res_done, r + 1)
                for k in range(kt):
                    if norm is not None and k == 5:
                        shift_mean(norm)
                    if k == split_at:
                        mm.then_inc(res_ready, 1)
                        if before_b is not None:
                            pe.wait_ge(*before_b)
                    if k_sem is not None:
                        pe.wait_ge(k_sem, k0 + k + 1)
                    b = split_at is not None and k >= split_at
                    for wp, xp in PRODUCTS:
                        for h in range(2):
                            mm = nc.tensor.matmul(PS[:, 4 * b + 2 * s + h, 0:HALF], w(wp, k), src(xp, k)[:, h * HALF:(h + 1) * HALF],
                                                  start=k in (0, split_at) and wp + xp == 0,
                                                  stop=k + 1 in (kt, split_at) and xp == 1)
                mm.then_inc(res_ready if split_at is None else res_ready_b, 1)

            def ffn(f):
                for m in range(2):
                    gu_tile(GU[f] + m, (GU[f] + m) % 2, m, m, f, first=m == 0)
                with pe.Fori(0, (N_GU - 2) // 2) as i:
                    for t in range(2):
                        gu_tile(GU[f] + 2 + t + 2 * i, (GU[f] + t) % 2, 2 * i + 2 + t, t, f)

                def down_tile(c, slot, r, s, first=False, norm=None, before_b=None):
                    pe.wait_ge(w_ready, c + 1)
                    res_tile(r, s, lambda p, k: wsp[:, slot, p, k * P:(k + 1) * P], lambda p, k: hid_s[:, k, p, :], KF,
                             hs_ready if first else None, KF * f, norm, KF_A, before_b)

                pe.wait_ge(hid_done, 2 + KF * (f + 1) - 1)
                for q in range(2):
                    down_tile(DN[f] + q, (DN[f] + q) % 2, 2 * KD * f + q, q, first=q == 0,
                              before_b=(hid_done, 2 + KF * (f + 1)))
                with pe.Fori(0, (N_DN - 4) // 2) as i:
                    for t in range(2):
                        down_tile(DN[f] + 2 + t + 2 * i, (DN[f] + t) % 2, 2 * KD * f + 2 + t + 2 * i, t)
                L = 2 * f + 1
                for q in (N_DN - 2, N_DN - 1):
                    down_tile(DN[f] + q, (DN[f] + q) % 2, 2 * KD * f + q, q % 2, norm=L if q == SHIFT_TILES[L] else None,
                              before_b=(centred, KD * (L + 1)) if q == SHIFT_TILES[L] + 1 else None)

            def first_proj_tiles():
                pe.wait_ge(w_ready, IN0 + 1)
                for k in range(KD):
                    for n in range(2):
                        kind, _, c, col = TILES[n]
                        m = Z if kind == "z" else P
                        for wp, xp in PRODUCTS:
                            if n == 0 and wp == 0:
                                pe.wait_ge((x_hi, x_ready)[xp], KD + k + 1)
                            w = w_view(IN0 % 2, wp, KD, IN_COLS[c])[:, k, col:col + m]
                            for h in range(2):
                                mm = nc.tensor.matmul(PS[0:m, 2 * n + h, 0:HALF], w, xs[:, xp, k, h * HALF:(h + 1) * HALF],
                                                      start=k == 0 and wp + xp == 0, stop=k == KD - 1 and xp == 1)
                        if k == KD - 1:
                            mm.then_inc(proj_ready, 1)

            def proj_tile(n):
                kind, i, c, col = TILES[n]
                ci = IN0 + c
                pe.wait_ge(w_ready, ci + 1)
                bank = 2 * (n % 2)
                pe.wait_ge(proj_done, n + 1)

                def products(dst, cols, lhs_is_x, h=None):
                    for k in range(KD):
                        for wp, xp in PRODUCTS:
                            w = w_view(ci % 2, wp, KD, IN_COLS[c])[:, k, col:col + cols[0]]
                            x = xs[:, xp, k, cols[1]:cols[2]]
                            mm = nc.tensor.matmul(dst, x if lhs_is_x else w, w if lhs_is_x else x,
                                                  start=k == 0 and wp + xp == 0, stop=k == KD - 1 and xp == 1)
                    return mm

                if kind == "gv":
                    mm = products(PS[0:CH, bank, 0:2 * P], (2 * P, CH * (i % NCH), CH * (i % NCH + 1)), True)
                elif kind == "av":
                    for t in range(NB + 1):
                        rows = N_META if t == 0 else BLOCK
                        lo = 0 if t == 0 else N_META + BLOCK * (t - 1)
                        dst = PS[0:rows, bank + 1, 0:P] if t == 0 else PS[:, bank, P * (t - 1):P * t]
                        mm = products(dst, (P, lo, lo + rows), True)
                else:
                    m = Z if kind == "z" else P
                    for h in range(2):
                        mm = products(PS[0:m, bank + h, 0:HALF], (m, h * HALF, (h + 1) * HALF), False)
                mm.then_inc(proj_ready, 1)

            def gates(q):
                j, d = GATES[q]
                if q == 0:
                    pe.wait_ge(const_loaded, 16 * N_CONST)
                    pe.wait_ge(proj_done, 2 + 1)
                if q >= 2:
                    pe.wait_ge(gate_abs, q - 1)
                    pe.wait_ge(gate_min, q - 1)
                for h in range(2):
                    mm = nc.tensor.matmul(PS[:, 4 + 2 * (q % 2) + h, 0:HALF], w2[:, d, j * P:(j + 1) * P],
                                          zT[:, h * HALF:(h + 1) * HALF], start=True, stop=True)
                mm.then_inc(gate_ready, 1)

            def gla_keys(j, n):
                i = j * (NCH // 2) + n
                if n == 0:
                    pe.wait_ge(dec_pool, 2 * N_DIR * (j + 1))
                    if j:
                        pe.wait_ge(st_done, 2 * (NCH - 1))
                    else:
                        pe.wait_ge(gate_abs, len(GATES))
                        pe.wait_ge(gate_min, len(GATES))
                if i >= 2:
                    pe.wait_ge(kx_done, i - 1)
                for s in range(2):
                    for d in range(N_DIR):
                        mm = nc.tensor.transpose(PS[0:CH, 6 + i % 2, (2 * s + d) * P:(2 * s + d + 1) * P],
                                                 chunk(k_ex[j][:, d, :], 2 * n + s), ident[:, :])
                mm.then_inc(kx_ready, 1)

            def gla_states(j, s):
                n = j * (NCH - 1) + s
                if s == 0:
                    pe.wait_ge(kx_done, (NCH // 2) * (j + 1))
                if n >= 2:
                    pe.wait_ge(st_done, 2 * (n - 1))
                for d in range(N_DIR):
                    c = s if d == 0 else NCH - 1 - s
                    for a in range(2):
                        mm = nc.tensor.matmul(PS[DK * a:DK * (a + 1), 6 + n % 2, d * P:(d + 1) * P],
                                              kxT[:, c, d * P + DK * a:d * P + DK * (a + 1)],
                                              gv[:, c, (2 * j + a) * DV:(2 * j + a + 1) * DV], start=True, stop=True)
                mm.then_inc(st_ready, 1)

            def a_scores(j, c):
                n = j * NCH + c
                if n >= 2:
                    pe.wait_ge(a_masked, n - 1)
                elif n == 0:
                    pe.wait_ge(proj_done, 2 + len(TILES))
                if c == 0:
                    pe.wait_ge(dec_dve, 2 * N_DIR * (j + 1))
                for d in range(N_DIR):
                    for a in range(2):
                        rows = slice(DK * a, DK * (a + 1))
                        mm = nc.tensor.matmul(PS[0:CH, 2 * (n % 2) + a, d * CH:(d + 1) * CH],
                                              chunk(k_in[j][rows, d, :], c), chunk(q_in[j][rows, d, :], c),
                                              start=True, stop=True)
                mm.then_inc(a_ready, 1)

            def outputs(j, c):
                n = j * NCH + c
                pe.wait_ge(a_done, n + 1)
                if n:
                    pe.wait_ge(o_done, n)
                if c == 0:
                    pe.wait_ge(st_done, 2 * (NCH - 1) * (j + 1))
                for a in range(2):
                    rows = slice(DK * a, DK * (a + 1))
                    dst = PS[:, 4 + a, 0:CH]
                    dirs = [d for d in range(N_DIR) if (c > 0 if d == 0 else c < NCH - 1)]
                    nc.tensor.matmul(dst, gv[:, c, (2 * j + a) * DV:(2 * j + a + 1) * DV],
                                     a_sum[:, n % 2, a * CH:(a + 1) * CH], start=True, stop=False)
                    for d in dirs:
                        step = c if d == 0 else NCH - 1 - c
                        mm = nc.tensor.matmul(dst, state[j][rows, d, step, :], chunk(q_ex[j][rows, d, :], c),
                                              start=False, stop=d == dirs[-1])
                mm.then_inc(o_ready, 1)

            def gla():
                beside = {2: [(gla_keys, 0), (gla_keys, 1)], 3: [(gla_keys, 2)], 4: [(gla_states, 0)], 5: [(gla_states, 1)]}
                a_scores(0, 0)
                for c in range(NCH):
                    if c + 1 < NCH:
                        a_scores(0, c + 1)
                    for work, n in beside.get(c, []):
                        work(1, n)
                    outputs(0, c)
                gla_states(1, 2)
                a_scores(1, 0)
                gla_states(1, 3)
                a_scores(1, 1)
                gla_states(1, 4)
                for c in range(NCH):
                    if 1 <= c < NCH - 1:
                        a_scores(1, c + 1)
                    if c in NORM_SUMS:
                        norm_sums(NORM_SUMS.index(c))
                    outputs(1, c)

            def norm_sums(h):
                j, a = divmod(h, 2)
                pe.wait_ge(o_sq, h + 1)
                if h == 0:
                    pe.wait_ge(st_done, 2 * PAIRS * (NCH - 1))
                elif h == 1:
                    pe.wait_ge(o_std, 1)
                elif h == 2:
                    pe.wait_ge(o_done, PAIRS * NCH)
                else:
                    pe.wait_ge(o_std, 2)
                bank = 4 + 2 * (a if j else 1)
                for x in range(2):
                    mm = nc.tensor.matmul(PS[:, bank + x, 0:HALF], ones_dv[:, :],
                                          o_squares[j][:, a, x * HALF:(x + 1) * HALF], start=True, stop=True)
                mm.then_inc(o_ssum, 1)

            def att_scores(u):
                n, j = UNITS[u]
                runs, _ = unit_keys(n)
                if u < 2:
                    pe.wait_ge(a_masked, PAIRS * NCH)
                else:
                    pe.wait_ge(s_max, 2 * (u - 1))
                for g in range(GROUPS):
                    rows = slice(DH * g, DH * (g + 1))
                    if n < 0:
                        for r in range(REP):
                            mm = nc.tensor.matmul(PS[MROW * r:MROW * (r + 1), 2 * (u % 2) + g, 0:S_META], qT[rows, r, 0:MROW],
                                                  kT[rows, 0:S_META], start=True, stop=True, tile_position=(DH * g, MROW * r))
                    else:
                        q = qT[rows, j, N_META + BLOCK * n:N_META + BLOCK * (n + 1)]
                        dst = PS[:, 2 * (u % 2) + g, :]
                        col = 0
                        for lo, hi in runs:
                            mm = nc.tensor.matmul(dst[:, col:col + hi - lo], q, kT[rows, lo:hi], start=True, stop=True)
                            col += hi - lo
                mm.then_inc(s_ready, 1)

            def att_transposes(u):
                n, j = UNITS[u]
                _, blocks = unit_keys(n)
                if u == 0:
                    pe.wait_ge(o_std, G_HEADS)
                else:
                    pe.wait_ge(pt_out, 2 * u)
                for g in range(GROUPS):
                    pe.wait_ge(diag_done, 2 * u + g + 1)
                    p = score_buf(2 * u + g)
                    for i, lo in enumerate([0] + [SINK_COL + 1 + BLOCK * b for b in range(len(blocks))]):
                        mm = nc.tensor.matmul(PS[:, 4 + g, i * P:(i + 1) * P], p[:, lo:lo + P], diag[:, u % 2, g, :],
                                              start=True, stop=True)
                    mm.then_inc(pt_ready, 1)

            def att_values(n):
                _, blocks = unit_keys(n)
                u = 0 if n < 0 else REP * (n + 1)
                pe.wait_ge(pt_out, 2 * u + 2)
                cols = P if n < 0 else REP * BLOCK
                if n >= 1:
                    pe.wait_ge(att_done, n)
                for g in range(GROUPS):
                    dst = PS[DH * g:DH * (g + 1), 6 + (n + 1) % 2, 0:cols]
                    c = slice(DH * g, DH * (g + 1))
                    nc.tensor.matmul(dst, av[0:N_META, 0, c], PT[0:N_META, g, 0, 0:cols], start=True, stop=False)
                    for i, b in enumerate(blocks):
                        mm = nc.tensor.matmul(dst, av[:, 1 + b, c], PT[:, g, i + 1, 0:cols],
                                              start=False, stop=i == len(blocks) - 1)
                mm.then_inc(att_ready, 1)

            for s in (hid_done, res_done, proj_done):
                pe.wait_ge(s, 2)
            pe.wait_ge(ready0, 5)
            shift_mean(0)
            layer_norm(0)
            ffn(0)
            layer_norm(1)
            first_proj_tiles()
            for n in range(2, len(TILES)):
                proj_tile(n)
                if n in LAST_OF:
                    for q in GATES_AFTER.get(LAST_OF.index(n), []):
                        gates(q)
                if n == LAST_QUERY:
                    for i in range(NCH // 2):
                        gla_keys(0, i)
                elif n > LAST_QUERY:
                    for i in range(2) if n == LAST_QUERY + 1 else range(2, NCH - 1):
                        gla_states(0, i)
            gla()
            norm_sums(2)
            norm_sums(3)
            att_scores(0)
            att_scores(1)
            for u in range(len(UNITS)):
                att_transposes(u)
                if u + 2 < len(UNITS):
                    att_scores(u + 2)
                if u == 0 or UNITS[u][1] == REP - 1:
                    att_values(UNITS[u][0])
            for n in range(KD):
                c = OUT0 + n // 2
                pe.wait_ge(w_ready, c + 1)
                res_tile(KD + n, n % 2, lambda p, k: w_view(c % 2, p, KD, 2 * P)[:, k, P * (n % 2):P * (n % 2 + 1)],
                         lambda p, k: xs[:, p, k, :], KD, m_ready if n == 0 else None, norm=2 if n == SHIFT_TILES[2] else None)
            layer_norm(2)
            ffn(1)
            layer_norm(3)

        @block.scalar
        def _(act):
            act.dma_start(par[:, :], params).then_inc(par_loaded, 16)

            def square(L, k):
                if L and k >= SHIFT_TILES[L]:
                    act.wait_ge(res_done, 2 + KD * (L - 1) + k + 1)
                else:
                    act.wait_ge(centred, centre_count(L, k))
                if k >= 2:
                    act.wait_ge(sq_summed, (KD - 2) * L + max(1, k - 2))
                nc.scalar.activation(tmp_b[:, k % 2, :], X[:, k, :], ACT.Square).then_inc(squared, 1)

            def layer_norm(L, chunk=None):
                if L == 0:
                    act.wait_ge(par_loaded, 16)
                    act.wait_ge(ready0, 5)
                act.wait_ge(delta_ready, L + 1)
                nc.scalar.activation(halves(delta), pair(0), ACT.Copy).then_inc(delta_out, 1)
                nc.scalar.activation(halves(delta_sq), pair(0), ACT.Square).then_inc(delta_out, 1)
                act.wait_ge(var_ready, L + 1)
                e = min(L, 1)
                nc.scalar.activation(std[:, :], std[:, :], ACT.Sqrt, bias=eps[:, e:e + 1]).then_inc(std_ready, 1)
                if chunk is not None:
                    split_hi(*chunk)
                for k in range(KD):
                    act.wait_ge(normed, KD * L + k + 1)
                    if L < 3:
                        if L == 0 and k == 0:
                            act.wait_ge(b_step, B_STEPS)
                        nc.scalar.activation(xs[:, 0, k, :], X[:, k, :], ACT.Identity, scale=par_s[:, C_G[L] + k:C_G[L] + k + 1],
                                             bias=par_s[:, C_B[L] + k:C_B[L] + k + 1]).then_inc(x_hi, 1)
                    nc.scalar.activation(H[:, k, :], X[:, k, :], ACT.Identity, scale=par[:, C_G[L] + k:C_G[L] + k + 1],
                                         bias=par[:, C_B[L] + k:C_B[L] + k + 1]).then_inc(h_ready, 1)

            def split_hi(c, slot, cols):
                act.wait_ge(w_scale, 4 * c + 3)
                nc.scalar.activation(wsp[:, slot, 0, 0:cols], stage[:, slot, 0:cols], ACT.Copy,
                                     scale=wscale[:, slot:slot + 1]).then_inc(w_hi, 1)

            def silu_tile(c, slot, m, s, f):
                act.wait_ge(gu_ready, KF * f + m + 1)
                act.wait_ge(out_scale, c + 1)
                nc.scalar.activation(halves(tmp_a[:, s, :]), pair(4 * s), ACT.Silu,
                                     scale=oscale[:, slot:slot + 1]).then_inc(silu_ready, 1)

            def ffn(f):
                for m in range(2):
                    c = GU[f] + m
                    if m:
                        split_hi(c + 1, (c + 1) % 2, GU_COLS)
                    silu_tile(c, c % 2, m, m, f)
                with act.Fori(0, (N_GU - 6) // 2) as i:
                    for t in range(2):
                        c, slot = GU[f] + 2 + t + 2 * i, (GU[f] + t) % 2
                        split_hi(c + 1, 1 - slot, GU_COLS)
                        silu_tile(c, slot, 2 * i + 2 + t, t, f)
                def hidden_hi(first, last):
                    for m in range(first, last):
                        i = HID[f] if m < KF_A else HID_B[f]
                        if m in (0, KF_A):
                            act.wait_ge(h_step, 4 * i + 3)
                            act.wait_ge(hid_done, 2 + KF * f + (KF_A if m == 0 else KF))
                        if m >= 2:
                            act.wait_ge(hs_ready, KF * f + m - 1)
                        nc.scalar.activation(hid_s[:, m, 0, :], hid[:, m + 2, :], ACT.Copy,
                                             scale=hscale[:, i:i + 1]).then_inc(hs_hi, 1)

                c = GU[f] + KF - 4
                split_hi(c + 1, (c + 1) % 2, GU_COLS)
                silu_tile(c, c % 2, KF - 4, 0, f)
                split_hi(c + 2, c % 2, GU_COLS)
                hidden_hi(0, HI_STEPS[0])
                silu_tile(c + 1, (c + 1) % 2, KF - 3, 1, f)
                split_hi(c + 3, (c + 1) % 2, GU_COLS)
                hidden_hi(HI_STEPS[0], HI_STEPS[1])
                silu_tile(c + 2, c % 2, KF - 2, 0, f)
                split_hi(c + 4, c % 2, DN_COLS)
                hidden_hi(HI_STEPS[1], HI_STEPS[2])
                silu_tile(c + 3, (c + 1) % 2, KF - 1, 1, f)
                hidden_hi(HI_STEPS[2], HI_STEPS[3])
                split_hi(c + 5, (c + 1) % 2, DN_COLS)
                hidden_hi(HI_STEPS[3], KF)
                L = 2 * f + 1
                for q in range(N_DN):
                    c = DN[f] + q + 1
                    if 0 < q < N_DN - 1 or q and f == 0:
                        act.wait_ge(res_ready_b, KD * f + q)
                        split_hi(c, c % 2, DN_COLS if q < N_DN - 1 else KD * IN_COLS[0])
                    if q >= SHIFT_TILES[L]:
                        for k in range(0 if q == SHIFT_TILES[L] else q, q + 1):
                            square(L, k)

            def proj_out(n):
                kind, i, c, _ = TILES[n]
                bank = 2 * (n % 2)
                slot = (IN0 + c) % 2
                back = oscale[:, slot:slot + 1]

                def out(dst, src, func=ACT.Copy):
                    return nc.scalar.activation(dst, src, func, scale=back[0:src.shape[0]])

                act.wait_ge(proj_ready, n + 1)
                act.wait_ge(out_scale, IN0 + c + 1)
                if kind == "z":
                    last = out(halves(zT), pair(bank, Z))
                elif kind == "g":
                    last = out(halves(sg[:, i, :]), pair(bank), ACT.Silu)
                elif kind == "gv":
                    last = out(gv[:, i % NCH, 2 * P * (i // NCH):2 * P * (i // NCH + 1)], PS[0:CH, bank, 0:2 * P])
                elif kind == "aq":
                    act.wait_ge(q_scale, i + 1)
                    out(qT[:, i, 0:N_META], PS[:, bank, 0:N_META])
                    back = qscale[:, i:i + 1]
                    out(qT[:, i, N_META:HALF], PS[:, bank, N_META:HALF])
                    last = out(qT[:, i, HALF:T], PS[:, bank + 1, 0:HALF])
                elif kind == "ak":
                    out(kT[:, 0:N_META], PS[:, bank, 0:N_META])
                    out(kT[:, N_META + 1:HALF + 1], PS[:, bank, N_META:HALF])
                    last = out(kT[:, HALF + 1:KEYS], PS[:, bank + 1, 0:HALF])
                elif kind == "av":
                    out(av[:, 1:NB + 1, :], PS[:, bank, :].rearrange("p (t n) -> p t n", n=P))
                    last = out(av[0:N_META, 0, :], PS[0:N_META, bank + 1, 0:P])
                else:
                    last = out(halves({"gq": gqT, "gk": gkT}[kind][:, i, :]), pair(bank))
                last.then_inc(proj_done, 1)

            def gates(q):
                act.wait_ge(gate_ready, q + 1)
                if q >= 2:
                    act.wait_ge(log_gate, q - 1)
                ln = tmp_a[:, q % 2, :]
                nc.scalar.activation(halves(ln), pair(4 + 2 * (q % 2)), ACT.Abs,
                                     bias=par[:, C_GATE + gate_col(q):C_GATE + gate_col(q) + 1]).then_inc(gate_abs, 1)
                act.wait_ge(gate_abs, q + 1)
                nc.scalar.activation(ln, ln, ACT.Exp, scale=-1.0).then_inc(gate_exp, 1)
                act.wait_ge(gate_exp, q + 1)
                nc.scalar.activation(ln, ln, ACT.Ln, bias=1.0).then_inc(gate_ln, 1)

            def decays(j, dirs=range(N_DIR)):
                for d in dirs:
                    q = N_DIR * j + d
                    sign = 1.0 if d == 0 else -1.0
                    act.wait_ge(ends_done, q + 1)
                    nc.scalar.activation(E_end[:, q, :], B_end[:, q, :], ACT.Exp, scale=1.0 / TAU).then_inc(end_exp, 1)
                    act.wait_ge(clamped, q + 1)
                    nc.scalar.activation(q_in[j][:, d, :], tmp_a[:, d, :], ACT.Exp, scale=sign / TAU).then_inc(dec_exp, 1)
                    nc.scalar.activation(k_in[j][:, d, :], tmp_a[:, d, :], ACT.Exp, scale=-sign / TAU).then_inc(dec_exp, 1)
                    act.wait_ge(rel_b, q + 1)
                    from_start, to_end = V[:, j, d, :], tmp_b[:, d, :]
                    ex_q, ex_k = (from_start, to_end) if d == 0 else (to_end, from_start)
                    nc.scalar.activation(q_ex[j][:, d, :], ex_q, ACT.Exp, scale=1.0 / TAU).then_inc(dec_exp, 1)
                    nc.scalar.activation(k_ex[j][:, d, :], ex_k, ACT.Exp, scale=1.0 / TAU).then_inc(dec_exp, 1)

            def keys_out(j, cc):
                n = j * (NCH // 2) + cc
                act.wait_ge(kx_ready, n + 1)
                if cc == 0 and j:
                    act.wait_ge(st_ready, NCH - 1)
                nc.scalar.activation(kxT[:, 2 * cc:2 * cc + 2, :],
                                     PS[0:CH, 6 + n % 2, :].rearrange("p (s n) -> p s n", s=2), ACT.Copy).then_inc(kx_done, 1)

            def outputs_out(j, c):
                n = j * NCH + c
                act.wait_ge(o_ready, n + 1)
                nc.scalar.activation(chunk(gO[:, 2 * j:2 * j + 2, :], c), PS[:, 4:6, 0:CH], ACT.Copy).then_inc(o_done, 1)

            def gla():
                decays(1, [0])
                outputs_out(0, 0)
                decays(1, [1])
                outputs_out(0, 1)
                keys_out(1, 0)
                keys_out(1, 1)
                outputs_out(0, 2)
                keys_out(1, 2)
                for c in range(3, NCH):
                    outputs_out(0, c)
                act.wait_ge(dec_dve, 2 * N_DIR * PAIRS)
                act.wait_ge(dec_pool, 2 * N_DIR * PAIRS)
                norm_squares(0)
                for c in range(NCH):
                    if c in NORM_SUMS:
                        norm_root(NORM_SUMS.index(c))
                    outputs_out(1, c)
                norm_squares(1)
                norm_root(2)
                norm_root(3)

            def norm_squares(j):
                act.wait_ge(o_done, NCH * (j + 1))
                for a in range(2):
                    nc.scalar.activation(o_squares[j][:, a, :], gO[:, 2 * j + a, :], ACT.Square).then_inc(o_sq, 1)

            def norm_root(h):
                j, a = divmod(h, 2)
                act.wait_ge(o_ssum, h + 1)
                nc.scalar.activation(halves(o_rms[j][:, a, :]), pair(4 + 2 * (a if j else 1)), ACT.Sqrt,
                                     bias=eps[:, 0:1]).then_inc(o_std, 1)

            def att_exp(u):
                cols = unit_cols(u)
                for g in range(GROUPS):
                    i = 2 * u + g
                    act.wait_ge(s_max, i + 1)
                    p = score_buf(i)[:, 0:cols]
                    nc.scalar.activation(p, p, ACT.Exp, scale=-1.0, bias=smin[:, i:i + 1],
                                         accum_out=ssum[:, i:i + 1]).then_inc(p_exp, 1)

            def att_copy(u):
                n, j = UNITS[u]
                k = len(unit_keys(n)[1]) + 1
                if n >= 0:
                    act.wait_ge(att_ready, n + 1)
                if n < 0:
                    act.wait_ge(o_final, 2)
                for g in range(GROUPS):
                    act.wait_ge(pt_ready, 2 * u + g + 1)
                    nc.scalar.activation(PT[:, g, 0:k, j * P:(j + 1) * P],
                                         PS[:, 4 + g, 0:k * P].rearrange("p (k n) -> p k n", n=P), ACT.Copy).then_inc(pt_out, 1)

            for k in range(KD):
                square(0, k)
                if k == 5:
                    split_hi(0, 0, GU_COLS)
            layer_norm(0, (GU[0] + 1, 1, GU_COLS))
            act.dma_start(ident[:, :], ident_in).then_inc(const_loaded, 16)
            act.dma_start(masks[:, :, :], masks_in).then_inc(const_loaded, 16)
            act.dma_start(reset[:, :], reset_in).then_inc(const_loaded, 16)
            act.dma_start(w2[:, :, :], w2_in).then_inc(const_loaded, 16)
            act.dma_start(rel[:, :], rel_in).then_inc(const_loaded, 16)
            act.dma_start(head[:, :], head_in).then_inc(const_loaded, 16)
            act.dma_start(bias_m[:, :, :], bias_meta).then_inc(const_loaded, 16)
            ffn(0)
            layer_norm(1, (IN0 + 1, (IN0 + 1) % 2, KD * 2 * P))
            for n in range(len(TILES)):
                if n - 1 in LAST_OF:
                    c = IN0 + TILES[n][2] + 1
                    split_hi(c, c % 2, KD * 2 * P)
                    for q in GATES_AFTER.get(TILES[n][2] - 1, []):
                        gates(q)
                    if TILES[n][2] in DECAYS_AT:
                        decays(0, [DECAYS_AT[TILES[n][2]]])
                proj_out(n)
                if n == LAST_QUERY:
                    for i in range(NCH // 2):
                        keys_out(0, i)
            gla()
            att_exp(0)
            att_exp(1)
            for u in range(len(UNITS)):
                att_copy(u)
                if u + 2 < len(UNITS):
                    att_exp(u + 2)
            for k in range(KD):
                act.wait_ge(h_step, 4 * MIX + 3)
                nc.scalar.activation(xs[:, 0, k, :], mix[:, k, :], ACT.Copy, scale=hscale[:, MIX:MIX + 1]).then_inc(m_hi, 1)
            for n in range(N_OUT):
                c = OUT0 + n + 1
                if n:
                    act.wait_ge(res_ready, KD + 2 * n)
                split_hi(c, c % 2, OUT_COLS if n < N_OUT - 1 else GU_COLS)
                if 2 * n >= SHIFT_TILES[2]:
                    for k in range(0 if 2 * n == SHIFT_TILES[2] else 2 * n, 2 * n + 2):
                        square(2, k)
            layer_norm(2, (GU[1] + 1, (GU[1] + 1) % 2, GU_COLS))
            ffn(1)
            layer_norm(3)

        @block.vector
        def _(dve):
            def centre(L, tiles=None):
                dve.wait_ge(mean_ready, L + 1)
                for k in centre_order(L) if tiles is None else tiles:
                    x = halves((X if L == 0 or k < SHIFT_TILES[L] else H)[:, k, :])
                    nc.vector.scalar_tensor_tensor(x, pair(6), -float(KD) / SHIFT_TILES[L], x, ALU.mult, ALU.add).then_inc(centred, 1)

            def layer_norm(L, chunk=None):
                dve.wait_ge(delta_out, 2 * L + 2)
                dve.wait_ge(sq_total, L + 1)
                nc.vector.tensor_tensor(halves(std[:, :]), pair(4), halves(delta_sq), ALU.subtract).then_inc(var_ready, 1)
                nc.vector.tensor_tensor(X[:, 0, :], X[:, 0, :], delta, ALU.subtract).then_inc(shifted0, 1)
                if chunk is not None:
                    chunk_scale(*chunk)
                dve.wait_ge(std_ready, L + 1)
                nc.vector.reciprocal(rstd[:, :], std[:, :]).then_inc(rstd_ready, 1)
                dve.wait_ge(rstd_ready, L + 1)

                def split_lo(k):
                    dve.wait_ge(h_ready, KD * L + k + 1)
                    nc.vector.scalar_tensor_tensor(xs[:, 1, k, :], H[:, k, :], xscale[:, L:L + 1], xs[:, 0, k, :],
                                                   ALU.mult, ALU.subtract).then_inc(x_ready, 1)

                for k in range(KD):
                    if k == 0:
                        dve.wait_ge(shifted0, L + 1)
                    else:
                        dve.wait_ge(shifted, (KD - 1) * L + k)
                    nc.vector.tensor_tensor(X[:, k, :], X[:, k, :], rstd[:, :], ALU.mult).then_inc(normed, 1)
                    if k >= 2 and L < 3:
                        split_lo(k - 2)
                if L < 3:
                    split_lo(KD - 2)
                    split_lo(KD - 1)

            def scale_of(largest, e, neg, scale, inv, signal, at):
                nc.vector.tensor_scalar(e, largest.bitcast(I32), EXP_MASK, None, ALU.bitwise_and).then_inc(signal, 1)
                dve.wait_ge(signal, at + 1)
                nc.vector.tensor_scalar(neg, e, (EXP_TOP + 1) * EXP_ONE, -1.0, ALU.max, ALU.mult).then_inc(signal, 1)
                dve.wait_ge(signal, at + 2)
                nc.vector.tensor_scalar(scale.bitcast(I32), neg, (2 * 127 + EXP_TOP) * EXP_ONE, None, ALU.add).then_inc(signal, 1)
                nc.vector.tensor_scalar(inv.bitcast(I32), neg, -1.0, -EXP_TOP * EXP_ONE, ALU.mult, ALU.add).then_inc(signal, 1)

            def hidden_max(m):
                nc.vector.tensor_reduce(hmax[:, :].unsqueeze(2)[:, m, :], hid[:, m + 2, :], AX.X, ALU.max,
                                        apply_absolute_value=True).then_inc(h_max, 1)

            def chunk_max(c, slot, half_c, cols, tile=None, tile_at=0):
                one = slice(slot, slot + 1)
                if tile is not None:
                    dve.wait_ge(hid_done, 2 + tile_at + tile + 1)
                dve.wait_ge(w_loaded[slot], 32 * half_c + 32)
                nc.vector.tensor_reduce(cmax[:, one], stage[:, slot, 0:cols], AX.X, ALU.max,
                                        apply_absolute_value=True).then_inc(w_max, 1)
                if tile is not None:
                    hidden_max(tile)

            def split(c, slot, cols, xf=None, used=None):
                chunk_scale(c, slot, xf, used)
                chunk_lo(c, slot, cols)

            def chunk_scale(c, slot, xf=None, used=None):
                one = slice(slot, slot + 1)
                dve.wait_ge(w_all, c + 1)
                scale_of(call[:, one], cexp[:, one], cneg[:, one], wscale[:, one], winv[:, one], w_scale, 4 * c)
                if used is not None:
                    dve.wait_ge(proj_done, used)
                if xf is not None:
                    out_scale_of(c, slot, xf)

            def chunk_lo(c, slot, cols):
                one = slice(slot, slot + 1)
                dve.wait_ge(w_hi, c + 1)
                nc.vector.scalar_tensor_tensor(wsp[:, slot, 1, 0:cols], stage[:, slot, 0:cols], wscale[:, one],
                                               wsp[:, slot, 0, 0:cols], ALU.mult, ALU.subtract).then_inc(w_ready, 1)

            def out_scale_of(c, slot, xf):
                dve.wait_ge(w_scale, 4 * c + 4)
                nc.vector.tensor_tensor(oscale[:, slot:slot + 1], winv[:, slot:slot + 1], xinv[:, xf:xf + 1],
                                        ALU.mult).then_inc(out_scale, 1)

            def hidden_tile(m, slot, s, f):
                dve.wait_ge(silu_ready, KF * f + m + 1)
                nc.vector.scalar_tensor_tensor(halves(hid[:, m + 2, :]), pair(4 * s + 2), oscale[:, slot:slot + 1],
                                               halves(tmp_a[:, s, :]), ALU.mult, ALU.mult).then_inc(hid_done, 1)

            def residual_tile(n, s, r, slot, r_b=None):
                dve.wait_ge(res_ready, r + 1)
                sum_a = nc.vector.scalar_tensor_tensor(halves(X[:, n, :]), pair(2 * s), oscale[:, slot:slot + 1], halves(H[:, n, :]),
                                                       ALU.mult, ALU.add)
                if r_b is None:
                    sum_a.then_inc(res_done, 1)
                else:
                    sum_a.then_inc(res_a, 1)
                    dve.wait_ge(res_a, r_b + 1)
                    dve.wait_ge(res_ready_b, r_b + 1)
                    nc.vector.scalar_tensor_tensor(halves(X[:, n, :]), pair(4 + 2 * s), oscale_b[:, slot:slot + 1],
                                                   halves(X[:, n, :]), ALU.mult, ALU.add).then_inc(res_done, 1)

            def back_scale(i, share):
                one = slice(i, i + 1)
                dve.wait_ge(h_all, i + 1)
                scale_of(hall[:, one], hexp[:, one], hneg[:, one], hscale[:, one], hinv[:, one], h_step, 4 * i)
                dve.wait_ge(h_step, 4 * i + 4)
                nc.vector.tensor_scalar(xinv[:, XF_FOUND + i:XF_FOUND + i + 1], hinv[:, one], share, None, ALU.mult).then_inc(xf_done, 1)

            def ffn(f):
                def step(m):
                    c = GU[f] + m
                    last = m == KF - 1
                    cols = DN_COLS if last else GU_COLS
                    if m:
                        chunk_max(c + 1, (c + 1) % 2, (c + 1) // 2, cols, m - 1, KF * f)
                        split(c + 1, (c + 1) % 2, cols, None if last else XF_GU[f])
                    else:
                        chunk_lo(c + 1, (c + 1) % 2, cols)
                    hidden_tile(m, c % 2, m % 2, f)

                def largest_hidden(i, first, last, reductions):
                    dve.wait_ge(h_max, (KF + 2) * f + last + reductions)
                    nc.vector.tensor_reduce(hm[:, i:i + 1], hmax[:, first:last], AX.X, ALU.max).then_inc(h_max, 1)

                def written_max(m):
                    dve.wait_ge(hid_done, 2 + KF * f + m + 1)
                    hidden_max(m)

                def hidden_lo(first, last):
                    for m in range(first, last):
                        i = HID[f] if m < KF_A else HID_B[f]
                        dve.wait_ge(hs_hi, KF * f + m + 1)
                        nc.vector.scalar_tensor_tensor(hid_s[:, m, 1, :], hid[:, m + 2, :], hscale[:, i:i + 1], hid_s[:, m, 0, :],
                                                       ALU.mult, ALU.subtract).then_inc(hs_ready, 1)

                step(0)
                step(1)
                with dve.Fori(0, (N_GU - 6) // 2) as i:
                    for t in range(2):
                        m, c, slot = 2 + t + 2 * i, GU[f] + 2 + t + 2 * i, (GU[f] + t) % 2
                        chunk_max(c + 1, 1 - slot, (GU[f] + t + 3) // 2 + i, GU_COLS, m - 1, KF * f)
                        split(c + 1, 1 - slot, GU_COLS, XF_GU[f])
                        hidden_tile(m, slot, t, f)
                step(KF - 4)
                m, c, f0 = KF - 3, GU[f] + KF - 3, KF * f
                slot, other = c % 2, (c + 1) % 2
                chunk_max(c + 1, other, (c + 1) // 2, GU_COLS, m - 1, f0)
                largest_hidden(HID[f], 0, KF_A, 0)
                chunk_scale(c + 1, other, XF_GU[f])
                back_scale(HID[f], 0.5 / ALPHA)
                chunk_lo(c + 1, other, GU_COLS)
                chunk_max(c + 2, slot, (c + 2) // 2, GU_COLS)
                hidden_lo(0, LO_STEPS[0])
                hidden_tile(m, slot, 1, f)

                chunk_scale(c + 2, slot, XF_GU[f])
                written_max(m)
                hidden_lo(LO_STEPS[0], LO_STEPS[1])
                chunk_lo(c + 2, slot, GU_COLS)
                chunk_max(c + 3, other, (c + 3) // 2, DN_COLS)
                hidden_lo(LO_STEPS[1], LO_STEPS[2])
                hidden_tile(m + 1, other, 0, f)

                chunk_scale(c + 3, other)
                written_max(m + 1)
                hidden_lo(LO_STEPS[2], LO_STEPS[3])
                chunk_lo(c + 3, other, DN_COLS)
                chunk_max(c + 4, slot, (c + 4) // 2, DN_COLS)
                hidden_lo(LO_STEPS[3], LO_STEPS[4])
                hidden_tile(m + 2, slot, 1, f)

                chunk_scale(c + 4, slot)
                written_max(m + 2)
                largest_hidden(HID_B[f], KF_A, KF, 1)
                hidden_lo(LO_STEPS[4], LO_STEPS[5])
                chunk_lo(c + 4, slot, DN_COLS)
                hidden_lo(LO_STEPS[5], KF_A)
                back_scale(HID_B[f], 0.5 / ALPHA)
                hidden_lo(KF_A, KF)
                dve.wait_ge(xf_done, HID_B[f] + 1)
                for q in range(N_DN):
                    c = DN[f] + q
                    out_scale_of(c, c % 2, XF_FOUND + HID[f])
                    nc.vector.tensor_tensor(oscale_b[:, c % 2:c % 2 + 1], winv[:, c % 2:c % 2 + 1],
                                            xinv[:, XF_FOUND + HID_B[f]:XF_FOUND + HID_B[f] + 1],
                                            ALU.mult).then_inc(out_scale_b, 1)
                    if 0 < q < N_DN - 1 or q and f == 0:
                        cols, xf = (DN_COLS, None) if q < N_DN - 1 else (KD * IN_COLS[0], XF_IN)
                        chunk_max(c + 1, (c + 1) % 2, (c + 1) // 2, cols)
                        split(c + 1, (c + 1) % 2, cols, xf)
                    if q == SHIFT_TILES[2 * f + 1]:
                        centre(2 * f + 1)
                        dve.wait_ge(centred, KD * (2 * f + 2))
                    dve.wait_ge(out_scale, c + 1)
                    dve.wait_ge(out_scale_b, KD * f + q + 1)
                    residual_tile(q, q % 2, 2 * KD * f + q, c % 2, KD * f + q)

            def gates(q):
                j, d = GATES[q]
                v = V[:, j, d, :]
                lg = tmp_b[:, q % 2, :]
                dve.wait_ge(gate_abs, q + 1)
                nc.vector.tensor_scalar(halves(lg), pair(4 + 2 * (q % 2)), par[:, C_GATE + gate_col(q):C_GATE + gate_col(q) + 1],
                                        0.0, ALU.add, ALU.min).then_inc(gate_min, 1)
                dve.wait_ge(gate_min, q + 1)
                dve.wait_ge(gate_ln, q + 1)
                nc.vector.tensor_tensor(lg, lg, tmp_a[:, q % 2, :], ALU.subtract).then_inc(log_gate, 1)
                dve.wait_ge(log_gate, q + 1)
                nc.vector.tensor_tensor_scan(v, reset[:, :], lg, 0.0, ALU.mult, ALU.add).then_inc(scanned, 1)
                dve.wait_ge(scanned, q + 1)
                nc.vector.tensor_copy(B_end[:, q, :], v.rearrange("p (c t) -> p c t", c=NCH)[:, :, CH - 1]).then_inc(ends_done, 1)
                if d == 1:
                    dve.wait_ge(ends_done, q + 1)
                    nc.vector.tensor_tensor(v, v, lg, ALU.subtract).then_inc(decay_done, 1)

            def exponents(j, d):
                dve.wait_ge(decay_done, j + 1)
                if j:
                    dve.wait_ge(dec_exp, 4 * N_DIR * j)
                q = N_DIR * j + d
                v = V[:, j, d, :].rearrange("p (c t) -> p c t", c=NCH)
                a = tmp_a[:, d, :].rearrange("p (c t) -> p c t", c=NCH)
                b = tmp_b[:, d, :].rearrange("p (c t) -> p c t", c=NCH)
                nc.vector.tensor_tensor(a, v, v[:, :, MID:MID + 1].to_broadcast([P, NCH, CH]),
                                        ALU.subtract).then_inc(rel_a, 1)
                nc.vector.tensor_tensor(b, B_end[:, q, :].unsqueeze(2).to_broadcast([P, NCH, CH]), v,
                                        ALU.subtract).then_inc(rel_b, 1)
                dve.wait_ge(rel_a, q + 1)
                nc.vector.tensor_scalar(tmp_a[:, d, :], tmp_a[:, d, :], -EXP_LIMIT, EXP_LIMIT,
                                        ALU.max, ALU.min).then_inc(clamped, 1)

            def decayed(j, d):
                q = N_DIR * j + d
                dve.wait_ge(dec_exp, 4 * q + 1)
                nc.vector.tensor_tensor(q_in[j][:, d, :], q_in[j][:, d, :], gqT[:, j, :], ALU.mult).then_inc(dec_dve, 1)
                dve.wait_ge(dec_exp, 4 * q + 2)
                nc.vector.tensor_tensor(k_in[j][:, d, :], k_in[j][:, d, :], gkT[:, j, :], ALU.mult).then_inc(dec_dve, 1)

            def state_step(j, s):
                n = j * (NCH - 1) + s
                dve.wait_ge(st_ready, n + 1)
                if s:
                    dve.wait_ge(st_done, 2 * n)
                for d in range(N_DIR):
                    q = N_DIR * j + d
                    c = s if d == 0 else NCH - 1 - s
                    new = PS[:, 6 + n % 2, d * P:(d + 1) * P]
                    if s == 0:
                        nc.vector.tensor_copy(state[j][:, d, 1, :], new).then_inc(st_done, 1)
                    else:
                        dve.wait_ge(end_exp, q + 1)
                        nc.vector.scalar_tensor_tensor(state[j][:, d, s + 1, :], state[j][:, d, s, :], E_end[:, q, c:c + 1],
                                                       new, ALU.mult, ALU.add).then_inc(st_done, 1)

            def mask_scores(j, c):
                n = j * NCH + c
                dve.wait_ge(a_ready, n + 1)
                both = a_dir[:, n % 2, :]
                nc.vector.tensor_tensor(both.rearrange("p (a d t) -> p a d t", d=2, a=2),
                                        PS[0:CH, 2 * (n % 2):2 * (n % 2) + 2, 0:2 * CH].rearrange("p a (d t) -> p a d t", d=2),
                                        masks[:, :, :].unsqueeze(1).to_broadcast([CH, 2, N_DIR, CH]),
                                        ALU.mult).then_inc(a_masked, 1)
                dve.wait_ge(a_masked, n + 1)
                if n >= 2:
                    dve.wait_ge(o_ready, n - 1)
                both = both.rearrange("p (a d t) -> p a d t", d=2, a=2)
                nc.vector.tensor_tensor(a_sum[:, n % 2, :].rearrange("p (a t) -> p a t", a=2), both[:, :, 0, :], both[:, :, 1, :],
                                        ALU.add).then_inc(a_done, 1)

            def gla():
                for d in range(N_DIR):
                    exponents(1, d)
                for s in range(NCH - 1):
                    state_step(0, s)
                for c in range(NCH):
                    mask_scores(0, c)
                    if c < N_DIR:
                        decayed(1, c)
                for s in range(3):
                    state_step(1, s)
                mask_scores(1, 0)
                state_step(1, 3)
                mask_scores(1, 1)
                state_step(1, 4)
                step = 0
                for c in range(2, NCH):
                    mask_scores(1, c)
                    for _ in range(3 if c < 4 else 2):
                        norm_step(step)
                        step += 1

            def norm_step(n):
                h, step = divmod(n, NORM_STEPS)
                o, rms = gO[:, h, :], o_rms[h // 2][:, h % 2, :]
                if step < 4:
                    dve.wait_ge(o_std, h + 1)
                    q = rms[:, step * (T // 4):(step + 1) * (T // 4)]
                    nc.vector.reciprocal(q, q).then_inc(o_rstd, 1)
                else:
                    dve.wait_ge(o_rstd, 4 * (h + 1))
                    dve.wait_ge(o_gated, h + 1)
                    nc.vector.scalar_tensor_tensor(o, o, par[:, C_NORM:C_NORM + 1], rms, ALU.mult, ALU.mult).then_inc(o_final, 1)

            def largest_gla():
                dve.wait_ge(o_final, G_HEADS)
                nc.vector.tensor_reduce(mmax[:, 0:1], gO.rearrange("p k t -> p (k t)"), AX.X, ALU.max,
                                        apply_absolute_value=True).then_inc(m_max, 1)

            def att_max(u):
                n, j = UNITS[u]
                cols = unit_cols(u)
                dve.wait_ge(s_ready, u + 1)
                if n < 0:
                    dve.wait_ge(bias_done, 1)
                if u >= 2:
                    dve.wait_ge(pt_ready, 2 * (u - 1))
                for g in range(GROUPS):
                    i = 2 * u + g
                    h = REP * g + j
                    start = rel_start(n)
                    bias, slope = (bias_m[:, g, :], 1.0) if n < 0 else (rels[g][:, start:start + cols], slopes()[h])
                    if n >= 0:
                        dve.wait_ge(sink_set, 2 * (u - 1) + g + 1)
                    nc.vector.tensor_tensor_reduce(out=score_buf(i)[:, 0:cols], in0=PS[:, 2 * (u % 2) + g, 0:cols], in1=bias, scale=-slope,
                                                   scalar=-NEG, op0=ALU.add, op1=ALU.min,
                                                   accum_out=smin[:, i:i + 1]).then_inc(s_max, 1)

            def att_recip(u):
                for g in range(GROUPS):
                    i = 2 * u + g
                    dve.wait_ge(p_exp, i + 1)
                    nc.vector.reciprocal(srec[:, i:i + 1], ssum[:, i:i + 1]).then_inc(p_rec, 1)
                if u >= 2:
                    dve.wait_ge(pt_ready, 2 * (u - 1))
                for g in range(GROUPS):
                    i = 2 * u + g
                    dve.wait_ge(p_rec, i + 1)
                    nc.vector.tensor_scalar(diag[:, u % 2, g, :], ident[:, :], srec[:, i:i + 1], None, ALU.mult).then_inc(diag_done, 1)

            def att_out(n):
                dve.wait_ge(att_ready, n + 2)
                o = PS[:, 6 + (n + 1) % 2, :]
                if n < 0:
                    dst = mix[:, 0:REP, 0:N_META]
                    o = o[:, 0:P].rearrange("p (r m) -> p r m", r=REP)[:, :, 0:N_META]
                else:
                    dst = mix[:, 0:REP, N_META + n * BLOCK:N_META + (n + 1) * BLOCK]
                    o = o.rearrange("p (r m) -> p r m", r=REP)
                nc.vector.tensor_copy(dst, o).then_inc(att_done, 1)
                dve.wait_ge(att_done, n + 2)
                nc.vector.tensor_reduce(mmax[:, 1 + (n + 1) * REP:1 + (n + 2) * REP], dst, AX.X, ALU.max,
                                        apply_absolute_value=True).then_inc(m_max, 1)

            def layer_norm_scales():
                dve.wait_ge(par_loaded, 16)
                nc.vector.tensor_reduce(bmax[:, :], par[:, 0:48].rearrange("p (v k) -> p v k", k=KD), AX.X, ALU.max,
                                        apply_absolute_value=True).then_inc(b_max, 1)
                dve.wait_ge(b_all, 1)
                gain_bias = ball[:, :].rearrange("p (l v) -> p l v", v=2)
                nc.vector.scalar_tensor_tensor(bound[:, :], gain_bias[:, :, 0], D_MODEL ** 0.5, gain_bias[:, :, 1],
                                               ALU.mult, ALU.add).then_inc(b_step, 1)
                dve.wait_ge(b_step, 1)
                scale_of(bound[:, :], bexp[:, :], bneg[:, :], xscale[:, :], xinv[:, 0:3], b_step, 1)
                dve.wait_ge(b_step, 5)
                nc.vector.tensor_scalar(xinv[:, XF_INQ:XF_INQ + 1], xinv[:, XF_IN:XF_IN + 1], DH ** -0.5, None,
                                        ALU.mult).then_inc(b_step, 1)
                for L in range(3):
                    nc.vector.tensor_scalar(par_s[:, 16 * L:16 * L + 16], par[:, 16 * L:16 * L + 16], xscale[:, L:L + 1], None,
                                            ALU.mult).then_inc(b_step, 1)
                dve.wait_ge(b_step, B_STEPS)

            layer_norm_scales()
            dve.wait_ge(x_loaded[0], 16)
            for n in range(1, SHIFT_TILES[0]):
                add_tile(nc.vector, dve, 0, n)
            dve.wait_ge(x_loaded[1], 16)
            centre(0)
            chunk_max(0, 0, 0, GU_COLS)
            chunk_scale(0, 0, XF_GU[0])
            chunk_max(1, 1, 0, GU_COLS)
            chunk_lo(0, 0, GU_COLS)
            layer_norm(0, (1, 1, XF_GU[0]))
            ffn(0)
            chunk_max(IN0 + 1, (IN0 + 1) % 2, (IN0 + 1) // 2, KD * 2 * P)
            layer_norm(1, (IN0 + 1, (IN0 + 1) % 2, XF_IN))
            for i in range(N_IN):
                c = IN0 + i + 1
                if i:
                    chunk_max(c, c % 2, c // 2, KD * 2 * P)
                d = DECAYS_AT.get(i)
                if d is not None:
                    exponents(0, d)
                xf = None if i == N_IN - 1 else XF_INQ if i + 1 in (2, 6, 7) else XF_IN
                if i:
                    split(c, c % 2, KD * 2 * P, xf, 2 + LAST_OF[i - 1] + 1 if xf is not None else None)
                else:
                    chunk_lo(c, c % 2, KD * 2 * P)
                for t in [t for t in TILES if t[0] == "aq" and t[2] == i + 1]:
                    if t[1] == 0:
                        dve.wait_ge(const_loaded, 16 * N_CONST)
                    dve.wait_ge(out_scale, c + 1)
                    nc.vector.tensor_tensor(qscale[:, t[1]:t[1] + 1], oscale[:, c % 2:c % 2 + 1], head[:, t[1]:t[1] + 1],
                                            ALU.mult).then_inc(q_scale, 1)
                for q in GATES_AFTER.get(i - 1, []):
                    gates(q)
                if d is not None:
                    decayed(0, d)
            gla()
            att_max(0)
            att_max(1)
            att_recip(0)
            for u in range(len(UNITS)):
                if u + 1 < len(UNITS):
                    att_recip(u + 1)
                if u + 2 < len(UNITS):
                    att_max(u + 2)
                if u == 0 or UNITS[u][1] == REP - 1:
                    att_out(UNITS[u][0])
                if u < 2 * NORM_STEPS:
                    norm_step(2 * NORM_STEPS + u)
                elif u == 2 * NORM_STEPS:
                    largest_gla()
            dve.wait_ge(m_max, NB + 2)
            nc.vector.tensor_reduce(hm[:, MIX:MIX + 1], mmax[:, :], AX.X, ALU.max).then_inc(m_max, 1)
            back_scale(MIX, 1.0 / ALPHA)
            for k in range(KD):
                dve.wait_ge(m_hi, k + 1)
                nc.vector.scalar_tensor_tensor(xs[:, 1, k, :], mix[:, k, :], hscale[:, MIX:MIX + 1], xs[:, 0, k, :],
                                               ALU.mult, ALU.subtract).then_inc(m_ready, 1)
            dve.wait_ge(xf_done, MIX + 1)
            for n in range(N_OUT):
                c = OUT0 + n
                out_scale_of(c, c % 2, XF_FOUND + MIX)
                last = n == N_OUT - 1
                cols = GU_COLS if last else OUT_COLS
                chunk_max(c + 1, (c + 1) % 2, (c + 1) // 2, cols)
                chunk_scale(c + 1, (c + 1) % 2, XF_GU[1] if last else None)
                if not last:
                    chunk_lo(c + 1, (c + 1) % 2, cols)
                if 2 * n == SHIFT_TILES[2]:
                    centre(2, range(2 * n, KD))
                    dve.wait_ge(centred, centre_count(2, KD - 1))
                dve.wait_ge(out_scale, c + 1)
                for t in range(2):
                    if 2 * n + t == SHIFT_TILES[2] + 1:
                        centre(2, range(2 * n))
                    residual_tile(2 * n + t, t, KD + 2 * n + t, c % 2)
            chunk_lo(GU[1], GU[1] % 2, GU_COLS)
            chunk_max(GU[1] + 1, (GU[1] + 1) % 2, (GU[1] + 1) // 2, GU_COLS)
            layer_norm(2, (GU[1] + 1, (GU[1] + 1) % 2, XF_GU[1]))
            ffn(1)
            layer_norm(3)

        @block.gpsimd
        def _(pool):
            nc.gpsimd.memset(ones[:, :], 1.0 / D_MODEL).then_inc(ready0, 1)
            nc.gpsimd.memset(ones_dv[:, :], 1.0 / DV).then_inc(ready0, 1)
            nc.gpsimd.memset(eps[:, 0:1], EPS).then_inc(ready0, 1)
            nc.gpsimd.memset(eps[:, 1:2], EPS / ALPHA ** 2).then_inc(ready0, 1)
            nc.gpsimd.memset(kT[:, SINK_COL:SINK_COL + 1], 0.0).then_inc(ready0, 1)
            for n, s in enumerate((hid_done, hid_done, res_done, res_done, proj_done, proj_done)):
                nc.gpsimd.memset(credit[:, n:n + 1], 0.0).then_inc(s, 1)

            def over_all(c, slot):
                pool.wait_ge(w_max, c + 1)
                nc.gpsimd.partition_all_reduce(call[:, slot:slot + 1], cmax[:, slot:slot + 1], P, LARGEST).then_inc(w_all, 1)

            def add_squares(L, first, last):
                for n in range(first, last + 1):
                    pool.wait_ge(squared, KD * L + n + 1)
                    if n > 1:
                        pool.wait_ge(sq_summed, (KD - 2) * L + n - 1)
                    nc.gpsimd.tensor_tensor(sq_sum[:, :], tmp_b[:, 0, :] if n == 1 else sq_sum[:, :], tmp_b[:, n % 2, :],
                                            ALU.add).then_inc(sq_summed, 1)

            def add_tiles(L, first, last):
                for n in range(first, last + 1):
                    pool.wait_ge(res_done, 2 + KD * (L - 1) + n + 1)
                    add_tile(nc.gpsimd, pool, L, n)

            def shift_tiles(L):
                pool.wait_ge(delta_out, 2 * L + 1)
                for k in range(1, KD):
                    nc.gpsimd.tensor_tensor(X[:, k, :], X[:, k, :], delta, ALU.subtract).then_inc(shifted, 1)

            def hidden_chunks(f):
                for c in range(GU[f] + 2, DN[f] + 2):
                    over_all(c, c % 2)
                    if c == GU[f] + KF_A + 1:
                        pool.wait_ge(h_max, (KF + 2) * f + KF_A + 1)
                        over_all_h(HID[f])
                pool.wait_ge(h_max, (KF + 2) * (f + 1))
                over_all_h(HID_B[f])

            def down_chunks(f):
                L = 2 * f + 1
                for q in range(N_DN):
                    c = DN[f] + q + 1
                    if 0 < q < N_DN - 1 or q and f == 0:
                        over_all(c, c % 2)
                    if q == 1:
                        add_tiles(L, 1, 1)
                    elif 1 < q < SHIFT_TILES[L]:
                        add_tiles(L, q, q)
                    elif q >= SHIFT_TILES[L]:
                        if q < KD - 1:
                            add_squares(L, 1 if q == SHIFT_TILES[L] else q, q)
                if f == 0:
                    over_all(IN0 + 1, (IN0 + 1) % 2)
                shift_tiles(L)

            def over_all_h(i):
                nc.gpsimd.partition_all_reduce(hall[:, i:i + 1], hm[:, i:i + 1], P, LARGEST).then_inc(h_all, 1)

            pool.wait_ge(b_max, 1)
            nc.gpsimd.partition_all_reduce(ball[:, :], bmax[:, :], P, LARGEST).then_inc(b_all, 1)
            add_squares(0, 1, 3)
            over_all(0, 0)
            add_squares(0, 4, KD - 2)
            over_all(1, 1)
            shift_tiles(0)
            hidden_chunks(0)
            pool.wait_ge(const_loaded, 16 * N_CONST)
            nc.gpsimd.tensor_copy(bias_m[:, :, SINK_COL:SINK_COL + 1], par[:, C_SINKM:C_SINKM + GROUPS].unsqueeze(2)).then_inc(bias_done, 1)
            nc.gpsimd.tensor_tensor(sinks[:, :], par[:, C_SINK:C_SINK + HEADS], head[:, REP:REP + HEADS], ALU.mult).then_inc(sinks_done, 1)
            down_chunks(0)

            def decays(j, dirs=range(N_DIR)):
                for d in dirs:
                    q = N_DIR * j + d
                    pool.wait_ge(dec_exp, 4 * q + 3)
                    nc.gpsimd.tensor_tensor(q_ex[j][:, d, :], q_ex[j][:, d, :], gqT[:, j, :], ALU.mult).then_inc(dec_pool, 1)
                    pool.wait_ge(dec_exp, 4 * q + 4)
                    nc.gpsimd.tensor_tensor(k_ex[j][:, d, :], k_ex[j][:, d, :], gkT[:, j, :], ALU.mult).then_inc(dec_pool, 1)

            for i in range(N_IN):
                if i:
                    over_all(IN0 + i + 1, (IN0 + i + 1) % 2)
                if i in DECAYS_AT:
                    decays(0, [DECAYS_AT[i]])

            def gate_outputs(j):
                for h in (2 * j, 2 * j + 1):
                    pool.wait_ge(o_sq, h + 1)
                    nc.gpsimd.tensor_tensor(gO[:, h, :], gO[:, h, :], sg[:, h, :], ALU.mult).then_inc(o_gated, 1)

            decays(1)
            gate_outputs(0)
            pool.wait_ge(o_done, PAIRS * NCH)
            nc.gpsimd.tensor_copy(rel_1[:, :], rel[:, :]).then_inc(rel_copied, 1)
            gate_outputs(1)
            pool.wait_ge(rel_copied, 1)
            pool.wait_ge(sinks_done, 1)
            for u in range(1, len(UNITS)):
                n, j = UNITS[u]
                for g in range(GROUPS):
                    if u >= 2:
                        pool.wait_ge(s_max, 2 * (u - 1) + g + 1)
                    col = rel_start(n) + SINK_COL
                    h = REP * g + j
                    nc.gpsimd.tensor_copy(rels[g][:, col:col + 1], sinks[:, h:h + 1]).then_inc(sink_set, 1)
            pool.wait_ge(m_max, NB + 3)
            over_all_h(MIX)
            for n in range(N_OUT):
                over_all(OUT0 + n + 1, (OUT0 + n + 1) % 2)
                if 2 * n < SHIFT_TILES[2]:
                    add_tiles(2, max(1, 2 * n), 2 * n + 1)
                else:
                    add_squares(2, *((1, 2) if 2 * n == SHIFT_TILES[2] else (3, KD - 2)))
            over_all(GU[1] + 1, (GU[1] + 1) % 2)
            shift_tiles(2)
            hidden_chunks(1)
            down_chunks(1)


def shape_constants():
    i, m = np.arange(BLOCK)[:, None], np.arange(3 * BLOCK)[None, :]
    dist = np.abs(m - BLOCK - i).astype(np.float32)
    band = np.where(dist <= WINDOW, -dist, NEG).astype(np.float32)
    zeros = np.zeros((BLOCK, N_META + 1), np.float32)
    rel = np.concatenate([zeros, band, zeros, band[:, BLOCK:]], 1)
    half = np.arange(P)[:, None] // DH
    head = np.zeros((P, REP + HEADS), np.float32)
    head[:, :REP] = 1 / np.array(slopes(), np.float32)[half * REP + np.arange(REP)[None, :]]
    head[:, REP:] = 1 / np.array(slopes(), np.float32)
    row = np.arange(P)
    q = (row % MROW)[:, None]
    kpos = (N_META + np.arange(BLOCK))[None, :]
    dist = np.abs(kpos - q).astype(np.float32)
    bias_meta = np.zeros((P, GROUPS, S_META), np.float32)
    for g in range(GROUPS):
        slope = np.array([slopes()[REP * g + r // MROW] for r in row], np.float32)[:, None]
        bias_meta[:, g, N_META + 1:] = np.where(dist <= WINDOW, -slope * dist, NEG)
    s, t = np.arange(CH)[:, None], np.arange(CH)[None, :]
    masks = np.stack([s <= t, s > t], 1).astype(np.float32)
    reset = np.ones((P, T), np.float32)
    reset[:, ::CH] = 0.0
    return {"rel": rel, "head": head, "bias_meta": bias_meta,
            "ident": np.eye(P, dtype=np.float32), "masks": masks, "reset": reset}


def lay_out(x, meta_tokens, ln_in_g, ln_in_b, ffn1_ln_g, ffn1_ln_b, ffn1_w_gate, ffn1_w_up, ffn1_w_down,
            w_in, attn_sink, gla_gate_w2, gla_gate_b, gla_norm_g, w_out, mix_ln_g, mix_ln_b,
            ffn2_w_gate, ffn2_w_up, ffn2_w_down, ffn2_ln_g, ffn2_ln_b):
    def kcols(w):
        return w.reshape(-1, P, w.shape[1]).transpose(1, 0, 2)

    def chunks(w, cols):
        k = kcols(w)
        n = w.shape[1] // cols
        return k.reshape(P, -1, n, cols).transpose(2, 0, 1, 3).reshape(n, P, -1)

    tokens = np.concatenate([meta_tokens, x[0]], 0)
    arrays = {"xT": kcols(tokens.T).reshape(P, -1)}
    cols = [v.reshape(KD, P).T for v in (ln_in_g, ln_in_b, ffn1_ln_g, ffn1_ln_b, mix_ln_g, mix_ln_b, ffn2_ln_g, ffn2_ln_b)]
    cols.append(gla_norm_g.reshape(DV, 1))
    cols.append(gla_gate_b.reshape(N_DIR * PAIRS, P).T)
    cols.append(np.broadcast_to(attn_sink.reshape(1, HEADS), (P, HEADS)))
    cols.append(np.repeat(attn_sink.reshape(GROUPS, REP), MROW, 1).T)
    arrays["params"] = np.concatenate(cols, 1)
    w2 = np.zeros((N_DIR * RANK, N_DIR, PAIRS * P), gla_gate_w2.dtype)
    for d in range(N_DIR):
        w2[d * RANK:(d + 1) * RANK, d] = gla_gate_w2[0, d]
    arrays["w2"] = w2
    for f, (g, u, dn) in enumerate([(ffn1_w_gate, ffn1_w_up, ffn1_w_down), (ffn2_w_gate, ffn2_w_up, ffn2_w_down)]):
        arrays[f"gate{f}"] = chunks(g[0], P)
        arrays[f"up{f}"] = chunks(u[0], P)
        arrays[f"down{f}"] = chunks(dn[0], P)
    at = np.cumsum([0, HEADS * DH, GROUPS * DH, GROUPS * DH, G_HEADS * DK, G_HEADS * DK, G_HEADS * DV, G_HEADS * DV,
                    N_DIR * RANK])
    aq, ak, av, gq, gk, gv, gg, gz = [w_in[0][:, a:b] for a, b in zip(at[:-1], at[1:])]
    aq = aq.reshape(D_MODEL, GROUPS, REP, DH).transpose(0, 2, 1, 3).reshape(D_MODEL, -1)
    groups = [[gz, gg[:, :256]], [gg[:, 256:]], [gq], [gk], [gv[:, :256]], [gv[:, 256:]], [aq[:, :256]], [aq[:, 256:]],
              [ak, av]]
    for n, ws in enumerate(groups):
        arrays[f"w_in{n}"] = kcols(np.concatenate(ws, 1)).reshape(P, -1)
    wo = w_out[0]
    att = wo[:HEADS * DH].reshape(GROUPS, REP, DH, D_MODEL).transpose(1, 0, 2, 3).reshape(-1, D_MODEL)
    arrays["w_out"] = chunks(np.concatenate([att, wo[HEADS * DH:]], 0), 2 * P)
    return arrays


def kernel(**inputs):
    import concourse.bacc as bacc
    from concourse.bass_utils import run_bass_kernel_spmd

    arrays = lay_out(**{k: np.asarray(v) for k, v in inputs.items()})
    arrays.update(shape_constants())
    arrays = {k: np.ascontiguousarray(v) for k, v in arrays.items()}
    nc = bacc.Bacc("TRN2", target_bir_lowering=False, num_devices=1)
    ap = {k: nc.dram_tensor(f"in_{k}", v.shape, F32, kind="ExternalInput").ap() for k, v in arrays.items()}
    out = nc.dram_tensor("out_T", (KD, P, SEQ), F32, kind="ExternalOutput").ap()
    build(nc, ap["xT"], ap["params"], ap["rel"], ap["head"], ap["bias_meta"], ap["ident"], ap["masks"],
          ap["reset"], ap["w2"], [ap["gate0"], ap["gate1"]], [ap["up0"], ap["up1"]], [ap["down0"], ap["down1"]],
          [ap[f"w_in{n}"] for n in range(N_IN)], ap["w_out"], out)
    r = run_bass_kernel_spmd(nc, [{f"in_{k}": v for k, v in arrays.items()}], core_ids=[0])
    y = r.results[0]["out_T"]
    return np.ascontiguousarray(y.reshape(D_MODEL, SEQ).T.reshape(1, SEQ, D_MODEL))
```
